# Optimizing a Trainium2 kernel written in Bass

```python
import jax, jax.numpy as jnp
from jax import lax
import numpy as np
import math

D_MODEL = 1024
BATCH = 1
SEQ = 256
DEPTH = 2

MLA_HEADS = 8
MLA_NOPE = 64
MLA_ROPE = 32
MLA_V = 64
Q_LORA = 384
KV_LORA = 256
ROPE_BASE = 10000.0
DSA_HEADS = 8
DSA_DIM = 64
IDX_HEADS = 8
IDX_DIM = 32
TOPK_MAX = 256
D_MIX = MLA_HEADS * MLA_V + DSA_HEADS * DSA_DIM
N_EXPERTS = 16
N_GROUPS = 4
EXPERTS_PER_GROUP = N_EXPERTS // N_GROUPS
TOP_K_EXPERTS = 2
GROUP_SCORE_K = 2
D_FF_EXPERT = 512
ALPHA = (2.0 * DEPTH) ** 0.25
BETA = (8.0 * DEPTH) ** -0.25
Q_BLOCK = 128
LN_EPS = 1e-5
RMS_EPS = 1e-6

SPLIT_SIZES = (Q_LORA, KV_LORA, MLA_ROPE, DSA_HEADS * DSA_DIM, DSA_DIM, DSA_DIM,
               IDX_HEADS * IDX_DIM, IDX_DIM, IDX_HEADS)
SPLIT_POINTS = tuple(int(v) for v in np.cumsum(SPLIT_SIZES)[:-1])
IN_COLS = int(sum(SPLIT_SIZES))
DSA_V_START = int(sum(SPLIT_SIZES[:5]))


def layer_norm(x, g, b):
    xf = x.astype(jnp.float32)
    mu = jnp.mean(xf, axis=-1, keepdims=True)
    var = jnp.mean(jnp.square(xf - mu), axis=-1, keepdims=True)
    y = (xf - mu) * lax.rsqrt(var + LN_EPS) * g.astype(jnp.float32) + b.astype(jnp.float32)
    return y.astype(x.dtype)

def rms_norm(x, g):
    xf = x.astype(jnp.float32)
    y = xf * lax.rsqrt(jnp.mean(jnp.square(xf), axis=-1, keepdims=True) + RMS_EPS)
    return (y * g.astype(jnp.float32)).astype(x.dtype)

def rope(x, pos):
    half = x.shape[-1] // 2
    inv = ROPE_BASE ** (-jnp.arange(half, dtype=jnp.float32) / half)
    ang = pos[:, None] * inv[None, :]
    cos = jnp.cos(ang)[None, :, None, :]
    sin = jnp.sin(ang)[None, :, None, :]
    xf = x.astype(jnp.float32)
    x1, x2 = xf[..., :half], xf[..., half:]
    return jnp.concatenate([x1 * cos - x2 * sin, x1 * sin + x2 * cos], axis=-1).astype(x.dtype)

def sweep_query_blocks(block_fn, seq_len):
    starts = jnp.arange(seq_len // Q_BLOCK, dtype=jnp.int32) * Q_BLOCK
    out = lax.map(block_fn, starts)
    nb, b, qb, h, d = out.shape
    return jnp.transpose(out, (1, 0, 2, 3, 4)).reshape(b, nb * qb, h * d)

def mla_group(qa, kva, kr, q_norm_g, w_q_up, kv_norm_g, w_uk, w_uv, pos):
    B, T, _ = qa.shape
    q = (rms_norm(qa, q_norm_g) @ w_q_up).reshape(B, T, MLA_HEADS, MLA_NOPE + MLA_ROPE)
    q = jnp.concatenate([q[..., :MLA_NOPE], rope(q[..., MLA_NOPE:], pos)], axis=-1)
    c_kv = rms_norm(kva, kv_norm_g)
    k_nope = (c_kv @ w_uk).reshape(B, T, MLA_HEADS, MLA_NOPE)
    v = (c_kv @ w_uv).reshape(B, T, MLA_HEADS, MLA_V)
    k_rope = rope(kr[:, :, None, :], pos)
    k = jnp.concatenate([k_nope, jnp.broadcast_to(k_rope, (B, T, MLA_HEADS, MLA_ROPE))], axis=-1)
    scale = (MLA_NOPE + MLA_ROPE) ** -0.5
    key_idx = jnp.arange(T, dtype=jnp.int32)

    def block(start):
        qb = lax.dynamic_slice_in_dim(q, start, Q_BLOCK, axis=1)
        s = jnp.einsum('bthd,bshd->bhts', qb, k).astype(jnp.float32) * scale
        tq = start + jnp.arange(Q_BLOCK, dtype=jnp.int32)
        s = jnp.where(key_idx[None, :] <= tq[:, None], s, -jnp.inf)
        p = jax.nn.softmax(s, axis=-1).astype(v.dtype)
        return jnp.einsum('bhts,bshd->bthd', p, v)

    return sweep_query_blocks(block, T)

def dsa_group(dq, dk, dv, iq, ik, iw, slopes, n_keep):
    B, T, _ = dq.shape
    q = dq.reshape(B, T, DSA_HEADS, DSA_DIM)
    iq = iq.reshape(B, T, IDX_HEADS, IDX_DIM)
    iw = iw * (IDX_HEADS ** -0.5)
    key_idx = jnp.arange(T, dtype=jnp.int32)
    scale = DSA_DIM ** -0.5
    gather = jax.vmap(lambda arr, idx: arr[idx])

    def block(start):
        qb = lax.dynamic_slice_in_dim(q, start, Q_BLOCK, axis=1)
        iqb = lax.dynamic_slice_in_dim(iq, start, Q_BLOCK, axis=1)
        iwb = lax.dynamic_slice_in_dim(iw, start, Q_BLOCK, axis=1)
        tq = start + jnp.arange(Q_BLOCK, dtype=jnp.int32)
        rel = jax.nn.relu(jnp.einsum('bthd,bsd->bths', iqb, ik) * (IDX_DIM ** -0.5))
        score = jnp.einsum('bths,bth->bts', rel, iwb).astype(jnp.float32)
        score = jnp.where(key_idx[None, None, :] <= tq[None, :, None], score, -jnp.inf)
        _, sel = lax.top_k(score, n_keep)
        k_sel = gather(dk, sel)
        v_sel = gather(dv, sel)
        dist = (tq[None, :, None] - sel).astype(jnp.float32)
        s = jnp.einsum('bthd,btkd->bhtk', qb, k_sel).astype(jnp.float32) * scale
        s = s - slopes[None, :, None, None] * dist[:, None, :, :]
        s = jnp.where((dist >= 0.0)[:, None, :, :], s, -jnp.inf)
        p = jax.nn.softmax(s, axis=-1).astype(v_sel.dtype)
        return jnp.einsum('bhtk,btkd->bthd', p, v_sel)

    return sweep_query_blocks(block, T)

def hybrid_mixer(h, w_in, q_norm_g, w_q_up, kv_norm_g, w_uk, w_uv, w_o, pos, slopes, n_keep):
    proj = h @ w_in
    qa, kva, kr, dq, dk, dv, iq, ik, iw = jnp.split(proj, SPLIT_POINTS, axis=-1)
    out_a = mla_group(qa, kva, kr, q_norm_g, w_q_up, kv_norm_g, w_uk, w_uv, pos)
    out_b = dsa_group(dq, dk, dv, iq, ik, iw, slopes, n_keep)
    return jnp.concatenate([out_a, out_b], axis=-1) @ w_o

def grouped_moe(h, router_w, router_bias, w_gate, w_up, w_down):
    B, T, D = h.shape
    xt = h.reshape(B * T, D)
    aff = jax.nn.sigmoid((xt @ router_w).astype(jnp.float32))
    biased = aff + router_bias.astype(jnp.float32)
    grouped = biased.reshape(-1, N_GROUPS, EXPERTS_PER_GROUP)
    group_score = jnp.sum(lax.top_k(grouped, GROUP_SCORE_K)[0], axis=-1)
    g_sel = jnp.argmax(group_score, axis=-1)
    in_group = (jnp.arange(N_EXPERTS) // EXPERTS_PER_GROUP)[None, :] == g_sel[:, None]
    _, e_idx = lax.top_k(jnp.where(in_group, biased, -jnp.inf), TOP_K_EXPERTS)
    wts = jnp.take_along_axis(aff, e_idx, axis=-1)
    wts = wts / jnp.sum(wts, axis=-1, keepdims=True)
    gates = jnp.sum(jax.nn.one_hot(e_idx, N_EXPERTS, dtype=jnp.float32) * wts[..., None], axis=1)
    hg = jnp.einsum('nd,edf->nef', xt, w_gate)
    hu = jnp.einsum('nd,edf->nef', xt, w_up)
    act = jax.nn.silu(hg) * hu * gates[:, :, None].astype(hg.dtype)
    out = jnp.einsum('nef,efd->nd', act, w_down)
    return out.reshape(B, T, D)

def first_inputs(seed: int = 0) -> dict:
    key = jax.random.key(seed)
    ks = jax.random.split(key, 20)
    f32 = jnp.float32
    nrm = lambda k, shape, s: jax.random.normal(k, shape, f32) * s
    col_scale = np.ones((IN_COLS,), np.float32)
    col_scale[DSA_V_START:DSA_V_START + DSA_DIM] = BETA
    w_in = nrm(ks[1], (DEPTH, D_MODEL, IN_COLS), D_MODEL ** -0.5) * jnp.asarray(col_scale)
    return {
        'x': jax.random.normal(ks[0], (BATCH, SEQ, D_MODEL), f32),
        'w_in': w_in,
        'q_norm_g': 1.0 + nrm(ks[2], (DEPTH, Q_LORA), 0.02),
        'w_q_up': nrm(ks[3], (DEPTH, Q_LORA, MLA_HEADS * (MLA_NOPE + MLA_ROPE)), Q_LORA ** -0.5),
        'kv_norm_g': 1.0 + nrm(ks[4], (DEPTH, KV_LORA), 0.02),
        'w_uk': nrm(ks[5], (DEPTH, KV_LORA, MLA_HEADS * MLA_NOPE), KV_LORA ** -0.5),
        'w_uv': nrm(ks[6], (DEPTH, KV_LORA, MLA_HEADS * MLA_V), BETA * KV_LORA ** -0.5),
        'w_o': nrm(ks[7], (DEPTH, D_MIX, D_MODEL), BETA * D_MIX ** -0.5),
        'ln1_g': 1.0 + nrm(ks[8], (DEPTH, D_MODEL), 0.02),
        'ln1_b': nrm(ks[9], (DEPTH, D_MODEL), 0.02),
        'router_w': nrm(ks[10], (D_MODEL, N_EXPERTS), D_MODEL ** -0.5),
        'router_bias': nrm(ks[11], (N_EXPERTS,), 0.01),
        'w_gate': nrm(ks[12], (DEPTH, N_EXPERTS, D_MODEL, D_FF_EXPERT), BETA * D_MODEL ** -0.5),
        'w_up': nrm(ks[13], (DEPTH, N_EXPERTS, D_MODEL, D_FF_EXPERT), BETA * D_MODEL ** -0.5),
        'w_down': nrm(ks[14], (DEPTH, N_EXPERTS, D_FF_EXPERT, D_MODEL), BETA * D_FF_EXPERT ** -0.5),
        'ln2_g': 1.0 + nrm(ks[15], (DEPTH, D_MODEL), 0.02),
        'ln2_b': nrm(ks[16], (DEPTH, D_MODEL), 0.02),
    }

def first_block(x, w_in, q_norm_g, w_q_up, kv_norm_g, w_uk, w_uv, w_o, ln1_g, ln1_b,
              router_w, router_bias, w_gate, w_up, w_down, ln2_g, ln2_b):
    T = x.shape[1]
    pos = jnp.arange(T, dtype=jnp.float32)
    n_keep = min(TOPK_MAX, T // 4)
    slopes = 2.0 ** (-8.0 * jnp.arange(1, DSA_HEADS + 1, dtype=jnp.float32) / DSA_HEADS)
    for l in range(DEPTH):
        mix = hybrid_mixer(x, w_in[l], q_norm_g[l], w_q_up[l], kv_norm_g[l], w_uk[l], w_uv[l],
                           w_o[l], pos, slopes, n_keep)
        x = layer_norm(ALPHA * x + mix, ln1_g[l], ln1_b[l])
        ffn = grouped_moe(x, router_w, router_bias, w_gate[l], w_up[l], w_down[l])
        x = layer_norm(ALPHA * x + ffn, ln2_g[l], ln2_b[l])
    return x


CTX_LEN = 256
GRID_W = 64
N_EVEN = (DEPTH + 1) // 2
N_ODD = DEPTH // 2

DEEPNORM_ALPHA = (2.0 * DEPTH) ** 0.25
DEEPNORM_BETA = (8.0 * DEPTH) ** -0.25
N_MOD = 9

D_FF = 2816
MACARON_WEIGHT = 0.5

GDN_HEADS = 4
GDN_HEAD_DIM = 128
GDN_WIDTH = GDN_HEADS * GDN_HEAD_DIM
GDN_CONV = 5
GDN_CHUNK = 64
CONV_CH = D_MODEL // 2
CONV_WIDTH = 31
EVEN_SPLITS = (3 * GDN_WIDTH, 4 * GDN_WIDTH, 4 * GDN_WIDTH + 4 * GDN_HEADS)
EVEN_IN = 4 * GDN_WIDTH + 4 * GDN_HEADS + 2 * CONV_CH
EVEN_OUT = GDN_WIDTH + CONV_CH

ATT_HEADS = 8
ATT_KV_HEADS = 2
ATT_GROUP = ATT_HEADS // ATT_KV_HEADS
ATT_HEAD_DIM = 128
ATT_BLOCK = 128
ROPE_THETA = 10000.0
ODD_IN = (ATT_HEADS + 2 * ATT_KV_HEADS) * ATT_HEAD_DIM
ODD_OUT = ATT_HEADS * ATT_HEAD_DIM


def layer_norm_2(x, g, b):
    xf = x.astype(jnp.float32)
    mu = xf.mean(-1, keepdims=True)
    var = jnp.square(xf - mu).mean(-1, keepdims=True)
    return ((xf - mu) * lax.rsqrt(var + LN_EPS) * g + b).astype(x.dtype)

def rms_norm_2(x, g):
    xf = x.astype(jnp.float32)
    return (xf * lax.rsqrt(jnp.square(xf).mean(-1, keepdims=True) + RMS_EPS) * g).astype(x.dtype)

def l2_normalize(x):
    xf = x.astype(jnp.float32)
    return xf * lax.rsqrt(jnp.square(xf).sum(-1, keepdims=True) + RMS_EPS)

def modulate(x, shift, scale):
    return x * (1 + scale) + shift

def deepnorm_residual(x, y, g, b):
    return layer_norm_2(DEEPNORM_ALPHA * x + y, g, b)

def adaln_modulation(cond, w_ada, b_ada):
    return jnp.split(jax.nn.silu(cond) @ w_ada + b_ada, N_MOD, axis=-1)

def swiglu(x, w_gu, w_down):
    gate, up = jnp.split(x @ w_gu, 2, axis=-1)
    return (jax.nn.silu(gate) * up) @ w_down

def ffn_sublayer(x, shift, scale, gate, w_gu, w_down, g, b):
    y = swiglu(modulate(x, shift, scale), w_gu, w_down)
    return deepnorm_residual(x, MACARON_WEIGHT * gate * y, g, b)

def depthwise_conv(x, w):
    k = w.shape[0]
    return lax.conv_general_dilated(
        x, w[:, None, :], window_strides=(1,), padding=[(k // 2, k // 2)],
        dimension_numbers=('NWC', 'WIO', 'NWC'), feature_group_count=x.shape[-1])

def axial_rope_tables(rows, head_dim, dtype):
    row = jnp.repeat(jnp.arange(rows, dtype=jnp.float32), GRID_W)
    col = jnp.tile(jnp.arange(GRID_W, dtype=jnp.float32), rows)
    n_freq = head_dim // 4
    inv_freq = jnp.float32(ROPE_THETA) ** (-jnp.arange(n_freq, dtype=jnp.float32) / n_freq)
    ang = jnp.concatenate([row[:, None] * inv_freq, col[:, None] * inv_freq], axis=-1)
    return jnp.cos(ang).astype(dtype), jnp.sin(ang).astype(dtype)

def apply_rope(x, cos, sin):
    x1, x2 = x[..., 0::2], x[..., 1::2]
    c, s = cos[:, None, :], sin[:, None, :]
    return jnp.stack([x1 * c - x2 * s, x1 * s + x2 * c], axis=-1).reshape(x.shape)

def gated_delta_chunked(q, k, v, g, beta, state0):
    B, L, H, dk = q.shape
    dv = v.shape[-1]
    C = GDN_CHUNK
    n = L // C
    f32 = jnp.float32

    def to_chunks(t):
        t = t.astype(f32).reshape((B, n, C, H) + t.shape[3:])
        return jnp.moveaxis(t, (1, 3), (0, 2))

    qc = to_chunks(q) * (dk ** -0.5)
    kc, vc = to_chunks(k), to_chunks(v)
    gcum = jnp.cumsum(to_chunks(g), axis=-1)
    bc = to_chunks(beta)
    tril = jnp.tril(jnp.ones((C, C), dtype=bool))
    strict = jnp.tril(jnp.ones((C, C), dtype=bool), -1)
    diff = gcum[..., :, None] - gcum[..., None, :]
    decay = jnp.where(tril, jnp.exp(jnp.where(tril, diff, 0.0)), 0.0)
    k_beta = kc * bc[..., None]
    v_beta = vc * bc[..., None]
    m = jnp.where(strict, jnp.einsum('nbhik,nbhjk->nbhij', k_beta, kc) * decay, 0.0)
    a = jnp.eye(C, dtype=f32) + m
    u = lax.linalg.triangular_solve(a, v_beta, left_side=True, lower=True, unit_diagonal=True)
    w = lax.linalg.triangular_solve(a, k_beta * jnp.exp(gcum)[..., None],
                                    left_side=True, lower=True, unit_diagonal=True)
    attn_intra = jnp.where(tril, jnp.einsum('nbhik,nbhjk->nbhij', qc, kc) * decay, 0.0)
    g_last = gcum[..., -1]
    k_tail = kc * jnp.exp(g_last[..., None] - gcum)[..., None]

    def step(S, inp):
        q_i, u_i, w_i, at_i, gc_i, gl_i, kt_i = inp
        v_new = u_i - w_i @ S
        o = (q_i * jnp.exp(gc_i)[..., None]) @ S + at_i @ v_new
        S = S * jnp.exp(gl_i)[..., None, None] + jnp.swapaxes(kt_i, -1, -2) @ v_new
        return S, o

    S, o = lax.scan(step, state0.astype(f32), (qc, u, w, attn_intra, gcum, g_last, k_tail))
    o = jnp.moveaxis(o, (0, 2), (1, 3)).reshape(B, L, H, dv)
    return o, S

def gdn_bidirectional(q, k, v, g_f, g_b, b_f, b_b, s_f0, s_b0):
    flip = lambda t: jnp.flip(t, axis=1)
    o_f, s_f = gated_delta_chunked(q, k, v, g_f, b_f, s_f0)
    o_b, s_b = gated_delta_chunked(flip(q), flip(k), flip(v), flip(g_b), flip(b_b), s_b0)
    return o_f + flip(o_b), s_f, s_b

def gdn_gates(ab, a_log, dt_bias):
    B, L, _ = ab.shape
    af = ab.astype(jnp.float32)
    a = af[..., :2 * GDN_HEADS].reshape(B, L, 2, GDN_HEADS)
    b = af[..., 2 * GDN_HEADS:].reshape(B, L, 2, GDN_HEADS)
    g = -jnp.exp(a_log.astype(jnp.float32)) * jax.nn.softplus(a + dt_bias.astype(jnp.float32))
    beta = jax.nn.sigmoid(b)
    return g[:, :, 0], g[:, :, 1], beta[:, :, 0], beta[:, :, 1]

def even_mixer(h_lat, h_ctx, w_in, qkv_conv, a_log, dt_bias, out_norm,
               dw_conv, dw_bias, cln_g, cln_b, w_out, need_ctx):
    def project(h):
        B, L, _ = h.shape
        qkv, z, ab, glu = jnp.split(h @ w_in, EVEN_SPLITS, axis=-1)
        qkv = jax.nn.silu(depthwise_conv(qkv, qkv_conv))
        q, k, v = [t.reshape(B, L, GDN_HEADS, GDN_HEAD_DIM) for t in jnp.split(qkv, 3, axis=-1)]
        scan_in = (l2_normalize(q), l2_normalize(k), v) + gdn_gates(ab, a_log, dt_bias)
        return scan_in, z, glu

    def conformer(glu):
        val, gate = jnp.split(glu, 2, axis=-1)
        y = depthwise_conv(val * jax.nn.sigmoid(gate), dw_conv) + dw_bias
        return jax.nn.silu(layer_norm_2(y, cln_g, cln_b))

    def merge(o, z, glu):
        B, L, _ = z.shape
        o = rms_norm_2(o, out_norm).astype(z.dtype) * jax.nn.silu(z.reshape(B, L, GDN_HEADS, GDN_HEAD_DIM))
        return jnp.concatenate([o.reshape(B, L, GDN_WIDTH), conformer(glu)], axis=-1) @ w_out

    ctx_in, z_c, glu_c = project(h_ctx)
    lat_in, z_l, glu_l = project(h_lat)
    zeros = jnp.zeros((h_ctx.shape[0], GDN_HEADS, GDN_HEAD_DIM, GDN_HEAD_DIM), jnp.float32)
    o_c, s_f, s_b = gdn_bidirectional(*ctx_in, zeros, zeros)
    o_l, _, _ = gdn_bidirectional(*lat_in, s_f, s_b)
    lat_out = merge(o_l, z_l, glu_l)
    ctx_out = merge(o_c, z_c, glu_c) if need_ctx else None
    return lat_out, ctx_out

def gqa_attend(q, k, v):
    s = jnp.einsum('bqhgd,blhd->bhgql', q, k).astype(jnp.float32) * (ATT_HEAD_DIM ** -0.5)
    p = jax.nn.softmax(s, axis=-1).astype(v.dtype)
    return jnp.einsum('bhgql,blhd->bqhgd', p, v)

def odd_mixer(h_lat, h_ctx, w_in, q_norm, k_norm, w_out, rope_cos, rope_sin, need_ctx):
    hd = ATT_HEAD_DIM

    def project(h):
        B, L, _ = h.shape
        q, k, v = jnp.split(h @ w_in, [ATT_HEADS * hd, (ATT_HEADS + ATT_KV_HEADS) * hd], axis=-1)
        q = rms_norm_2(q.reshape(B, L, ATT_HEADS, hd), q_norm)
        k = rms_norm_2(k.reshape(B, L, ATT_KV_HEADS, hd), k_norm)
        return q, k, v.reshape(B, L, ATT_KV_HEADS, hd)

    q_c, k_c, v_c = project(h_ctx)
    q_l, k_l, v_l = project(h_lat)
    q_l = apply_rope(q_l, rope_cos, rope_sin)
    k_l = apply_rope(k_l, rope_cos, rope_sin)
    B, L = h_lat.shape[:2]
    k_all = jnp.concatenate([k_l, k_c], axis=1)
    v_all = jnp.concatenate([v_l, v_c], axis=1)
    n_blk = L // ATT_BLOCK
    q_blocks = q_l.reshape(B, n_blk, ATT_BLOCK, ATT_KV_HEADS, ATT_GROUP, hd).swapaxes(0, 1)
    o = lax.map(lambda qb: gqa_attend(qb, k_all, v_all), q_blocks)
    lat_out = o.swapaxes(0, 1).reshape(B, L, ODD_OUT) @ w_out
    ctx_out = None
    if need_ctx:
        Bc, Lc = h_ctx.shape[:2]
        o_c = gqa_attend(q_c.reshape(Bc, Lc, ATT_KV_HEADS, ATT_GROUP, hd), k_c, v_c)
        ctx_out = o_c.reshape(Bc, Lc, ODD_OUT) @ w_out
    return lat_out, ctx_out

def second_inputs(seed: int = 0) -> dict:
    key = jax.random.key(seed)
    ks = jax.random.split(key, 32)
    f32 = jnp.float32
    nrm = lambda k, shape, s: jax.random.normal(k, shape, f32) * s
    dt = jnp.exp(jax.random.uniform(ks[13], (N_EVEN, 2, GDN_HEADS), f32, math.log(1e-3), math.log(1e-1)))
    return {
        "x": nrm(ks[0], (BATCH, SEQ, D_MODEL), 1.0),
        "c": nrm(ks[1], (BATCH, D_MODEL), 1.0),
        "ctx": nrm(ks[2], (BATCH, CTX_LEN, D_MODEL), 1.0),
        "c_ctx": nrm(ks[3], (D_MODEL,), 1.0),
        "ada_w": nrm(ks[4], (DEPTH, D_MODEL, N_MOD * D_MODEL), 0.5 * D_MODEL ** -0.5),
        "ada_b": nrm(ks[5], (DEPTH, N_MOD * D_MODEL), 0.02),
        "ln_g": 1.0 + nrm(ks[6], (DEPTH, 3, D_MODEL), 0.02),
        "ln_b": nrm(ks[7], (DEPTH, 3, D_MODEL), 0.02),
        "ffn_w_gu": nrm(ks[8], (DEPTH, 2, D_MODEL, 2 * D_FF), D_MODEL ** -0.5),
        "ffn_w_down": nrm(ks[9], (DEPTH, 2, D_FF, D_MODEL), DEEPNORM_BETA * D_FF ** -0.5),
        "even_w_in": nrm(ks[10], (N_EVEN, D_MODEL, EVEN_IN), D_MODEL ** -0.5),
        "even_qkv_conv": nrm(ks[11], (N_EVEN, GDN_CONV, 3 * GDN_WIDTH), GDN_CONV ** -0.5),
        "gdn_a_log": jnp.log(jax.random.uniform(ks[12], (N_EVEN, 2, GDN_HEADS), f32, 1.0, 16.0)),
        "gdn_dt_bias": dt + jnp.log(-jnp.expm1(-dt)),
        "gdn_out_norm": 1.0 + nrm(ks[14], (N_EVEN, GDN_HEAD_DIM), 0.02),
        "cf_dw_conv": nrm(ks[15], (N_EVEN, CONV_WIDTH, CONV_CH), CONV_WIDTH ** -0.5),
        "cf_dw_bias": nrm(ks[16], (N_EVEN, CONV_CH), 0.02),
        "cf_ln_g": 1.0 + nrm(ks[17], (N_EVEN, CONV_CH), 0.02),
        "cf_ln_b": nrm(ks[18], (N_EVEN, CONV_CH), 0.02),
        "even_w_out": nrm(ks[19], (N_EVEN, EVEN_OUT, D_MODEL), DEEPNORM_BETA * EVEN_OUT ** -0.5),
        "attn_w_in": nrm(ks[20], (N_ODD, D_MODEL, ODD_IN), D_MODEL ** -0.5),
        "attn_q_norm": 1.0 + nrm(ks[21], (N_ODD, ATT_HEAD_DIM), 0.02),
        "attn_k_norm": 1.0 + nrm(ks[22], (N_ODD, ATT_HEAD_DIM), 0.02),
        "attn_w_out": nrm(ks[23], (N_ODD, ODD_OUT, D_MODEL), DEEPNORM_BETA * ODD_OUT ** -0.5),
    }

def second_block(x, c, ctx, c_ctx, ada_w, ada_b, ln_g, ln_b, ffn_w_gu, ffn_w_down,
              even_w_in, even_qkv_conv, gdn_a_log, gdn_dt_bias, gdn_out_norm,
              cf_dw_conv, cf_dw_bias, cf_ln_g, cf_ln_b, even_w_out,
              attn_w_in, attn_q_norm, attn_k_norm, attn_w_out):
    rows = x.shape[1] // GRID_W
    rope_cos, rope_sin = axial_rope_tables(rows, ATT_HEAD_DIM, x.dtype)
    for layer in range(DEPTH):
        last = layer == DEPTH - 1
        i = layer // 2
        mods_lat = [m[:, None, :] for m in adaln_modulation(c, ada_w[layer], ada_b[layer])]
        mods_ctx = adaln_modulation(c_ctx, ada_w[layer], ada_b[layer])
        x = ffn_sublayer(x, *mods_lat[0:3], ffn_w_gu[layer, 0], ffn_w_down[layer, 0], ln_g[layer, 0], ln_b[layer, 0])
        ctx = ffn_sublayer(ctx, *mods_ctx[0:3], ffn_w_gu[layer, 0], ffn_w_down[layer, 0], ln_g[layer, 0], ln_b[layer, 0])
        h_lat = modulate(x, *mods_lat[3:5])
        h_ctx = modulate(ctx, *mods_ctx[3:5])
        if layer % 2 == 0:
            o_lat, o_ctx = even_mixer(h_lat, h_ctx, even_w_in[i], even_qkv_conv[i], gdn_a_log[i], gdn_dt_bias[i],
                                      gdn_out_norm[i], cf_dw_conv[i], cf_dw_bias[i], cf_ln_g[i], cf_ln_b[i],
                                      even_w_out[i], not last)
        else:
            o_lat, o_ctx = odd_mixer(h_lat, h_ctx, attn_w_in[i], attn_q_norm[i], attn_k_norm[i], attn_w_out[i],
                                     rope_cos, rope_sin, not last)
        x = deepnorm_residual(x, mods_lat[5] * o_lat, ln_g[layer, 1], ln_b[layer, 1])
        x = ffn_sublayer(x, *mods_lat[6:9], ffn_w_gu[layer, 1], ffn_w_down[layer, 1], ln_g[layer, 2], ln_b[layer, 2])
        if not last:
            ctx = deepnorm_residual(ctx, mods_ctx[5] * o_ctx, ln_g[layer, 1], ln_b[layer, 1])
            ctx = ffn_sublayer(ctx, *mods_ctx[6:9], ffn_w_gu[layer, 1], ffn_w_down[layer, 1], ln_g[layer, 2], ln_b[layer, 2])
    return x


def setup_inputs(seed=0):
    out = dict(first_inputs(seed))
    for name, value in second_inputs(seed + 1).items():
        if name != "x":
            out[name + "_2"] = value
    return out


def reference(
    x, w_in, q_norm_g, w_q_up, kv_norm_g, w_uk, w_uv, w_o, ln1_g, ln1_b, router_w, router_bias,
    w_gate, w_up, w_down, ln2_g, ln2_b, c_2, ctx_2, c_ctx_2, ada_w_2, ada_b_2, ln_g_2, ln_b_2,
    ffn_w_gu_2, ffn_w_down_2, even_w_in_2, even_qkv_conv_2, gdn_a_log_2, gdn_dt_bias_2,
    gdn_out_norm_2, cf_dw_conv_2, cf_dw_bias_2, cf_ln_g_2, cf_ln_b_2, even_w_out_2, attn_w_in_2,
    attn_q_norm_2, attn_k_norm_2, attn_w_out_2,
):
    x = first_block(
        x, w_in, q_norm_g, w_q_up, kv_norm_g, w_uk, w_uv, w_o, ln1_g, ln1_b, router_w,
        router_bias, w_gate, w_up, w_down, ln2_g, ln2_b,
    )
    return second_block(
        x, c_2, ctx_2, c_ctx_2, ada_w_2, ada_b_2, ln_g_2, ln_b_2, ffn_w_gu_2, ffn_w_down_2,
        even_w_in_2, even_qkv_conv_2, gdn_a_log_2, gdn_dt_bias_2, gdn_out_norm_2, cf_dw_conv_2,
        cf_dw_bias_2, cf_ln_g_2, cf_ln_b_2, even_w_out_2, attn_w_in_2, attn_q_norm_2,
        attn_k_norm_2, attn_w_out_2,
    )


_drawn_inputs = setup_inputs


def setup_inputs(seed=0):
    import zlib

    import numpy as np

    out = dict(_drawn_inputs(seed))
    spreads = {}
    factors = {'q_norm_g': 8.0,
     'kv_norm_g': 8.0,
     'router_bias': 4.081,
     'ctx_2': 7.544,
     'c_ctx_2': 3.819,
     'ada_b_2': 6.797,
     'gdn_a_log_2': 8.0,
     'gdn_dt_bias_2': 3.738,
     'gdn_out_norm_2': 33.965,
     'cf_dw_bias_2': 8.0,
     'cf_ln_g_2': 34.213,
     'cf_ln_b_2': 32.575,
     'attn_q_norm_2': 24.559,
     'attn_k_norm_2': 29.685}
    for name, (base, spread) in spreads.items():
        noise = np.random.default_rng([zlib.crc32(name.encode()), seed]).standard_normal(out[name].shape)
        drawn = base * np.exp(spread * noise) if base else spread * noise
        out[name] = __import__('jax').numpy.asarray(drawn.astype(out[name].dtype))
    for name, factor in factors.items():
        out[name] = (out[name] * factor).astype(out[name].dtype)
    return out
```

```python
from contextlib import ExitStack

import numpy as np

import concourse.bass as bass
from concourse import mybir

F32 = mybir.dt.float32
ALU = mybir.AluOpType
ACT = mybir.ActivationFunctionType
AXX = mybir.AxisListType.X

P = 128
D = 1024
DC = D // P
T = 256
TT = T // P
N2 = 2 * T
DEPTH = 2
H = 8
Q_LORA, KV_LORA = 384, 256
NOPE, ROPE_D, VD = 64, 32, 64
QC, KVC = Q_LORA // P, KV_LORA // P
IDX_DIM = 32
KEEP = T // 4
E_N, E_F = 16, 512
MOE_CH = E_N * E_F // P
DFF = 2816
FF_CH = DFF // P
GH, GD = 4, 128
GCONV, CCONV = 5, 31
CCH = 4
AH, AKV, AD = 8, 2, 128
N_MOD = 9
LEVELS = 7
ATANH_TERMS = 8
ALPHA = (2.0 * DEPTH) ** 0.25
LN_EPS, RMS_EPS = 1e-5, 1e-6
NEG = -1.0e30
TAKEN = -3.0e38
SLOTS = 4
UNIT = 2048
SLOPES = [2.0 ** (-8.0 * (h + 1) / H) for h in range(H)]


def columns(parts):
    table, at = {}, 0
    for name, n in parts:
        table[name] = (at, n)
        at += n
    return table, at


PER_LAYER = (("qg", QC), ("kvg", KVC), ("ln1g", DC), ("ln1b", DC), ("ln2g", DC), ("ln2b", DC), ("adab", N_MOD * DC),
             ("lng0", DC), ("lnb0", DC), ("lng1", DC), ("lnb1", DC), ("lng2", DC), ("lnb2", DC))
COLS, NCOLS = columns([(f"{n}{layer}", c) for layer in range(DEPTH) for n, c in PER_LAYER] + [
    ("cond", 2 * DC), ("gconv", 12 * GCONV), ("cconv", CCH * CCONV), ("cbias", CCH), ("clng", CCH), ("clnb", CCH),
    ("qn", 1), ("kn", 1), ("rbias", E_N), ("alog", 2 * GH), ("dtb", 2 * GH), ("outn", GD), ("rw", DC * E_N)])
CONS, NCONS = columns([
    ("ident", P), ("ones", P), ("perm32", P), ("permA", P), ("cos32", T), ("sin32", T), ("cosA", T), ("sinA", T),
    ("causal", TT * T), ("dist", TT * T), ("first4", 4), ("first16", E_N), ("tri0", P), ("tri1", P),
    ("lvl0", LEVELS * P), ("lvl1", LEVELS * P)])


class Stage:

    def __init__(self, name, base, marks):
        self.name, self.base, self.u0 = name, dict(base), None
        self.names, self.total, self.seen = {}, {}, {"pe": 0, "act": 0, "dve": 0}
        for eng in ("pe", "act", "dve"):
            m = marks.get(eng, [])
            self.names[eng] = {} if isinstance(m, int) else {n: i + 1 for i, n in enumerate(m)}
            self.total[eng] = (m if isinstance(m, int) else len(m)) + 1

    def v(self, eng, name):
        return self.base[eng] + (name if isinstance(name, int) else self.names[eng][name])

    def one(self, eng, name):
        self.seen[eng] += 1
        assert self.names[eng][name] == self.seen[eng], (self.name, eng, name, self.seen[eng])
        return 1


class Chain:

    def __init__(self, eng, step):
        self.eng, self.step, self.n = eng, step, 0

    def __call__(self, ins):
        ins.then_inc(self.step, 1)
        self.n += 1
        self.eng.wait_ge(self.step, self.n)

    def inside(self, i, per_turn):
        c = Chain(self.eng, self.step)
        c.n = self.n + i * per_turn
        return c


def outer(ap, n):
    return ap.unsqueeze(1).broadcast_to([P, n, ap.shape[-1]])


def inner(ap, n):
    return ap.unsqueeze(2).broadcast_to([P, ap.shape[-1], n])


def build(nc, w, out):
    with ExitStack() as ctx:
        def sb(name, shape):
            return ctx.enter_context(nc.sbuf_tensor(name, shape, F32))

        def sem(name):
            return ctx.enter_context(nc.semaphore(name))

        ring = sb("ring", [P, SLOTS, UNIT])
        cols = sb("cols", [P, NCOLS])
        cons = sb("cons", [P, NCONS])
        X = sb("X", [P, DC, N2])
        HM = sb("HM", [P, DC, N2])
        Y = sb("Y", [P, DC, N2])
        MD = sb("MD", [P, N_MOD, DC, 2])
        condT = sb("condT", [P, DC, 2])
        row = sb("row", [P, 2, N2])
        small = sb("small", [P, 32])
        AREA = 24000
        area = sb("area", [P, AREA])
        ps = ctx.enter_context(nc.psum_tensor("ps", [P, 8, 512], F32))

        pe_done, act_done, dve_done = sem("pe_done"), sem("act_done"), sem("dve_done")
        act_step, dve_step = sem("act_step"), sem("dve_step")
        arrived = [sem(f"arrived{i}") for i in range(SLOTS)]
        tables_in, zeroed, out_done = sem("tables_in"), sem("zeroed"), sem("out_done")

        def col(name, i=0, n=1):
            a = COLS[name][0] + i
            return cols[:, a:a + n]

        def con(name, a=0, n=None):
            s, c = CONS[name]
            return cons[:, s + a:s + (c if n is None else a + n)]

        ident, ones = con("ident"), con("ones")

        class Space:

            def __init__(self, at=0, end=AREA, base=area):
                self.at, self.end, self.base = at, end, base

            def take(self, *shape):
                n = int(np.prod(shape))
                v = self.base[:, self.at:self.at + n]
                self.at += n
                assert self.at <= self.end, self.at
                names = "abcd"[:len(shape)]
                if len(shape) > 1:
                    v = v.rearrange(f"p ({' '.join(names)}) -> p {' '.join(names)}", **dict(zip(names, shape)))
                return v

        s = Space()
        hid_moe = s.take(MOE_CH, T)
        gate_b = s.take(E_N, T)
        sg = s.take(2, N2)
        gated = s.take(2, T)
        hid_ff = Space().take(FF_CH, N2)
        s = Space()
        selE = s.take(E_N, P)
        G128, gT, R = s.take(TT, P), s.take(TT * P), s.take(16, 2 * E_N)
        s = Space()
        QA, KVA, DQ, IQ, KR = s.take(QC, T), s.take(KVC, T), s.take(4, T), s.take(2, T), s.take(T)
        padded_from = s.at
        IKz, DKz, KRz, KNz = s.take(4, T), s.take(2, T), s.take(4, T), s.take(4, 2, T)
        DVz, Vz = s.take(TT, 2, P), s.take(TT, H, P)
        zero_padded = area[:, padded_from:s.at]
        IW, QN, QR = s.take(TT, H), s.take(4, T), s.take(2, T)
        S1, PT = s.take(2048), s.take(16, P)
        SC, SB, top8 = s.take(2, T), s.take(H, T), s.take(8)
        OT1 = HM[:, :, 0:T]
        s = Space()
        CI = s.take(12, 2, T + GCONV - 1)
        QKV = s.take(12, N2)
        pair_at = s.at
        GL, VAL = s.take(CCH, 2, T + CCONV - 1), s.take(CCH, N2)
        pair_end = s.at
        Zr, AB, Gg, Bb = s.take(4, 512), s.take(4, 16), s.take(4, 8), s.take(4, 8)
        St, CF = s.take(2, GH * P), s.take(CCH, N2)
        gp = s.take(4, 40)
        SGt = s.take(N2)
        small2 = small
        Yf = Y[:].rearrange("p a b -> p (a b)")
        tail_at = s.at
        s = Space()
        rowK, rowV, OR = s.take(4, GH, P), s.take(4, GH, P), s.take(4, GH, P)
        assert s.at <= 12 * 2 * (T + GCONV - 1)
        big = [Y[:].rearrange("p a b -> p (a b)"), HM[:].rearrange("p a b -> p (a b)")]
        half = (pair_end - pair_at) // 2

        def per_direction(d):
            a, b = Space(0, 4096, big[d]), Space(pair_at + d * half, pair_at + (d + 1) * half)
            names = ("gB", "bB", "DEC", "MT", "AT", "XT", "Xi", "R")
            got = {n: a.take(GH, P) for n in names}
            got.update({n: b.take(GH, P) for n in ("Yv", "QS", "ET0", "ET1")})
            got["VB"] = Space(tail_at + d * 544).take(GH, P)
            got["sm"] = Space(tail_at + d * 544 + 512).take(32)
            return got

        DN = [per_direction(0), per_direction(1)]
        s = Space()
        AQ, AK, SQq, SQk = s.take(AH, T), s.take(AKV, N2), s.take(AH, T), s.take(AKV, N2)
        AV, S2, PT2 = s.take(4, AKV * AD), s.take(2048), s.take(16, P)
        OT2 = HM[:, :, 0:T]

        now = {"pe": 0, "act": 0, "dve": 0}
        stages, streams, unit_count = {}, [], [0]

        def stage(name, **marks):
            st = Stage(name, now, marks)
            for k in now:
                now[k] += st.total[k]
            stages[name] = st
            return st

        def stream(st, tensor, n, first, step, width=UNIT):
            if st.u0 is None:
                st.u0 = unit_count[0]
            streams.append((tensor, n, st.base["pe"] + first, step, width, unit_count[0]))
            unit_count[0] += n

        def ln_stage(name):
            stage(name, pe=["mean", "var"], act=["mean", *[f"sq{k}" for k in range(DC)], "root"], dve=["centred", "eps"])

        def attention_stage(name):
            stage(name, pe=["scores", "turned", "mixed"], act=["exp", "turned", "out"], dve=["ready", "probs"])

        def ffn_stages(name, chunks, wu, wd):
            stream(stage(name + "up", pe=2 * chunks, act=chunks, dve=chunks), wu, chunks, 2, 2)
            stream(stage(name + "down", pe=chunks // 2), wd, chunks // 2, 1, 1)

        for l in range(DEPTH):
            n = f"b1.{l}."
            st = stage(n + "in", pe=[f"c{c}" for c in range(14)] + ["rows"], act=[f"c{c}" for c in range(14)] + ["rows"], dve=["zeroed"])
            stream(st, w["w_in"][l], 7, 2, 2)
            stream(st, w["w_in_rows"][l], 1, 15, 1, DC * 72)
            stage(n + "rms", pe=["sums"], act=["sq", "root"], dve=["eps"])
            st = stage(n + "up", pe=[f"c{c}" for c in range(10)] + ["rows"], act=[f"c{c}" for c in range(10)] + ["rows"])
            stream(st, w["w_q_up"][l], 2, 3, 3, 3 * QC * P)
            stream(st, w["w_ukv"][l], 1, 11, 1)
            stage(n + "rope", pe=["swapped"])
            for t in range(TT):
                stage(f"{n}index{t}", pe=["scores"], act=["relu"])
                attention_stage(f"{n}mla{t}")
                attention_stage(f"{n}dsa{t}")
            stream(stage(n + "out", pe=DC), w["w_o"][l], DC // 2, 2, 2)
            ln_stage(n + "ln1")
            stage(n + "router", pe=["logits", "turned", "spread0", "spread1"], act=["exp", "turned", "spread0", "spread1"], dve=["gates"])
            ffn_stages(n + "moe.", MOE_CH, w["moe_up"][l], w["moe_down"][l])
            ln_stage(n + "ln2")
        for l in range(DEPTH):
            n = f"b2.{l}."
            stream(stage(n + "ada", pe=4 * N_MOD, dve=2 * N_MOD), w["ada"][l], 4 * N_MOD, 1, 1)
            stage(n + "mod0")
            ffn_stages(n + "ffn0.", FF_CH, w["ff_up"][l, 0], w["ff_down"][l, 0])
            ln_stage(n + "ln0")
            stage(n + "mod1")
            if l == 0:
                order = [f"c{c}" for c in range(20)]
                st = stage(n + "in", pe=order + ["ab", "z"], act=order + ["ab", "z"], dve=["g0", "g1", "g2", "g3"])
                stream(st, w["even_in"], 10, 2, 2)
                stream(st, w["even_ab"], 1, 21, 1, DC * 16)
                stream(st, w["even_z"], 2, 22, 0)
                stage(n + "conv", act=[f"silu{c}" for c in range(12)] + ["ln", "sq", "root"], pe=["mean", "var"],
                      dve=[f"c{c}" for c in range(12)] + ["y", "centred", "eps", "normed"])
                stage(n + "l2", pe=["sums"], act=["sq", "root"], dve=["eps"])
                stage(n + "rows", pe=["k0", "v0", "k1", "v1", "k2", "v2", "k3", "v3"],
                      act=["exp", "k0", "v0", "k1", "v1", "k2", "v2", "k3", "v3"], dve=["dt"])
                for i in range(4):
                    both = lambda *names: [f"{x}.{d}" for x in names for d in range(2)]
                    lv = [x for j in range(LEVELS) for x in both(f"Y{j}", f"Z{j}")]
                    stage(f"{n}scan{i}", pe=both("A", "B") + lv + both("V", "O"),
                          act=both("exp") + both("qs") + both(*[f"Y{j}" for j in range(LEVELS)]) + both("vn"),
                          dve=both("inp") + both("dec") + both("mt") + both("at") + both(*[f"X{j}" for j in range(LEVELS)]))
                stage(n + "merge", pe=["turned"], act=["sq", "root"], dve=["eps", "ready"])
            else:
                order = [f"q{c}" for c in range(AH)] + [f"k{c}" for c in range(AKV)] + ["v"]
                st = stage(n + "in", pe=order, act=order)
                stream(st, w["attn_in"], 5, 2, 2)
                stream(st, w["attn_v"], 1, 11, 1)
                stage(n + "rms", pe=["sums"], act=["sq", "root"], dve=["eps"])
                stage(n + "rope", pe=["swapped"])
                for t in range(TT):
                    for h in range(AKV):
                        attention_stage(f"{n}gqa{t}{h}")
            stream(stage(n + "out", pe=DC), w["even_out"] if l == 0 else w["attn_out"], DC // 2, 2, 2)
            ln_stage(n + "ln1")
            stage(n + "mod2")
            ffn_stages(n + "ffn1.", FF_CH, w["ff_up"][l, 1], w["ff_down"][l, 1])
            ln_stage(n + "ln2")

        def enter(eng, name):
            st = stages[name]
            if st.base["pe"]:
                eng.wait_ge(pe_done, st.base["pe"])
                eng.wait_ge(act_done, st.base["act"])
                eng.wait_ge(dve_done, st.base["dve"])
            return st

        def fill_ring(sp):
            released = []
            for tensor, n, first, step, width, u0 in streams:
                released += [first + c * step for c in range(n)]
            for tensor, n, first, step, width, u0 in streams:
                turns = max(0, n - SLOTS) // SLOTS
                head = SLOTS if turns > 1 else n
                if turns <= 1:
                    turns = 0

                def load(c, j, free):
                    if free is not None:
                        sp.wait_ge(pe_done, free)
                    sp.dma_start(ring[:, (u0 + j) % SLOTS, 0:width], tensor[c]).then_inc(arrived[(u0 + j) % SLOTS], 16)

                for c in range(head):
                    u = u0 + c
                    load(c, c, released[u - SLOTS] if u >= SLOTS else None)
                if turns:
                    with sp.Fori(0, turns) as i:
                        for j in range(SLOTS):
                            load(SLOTS * i + SLOTS + j, j, first + j * step + SLOTS * step * i)
                for c in range(head + SLOTS * turns, n):
                    load(c, c, released[u0 + c - SLOTS])

        def unit_here(pe, u, i=None):
            value = 16 * (u // SLOTS + 1)
            pe.wait_ge(arrived[u % SLOTS], value if i is None else value + 16 * i)
            return ring[:, u % SLOTS, :]

        def dot(pe, dst, pairs):
            for n, (a, b) in enumerate(pairs):
                ins = pe.matmul(dst, a, b, start=(n == 0), stop=(n == len(pairs) - 1))
            return ins

        def ffn_up_pe(pe, name, chunks, n, src):
            st = enter(pe, name)

            def chunk(j, i, free):
                wt = unit_here(pe, st.u0 + j, i)
                if free is not None:
                    pe.wait_ge(dve_done, free)
                for half_ in range(2):
                    b = 2 * (j % 2) + half_
                    dot(pe, ps[:, b, 0:n], [(wt[:, half_ * D + k * P:half_ * D + (k + 1) * P], src[:, k, 0:n])
                                            for k in range(DC)]).then_inc(pe_done, 1)

            for j in range(SLOTS):
                chunk(j, None, st.v("dve", j - 1) if j >= 2 else None)
            turns = chunks // SLOTS - 1
            with pe.Fori(0, turns) as i:
                for j in range(SLOTS):
                    chunk(SLOTS + j, i, st.v("dve", SLOTS + j - 1) + SLOTS * i)
            for j in range(SLOTS * (turns + 1), chunks):
                chunk(j, None, st.v("dve", j - 1))
            pe.drain().then_inc(pe_done, 1)

        def ffn_up_act(act, name, chunks, n):
            st = enter(act, name)

            def chunk(j, i, free):
                act.wait_ge(pe_done, st.v("pe", 2 * j + 1) + (0 if i is None else 2 * i))
                if free is not None:
                    act.wait_ge(dve_done, free)
                act.activation(sg[:, j % 2, 0:n], ps[:, 2 * (j % 2), 0:n], ACT.Silu).then_inc(act_done, 1)

            for j in range(2):
                chunk(j, None, None)
            with act.Fori(0, chunks - 2, 2) as i:
                for j in range(2):
                    chunk(2 + j, i, st.v("dve", 1 + j) + i)
            act.drain().then_inc(act_done, 1)

        def ffn_up_dve(dve, link, name, chunks, n, hid, moe):
            st = enter(dve, name)
            per = E_F // P if moe else 2
            with dve.Fori(0, chunks // per) as i:
                c = link.inside(i, per if moe else 0)
                for j in range(per):
                    dve.wait_ge(act_done, st.v("act", j + 1) + per * i)
                    dve.wait_ge(pe_done, st.v("pe", 2 * j + 2) + 2 * per * i)
                    h = hid[:, per * i + j, 0:n]
                    up = ps[:, 2 * (j % 2) + 1, 0:n]
                    if moe:
                        c(dve.tensor_tensor(gated[:, j % 2, :], sg[:, j % 2, 0:n], up, ALU.mult))
                        dve.tensor_tensor(h, gated[:, j % 2, :], gate_b[:, i, :], ALU.mult).then_inc(dve_done, 1)
                    else:
                        dve.tensor_tensor(h, sg[:, j % 2, 0:n], up, ALU.mult).then_inc(dve_done, 1)
            link.n += chunks if moe else 0
            dve.drain().then_inc(dve_done, 1)

        def ffn_down_pe(pe, name, chunks, n, hid):
            st = enter(pe, name)
            total = chunks // 2

            def unit(j, i, c, first, last):
                wt = unit_here(pe, st.u0 + j, i)
                for e in range(2):
                    for d in range(DC):
                        ins = pe.matmul(ps[:, d, 0:n], wt[:, e * D + d * P:e * D + (d + 1) * P], hid[:, c + e, 0:n],
                                        start=first and e == 0, stop=last and e == 1, skip_group_check=True)
                ins.then_inc(pe_done, 1)

            turns = total // SLOTS - 1
            if turns * SLOTS + SLOTS == total:
                turns -= 1
            for j in range(SLOTS):
                unit(j, None, 2 * j, j == 0, False)
            with pe.Fori(0, turns) as i:
                for j in range(SLOTS):
                    unit(SLOTS + j, i, 2 * SLOTS * i + 2 * (SLOTS + j), False, False)
            for j in range(SLOTS * (turns + 1), total):
                unit(j, None, 2 * j, False, j == total - 1)
            pe.drain().then_inc(pe_done, 1)

        def add_residual(dve, link, st, last_mark, gate, n):
            link(dve.tensor_scalar(Y[:, :, 0:n], X[:, :, 0:n], ALPHA, None, ALU.mult))
            if isinstance(last_mark, int):
                dve.wait_ge(pe_done, st.v("pe", last_mark))
            for d in range(DC):
                for part in range(n // T):
                    c = slice(part * T, (part + 1) * T)
                    if gate is None:
                        dve.tensor_tensor(Y[:, d, c], ps[:, d, c], Y[:, d, c], ALU.add)
                    else:
                        dve.scalar_tensor_tensor(Y[:, d, c], ps[:, d, c], MD[:, gate, d, part:part + 1], Y[:, d, c],
                                                 ALU.mult, ALU.add)
            dve.drain().then_inc(dve_done, 1)

        def ffn_down_dve(dve, link, name, chunks, gate, n):
            add_residual(dve, link, enter(dve, name), chunks // 2, gate, n)

        def out_pe(pe, name, src, n):
            st = enter(pe, name)
            for d in range(DC):
                wt = unit_here(pe, st.u0 + d // 2)
                o = (d % 2) * D
                dot(pe, ps[:, d, 0:n], [(wt[:, o + k * P:o + (k + 1) * P], src(k)) for k in range(DC)]).then_inc(pe_done, 1)
            pe.drain().then_inc(pe_done, 1)

        def ln_pe(pe, name, n):
            st = enter(pe, name)
            dot(pe, ps[:, 0, 0:n], [(ones, Y[:, k, 0:n]) for k in range(DC)]).then_inc(pe_done, st.one("pe", "mean"))
            for k in range(DC):
                pe.wait_ge(act_done, st.v("act", f"sq{k}"))
                ins = pe.matmul(ps[:, 1, 0:n], ones, HM[:, k, 0:n], start=(k == 0), stop=(k == DC - 1))
            ins.then_inc(pe_done, st.one("pe", "var"))
            pe.drain().then_inc(pe_done, 1)

        def ln_act(act, name, n):
            st = enter(act, name)
            act.wait_ge(pe_done, st.v("pe", "mean"))
            act.activation(row[:, 0, 0:n], ps[:, 0, 0:n], ACT.Copy, scale=1.0 / D).then_inc(act_done, st.one("act", "mean"))
            act.wait_ge(dve_done, st.v("dve", "centred"))
            for k in range(DC):
                act.activation(HM[:, k, 0:n], Y[:, k, 0:n], ACT.Square).then_inc(act_done, st.one("act", f"sq{k}"))
            act.wait_ge(dve_done, st.v("dve", "eps"))
            act.activation(row[:, 1, 0:n], row[:, 0, 0:n], ACT.Sqrt).then_inc(act_done, st.one("act", "root"))
            act.drain().then_inc(act_done, 1)

        def ln_dve(dve, link, name, n, g, b):
            st = enter(dve, name)
            dve.wait_ge(act_done, st.v("act", "mean"))
            dve.tensor_tensor(Y[:, :, 0:n], Y[:, :, 0:n], outer(row[:, 0, 0:n], DC), ALU.subtract)\
               .then_inc(dve_done, st.one("dve", "centred"))
            dve.wait_ge(pe_done, st.v("pe", "var"))
            dve.tensor_scalar(row[:, 0, 0:n], ps[:, 1, 0:n], 1.0 / D, LN_EPS, ALU.mult, ALU.add)\
               .then_inc(dve_done, st.one("dve", "eps"))
            dve.wait_ge(act_done, st.v("act", "root"))
            link(dve.reciprocal(row[:, 0, 0:n], row[:, 1, 0:n]))
            link(dve.tensor_tensor(Y[:, :, 0:n], Y[:, :, 0:n], outer(row[:, 0, 0:n], DC), ALU.mult))
            for k in range(DC):
                dve.tensor_scalar(X[:, k, 0:n], Y[:, k, 0:n], col(g, k), col(b, k), ALU.mult, ALU.add)
            dve.drain().then_inc(dve_done, 1)

        def modulate(dve, name, shift, scale):
            enter(dve, name)
            for k in range(DC):
                for part in range(2):
                    c = slice(part * T, (part + 1) * T)
                    dve.tensor_scalar(HM[:, k, c], X[:, k, c], MD[:, scale, k, part:part + 1],
                                      MD[:, shift, k, part:part + 1], ALU.mult, ALU.add)
            dve.drain().then_inc(dve_done, 1)

        def idle(eng, done, name):
            enter(eng, name)
            eng.drain().then_inc(done, 1)

        def attention_pe(pe, name, scores, mix, probs, turned):
            st = enter(pe, name)
            width = 2048 // len(scores)
            flat = ps[:].rearrange("p a b -> p (a b)")
            for h, pairs in enumerate(scores):
                ins = dot(pe, flat[:, h * width:(h + 1) * width], pairs)
            ins.then_inc(pe_done, st.one("pe", "scores"))
            pe.wait_ge(dve_done, st.v("dve", "probs"))
            for b in range(16):
                ins = pe.transpose(flat[:, 2048 + b * P:2048 + (b + 1) * P], probs[:, b * P:(b + 1) * P], ident)
            ins.then_inc(pe_done, st.one("pe", "turned"))
            pe.wait_ge(act_done, st.v("act", "turned"))
            for i, terms in enumerate(mix):
                ins = dot(pe, ps[:, 0, i * P:(i + 1) * P], [(v, turned[:, b, :]) for v, b in terms])
            ins.then_inc(pe_done, st.one("pe", "mixed"))
            pe.drain().then_inc(pe_done, 1)

        def attention_act(act, name, probs, turned, dst):
            st = enter(act, name)
            act.wait_ge(dve_done, st.v("dve", "ready"))
            act.activation(probs, probs, ACT.Exp).then_inc(act_done, st.one("act", "exp"))
            act.wait_ge(pe_done, st.v("pe", "turned"))
            act.activation(turned.rearrange("p a b -> p (a b)"), ps[:, 4:8, :].rearrange("p a b -> p (a b)"), ACT.Copy)\
               .then_inc(act_done, st.one("act", "turned"))
            act.wait_ge(pe_done, st.v("pe", "mixed"))
            act.activation(dst, ps[:, 0, :].rearrange("p (a b) -> p a b", a=4), ACT.Copy)\
               .then_inc(act_done, st.one("act", "out"))
            act.drain().then_inc(act_done, 1)

        def attention_dve(dve, link, name, heads, probs, scale, mask):
            st = enter(dve, name)
            keys = 2048 // heads
            s3 = probs.rearrange("p (h k) -> p h k", h=heads)
            p3 = ps[:, 0:4, :].rearrange("p a b -> p (a b)").rearrange("p (h k) -> p h k", h=heads)
            mx, total = small[:, 0:heads], small[:, 8:8 + heads]
            dve.wait_ge(pe_done, st.v("pe", "scores"))
            if mask is None:
                link(dve.tensor_scalar(s3, p3, scale, None, ALU.mult))
            else:
                link(dve.scalar_tensor_tensor(s3, p3, scale, mask, ALU.mult, ALU.add))
            link(dve.tensor_reduce(mx, s3, AXX, ALU.max))
            dve.tensor_tensor(s3, s3, inner(mx, keys), ALU.subtract).then_inc(dve_done, st.one("dve", "ready"))
            dve.wait_ge(act_done, st.v("act", "exp"))
            link(dve.tensor_reduce(total, s3, AXX, ALU.add))
            link(dve.reciprocal(mx, total))
            dve.tensor_tensor(s3, s3, inner(mx, keys), ALU.mult).then_inc(dve_done, st.one("dve", "probs"))
            dve.drain().then_inc(dve_done, 1)

        def in1_pe(pe, n):
            st = enter(pe, n)
            for c in range(14):
                wt = unit_here(pe, st.u0 + c // 2)
                if c >= 8:
                    pe.wait_ge(act_done, st.v("act", f"c{c - 8}"))
                o = (c % 2) * D
                dot(pe, ps[:, c % 8, 0:T], [(wt[:, o + k * P:o + (k + 1) * P], X[:, k, 0:T]) for k in range(DC)])\
                    .then_inc(pe_done, st.one("pe", f"c{c}"))
            wt = unit_here(pe, st.u0 + 7)
            pe.wait_ge(act_done, st.v("act", "c7"))
            for t in range(TT):
                ins = dot(pe, ps[:, 6 + t, 0:72], [(X[:, k, t * P:(t + 1) * P], wt[:, k * 72:(k + 1) * 72]) for k in range(DC)])
            ins.then_inc(pe_done, st.one("pe", "rows"))
            pe.drain().then_inc(pe_done, 1)

        def copy_marked(act, st, bank, pairs, mark):
            act.wait_ge(pe_done, st.v("pe", mark))
            for dst, src in pairs:
                ins = act.activation(dst, src, ACT.Copy)
            ins.then_inc(act_done, st.one("act", mark))

        def in1_act(act, n):
            st = enter(act, n)
            plain = [QA[:, 0, :], QA[:, 1, :], QA[:, 2, :], KVA[:, 0, :], KVA[:, 1, :],
                     *[DQ[:, i, :] for i in range(4)], IQ[:, 0, :], IQ[:, 1, :], KR]
            for c, dst in enumerate(plain):
                copy_marked(act, st, c % 8, [(dst, ps[:, c % 8, 0:T])], f"c{c}")
            act.wait_ge(dve_done, st.v("dve", "zeroed"))
            copy_marked(act, st, 4, [(IKz[32 * j:32 * j + 32, j, :], ps[32 * j:32 * j + 32, 4, 0:T]) for j in range(4)], "c12")
            copy_marked(act, st, 5, [(DKz[64 * j:64 * j + 64, j, :], ps[64 * j:64 * j + 64, 5, 0:T]) for j in range(2)], "c13")
            act.wait_ge(pe_done, st.v("pe", "rows"))
            for t in range(TT):
                act.activation(IW[:, t, :], ps[:, 6 + t, 0:H], ACT.Copy, scale=H ** -0.5)
                for e in range(2):
                    ins = act.activation(DVz[:, t, e, e * VD:(e + 1) * VD], ps[:, 6 + t, H:H + VD], ACT.Copy)
            ins.then_inc(act_done, st.one("act", "rows"))
            act.drain().then_inc(act_done, 1)

        def in1_dve(dve, n):
            st = enter(dve, n)
            dve.memset(zero_padded, 0.0).then_inc(dve_done, st.one("dve", "zeroed"))
            dve.drain().then_inc(dve_done, 1)

        def rms1_pe(pe, n):
            st = enter(pe, n)
            pe.wait_ge(act_done, st.v("act", "sq"))
            dot(pe, ps[:, 0, 0:T], [(ones, HM[:, k, 0:T]) for k in range(QC)])
            dot(pe, ps[:, 1, 0:T], [(ones, HM[:, QC + k, 0:T]) for k in range(KVC)]).then_inc(pe_done, st.one("pe", "sums"))
            pe.drain().then_inc(pe_done, 1)

        def rms1_act(act, n):
            st = enter(act, n)
            act.activation(HM[:, 0:QC, 0:T], QA, ACT.Square)
            act.activation(HM[:, QC:QC + KVC, 0:T], KVA, ACT.Square).then_inc(act_done, st.one("act", "sq"))
            act.wait_ge(dve_done, st.v("dve", "eps"))
            act.activation(row[:, 1, :], row[:, 0, :], ACT.Sqrt).then_inc(act_done, st.one("act", "root"))
            act.drain().then_inc(act_done, 1)

        def rms1_dve(dve, link, n, l):
            st = enter(dve, n)
            dve.wait_ge(pe_done, st.v("pe", "sums"))
            dve.tensor_scalar(row[:, 0, 0:T], ps[:, 0, 0:T], 1.0 / Q_LORA, RMS_EPS, ALU.mult, ALU.add)
            dve.tensor_scalar(row[:, 0, T:N2], ps[:, 1, 0:T], 1.0 / KV_LORA, RMS_EPS, ALU.mult, ALU.add)\
               .then_inc(dve_done, st.one("dve", "eps"))
            dve.wait_ge(act_done, st.v("act", "root"))
            link(dve.reciprocal(row[:, 0, :], row[:, 1, :]))
            for k in range(QC):
                dve.scalar_tensor_tensor(QA[:, k, :], QA[:, k, :], col(f"qg{l}", k), row[:, 0, 0:T], ALU.mult, ALU.mult)
            for k in range(KVC):
                dve.scalar_tensor_tensor(KVA[:, k, :], KVA[:, k, :], col(f"kvg{l}", k), row[:, 0, T:N2], ALU.mult, ALU.mult)
            dve.drain().then_inc(dve_done, 1)

        def up1_pe(pe, n):
            st = enter(pe, n)
            for c in range(6):
                wt = unit_here(pe, st.u0 + c // 3)
                o = (c % 3) * QC * P
                dot(pe, ps[:, c, 0:T], [(wt[:, o + k * P:o + (k + 1) * P], QA[:, k, :]) for k in range(QC)])\
                    .then_inc(pe_done, st.one("pe", f"c{c}"))
            wt = unit_here(pe, st.u0 + 2)
            for c in range(6, 10):
                if c >= 8:
                    pe.wait_ge(act_done, st.v("act", f"c{c - 8}"))
                o = (c - 6) * KVC * P
                dot(pe, ps[:, c % 8, 0:T], [(wt[:, o + k * P:o + (k + 1) * P], KVA[:, k, :]) for k in range(KVC)])\
                    .then_inc(pe_done, st.one("pe", f"c{c}"))
            pe.wait_ge(act_done, st.v("act", "c3"))
            for t in range(TT):
                ins = dot(pe, ps[:, 2 + t, :], [(KVA[:, k, t * P:(t + 1) * P], wt[:, 1024 + k * 512:1024 + (k + 1) * 512])
                                                for k in range(KVC)])
            ins.then_inc(pe_done, st.one("pe", "rows"))
            pe.drain().then_inc(pe_done, 1)

        def up1_act(act, n):
            st = enter(act, n)
            for c in range(6):
                copy_marked(act, st, c, [(QN[:, c, :] if c < 4 else QR[:, c - 4, :], ps[:, c, 0:T])], f"c{c}")
            for c in range(4):
                b = (c + 6) % 8
                copy_marked(act, st, b, [(KNz[64 * e:64 * e + 64, c, e, :], ps[64 * e:64 * e + 64, b, 0:T]) for e in range(2)], f"c{c + 6}")
            act.wait_ge(pe_done, st.v("pe", "rows"))
            for t in range(TT):
                v4 = ps[:, 2 + t, :].rearrange("p (h e d) -> p h e d", h=H // 2, e=2)
                z4 = Vz[:, t, :, :].rearrange("p (h e) d -> p h e d", e=2)
                for e in range(2):
                    ins = act.activation(z4[:, :, e, e * VD:(e + 1) * VD], v4[:, :, e, :], ACT.Copy)
            ins.then_inc(act_done, st.one("act", "rows"))
            act.drain().then_inc(act_done, 1)

        def rope1_pe(pe, n):
            st = enter(pe, n)
            for c, src in enumerate((QR[:, 0, :], QR[:, 1, :], KR)):
                ins = pe.matmul(ps[:, c, 0:T], con("perm32"), src, start=True, stop=True)
            ins.then_inc(pe_done, st.one("pe", "swapped"))
            pe.drain().then_inc(pe_done, 1)

        def rope1_dve(dve, link, n):
            st = enter(dve, n)
            dve.wait_ge(pe_done, st.v("pe", "swapped"))
            dve.tensor_tensor(QR, QR, outer(con("cos32"), 2), ALU.mult)
            dve.tensor_tensor(KR, KR, con("cos32"), ALU.mult)
            link(dve.tensor_tensor(HM[:, 0:3, 0:T], ps[:, 0:3, 0:T], outer(con("sin32"), 3), ALU.mult))
            dve.tensor_tensor(QR, QR, HM[:, 0:2, 0:T], ALU.add)
            for j in range(4):
                r = slice(32 * j, 32 * j + 32)
                dve.tensor_tensor(KRz[r, j, :], KR[r, :], HM[r, 2, 0:T], ALU.add)
            dve.drain().then_inc(dve_done, 1)

        def index_pe(pe, n, t):
            st = enter(pe, n)
            for h in range(H):
                ins = pe.matmul(ps[:, h // 2, (h % 2) * T:(h % 2 + 1) * T], IQ[:, h // 4, t * P:(t + 1) * P], IKz[:, h % 4, :],
                                start=True, stop=True)
            ins.then_inc(pe_done, st.one("pe", "scores"))
            pe.drain().then_inc(pe_done, 1)

        def index_act(act, n):
            st = enter(act, n)
            act.wait_ge(pe_done, st.v("pe", "scores"))
            act.activation(S1, ps[:, 0:4, :].rearrange("p a b -> p (a b)"), ACT.Relu, scale=IDX_DIM ** -0.5)\
               .then_inc(act_done, st.one("act", "relu"))
            act.drain().then_inc(act_done, 1)

        def index_dve(dve, link, n, t):
            st = enter(dve, n)
            rel = S1.rearrange("p (h k) -> p h k", h=H)
            score, left = SC[:, 0, :], SC[:, 1, :]
            dve.wait_ge(act_done, st.v("act", "relu"))
            link(dve.tensor_scalar(score, rel[:, 0, :], IW[:, t, 0:1], None, ALU.mult))
            for h in range(1, H):
                link(dve.scalar_tensor_tensor(score, rel[:, h, :], IW[:, t, h:h + 1], score, ALU.mult, ALU.add))
            link(dve.tensor_tensor(left, score, con("causal", t * T, T), ALU.add))
            for r in range(KEEP // 8):
                link(dve.max(top8, left))
                link(dve.match_replace(left, top8, left, TAKEN))
            link(dve.tensor_scalar(score, left, TAKEN, None, ALU.is_equal))
            link(dve.tensor_scalar(score, score, 1.0, -NEG, ALU.subtract, ALU.mult))
            link(dve.tensor_tensor(score, score, con("causal", t * T, T), ALU.add))
            for h in range(H):
                dve.scalar_tensor_tensor(SB[:, h, :], con("dist", t * T, T), -SLOPES[h], score, ALU.mult, ALU.add)
            dve.drain().then_inc(dve_done, 1)

        def tile(t):
            return slice(t * P, (t + 1) * P)

        def mla_scores(t):
            return [[(QN[:, h // 2, tile(t)], KNz[:, h // 2, h % 2, :]), (QR[:, h // 4, tile(t)], KRz[:, h % 4, :])] for h in range(H)]

        def dsa_scores(t):
            return [[(DQ[:, h // 2, tile(t)], DKz[:, h % 2, :])] for h in range(H)]

        def pair_mix(value):
            return [[(value(h, s_), h * TT + s_) for h in (2 * p_, 2 * p_ + 1) for s_ in range(TT)] for p_ in range(4)]

        def router_pe(pe, n):
            st = enter(pe, n)
            rw = cols[:, COLS["rw"][0]:COLS["rw"][0] + DC * E_N].rearrange("p (k e) -> p k e", k=DC)
            for t in range(TT):
                ins = dot(pe, ps[:, t, 0:E_N], [(X[:, k, tile(t)], rw[:, k, :]) for k in range(DC)])
            ins.then_inc(pe_done, st.one("pe", "logits"))
            pe.wait_ge(dve_done, st.v("dve", "gates"))
            for t in range(TT):
                ins = pe.transpose(ps[:, 2, tile(t)], G128[:, t, :], ident)
            ins.then_inc(pe_done, st.one("pe", "turned"))
            pe.wait_ge(act_done, st.v("act", "turned"))
            for r in range(2):
                if r:
                    pe.wait_ge(act_done, st.v("act", "spread0"))
                for e in range(8):
                    ins = pe.matmul(ps[:, e, 0:T], selE[:, 8 * r + e, :], gT, start=True, stop=True)
                ins.then_inc(pe_done, st.one("pe", f"spread{r}"))
            pe.drain().then_inc(pe_done, 1)

        def router_act(act, n):
            st = enter(act, n)
            act.wait_ge(pe_done, st.v("pe", "logits"))
            act.activation(R[:, 0, :].rearrange("p (t e) -> p t e", t=TT), ps[:, 0:TT, 0:E_N], ACT.Exp, scale=-1.0)\
               .then_inc(act_done, st.one("act", "exp"))
            act.wait_ge(pe_done, st.v("pe", "turned"))
            act.activation(gT, ps[:, 2, 0:T], ACT.Copy).then_inc(act_done, st.one("act", "turned"))
            for r in range(2):
                act.wait_ge(pe_done, st.v("pe", f"spread{r}"))
                act.activation(gate_b[:, 8 * r:8 * r + 8, :], ps[:, :, 0:T], ACT.Copy).then_inc(act_done, st.one("act", f"spread{r}"))
            act.drain().then_inc(act_done, 1)

        def router_dve(dve, link, n):
            st = enter(dve, n)
            link(dve.memset(G128, 0.0))
            dve.tensor_copy(selE, inner(con("ident", 0, E_N), P))
            dve.wait_ge(act_done, st.v("act", "exp"))
            flat = lambda i: R[:, i, :]
            te = lambda i: R[:, i, :].rearrange("p (t e) -> p t e", t=TT)
            ge = lambda i: R[:, i, :].rearrange("p (g e) -> p g e", e=4)
            tg = lambda i: R[:, i, 0:8].rearrange("p (t g) -> p t g", t=TT)
            link(dve.tensor_scalar(flat(0), flat(0), 1.0, None, ALU.add))
            link(dve.reciprocal(flat(1), flat(0)))
            link(dve.tensor_tensor(te(2), te(1), outer(col("rbias", 0, E_N), TT), ALU.add))
            a, b, c, d = [ge(2)[:, :, i] for i in range(4)]
            m = lambda i: R[:, 3 + i, 0:8]
            dve.tensor_tensor(m(0), a, b, ALU.max)
            dve.tensor_tensor(m(1), a, b, ALU.min)
            dve.tensor_tensor(m(2), c, d, ALU.max)
            link(dve.tensor_tensor(m(3), c, d, ALU.min))
            dve.tensor_tensor(m(4), m(0), m(2), ALU.max)
            dve.tensor_tensor(m(5), m(0), m(2), ALU.min)
            link(dve.tensor_tensor(m(6), m(1), m(3), ALU.max))
            link(dve.tensor_tensor(m(5), m(5), m(6), ALU.max))
            link(dve.tensor_tensor(m(0), m(4), m(5), ALU.add))
            best = R[:, 10, 0:TT]

            def first_best(values, weights, onehot, n_):
                link(dve.tensor_reduce(best, values, AXX, ALU.max))
                link(dve.tensor_tensor(onehot, values, inner(best, n_), ALU.is_equal))
                link(dve.tensor_tensor(onehot, onehot, outer(weights, TT), ALU.mult))
                link(dve.tensor_reduce(best, onehot, AXX, ALU.max))
                link(dve.tensor_tensor(onehot, onehot, inner(best, n_), ALU.is_equal))

            first_best(tg(3), con("first4"), tg(4), 4)
            ing = R[:, 4, 0:8]
            link(dve.tensor_scalar(R[:, 5, 0:8], ing, 1.0, -NEG, ALU.subtract, ALU.mult))
            link(dve.tensor_tensor(ge(2), ge(2), inner(ing, 4), ALU.mult))
            link(dve.tensor_tensor(ge(2), ge(2), inner(R[:, 5, 0:8], 4), ALU.add))
            first_best(te(2), con("first16"), te(6), E_N)
            link(dve.scalar_tensor_tensor(flat(2), flat(6), NEG, flat(2), ALU.mult, ALU.add))
            first_best(te(2), con("first16"), te(7), E_N)
            link(dve.tensor_tensor(flat(6), flat(6), flat(7), ALU.add))
            link(dve.tensor_tensor(flat(6), flat(6), flat(1), ALU.mult))
            link(dve.tensor_reduce(best, te(6), AXX, ALU.add))
            link(dve.reciprocal(R[:, 11, 0:TT], best))
            dve.tensor_tensor(G128[:, :, 0:E_N], te(6), inner(R[:, 11, 0:TT], E_N), ALU.mult)\
               .then_inc(dve_done, st.one("dve", "gates"))
            dve.drain().then_inc(dve_done, 1)

        def ada_pe(pe, n):
            st = enter(pe, n)

            def half_mod(hm, i, free):
                if free is not None:
                    pe.wait_ge(dve_done, free)
                for j in (2 * hm, 2 * hm + 1):
                    wt = unit_here(pe, st.u0 + j, i)
                    for e in range(2):
                        c = 2 * (j % 2) + e
                        ins = dot(pe, ps[:, hm % 2, 2 * c:2 * c + 2],
                                  [(wt[:, e * D + k * P:e * D + (k + 1) * P], condT[:, k, :]) for k in range(DC)])
                    ins.then_inc(pe_done, 1)

            half_mod(0, None, None)
            half_mod(1, None, None)
            with pe.Fori(0, N_MOD - 1) as i:
                for hm in range(2):
                    half_mod(2 + hm, i, st.v("dve", hm + 1) + 2 * i)
            pe.drain().then_inc(pe_done, 1)

        def ada_dve(dve, link, n, l):
            st = enter(dve, n)
            a = COLS[f"adab{l}"][0]
            bias = cols[:, a:a + N_MOD * DC].rearrange("p (m k) -> p m k", m=N_MOD)
            with dve.Fori(0, N_MOD) as i:
                for hm in range(2):
                    dve.wait_ge(pe_done, st.v("pe", 2 * hm + 2) + 4 * i)
                    dve.tensor_tensor(MD[:, i, 4 * hm:4 * hm + 4, :], ps[:, hm, 0:8].rearrange("p (c b) -> p c b", b=2),
                                      inner(bias[:, i, 4 * hm:4 * hm + 4], 2), ALU.add).then_inc(dve_done, 1)
            dve.wait_ge(dve_done, st.v("dve", 2 * N_MOD))
            for m in (1, 4, 7):
                dve.tensor_scalar(MD[:, m, :, :], MD[:, m, :, :], 1.0, None, ALU.add)
            for m in (2, 8):
                dve.tensor_scalar(MD[:, m, :, :], MD[:, m, :, :], 0.5, None, ALU.mult)
            dve.drain().then_inc(dve_done, 1)

        def in2_pe(pe, n):
            st = enter(pe, n)
            for c in range(20):
                wt = unit_here(pe, st.u0 + c // 2)
                if c >= 8:
                    pe.wait_ge(act_done, st.v("act", f"c{c - 8}"))
                o = (c % 2) * D
                dot(pe, ps[:, c % 8, :], [(wt[:, o + k * P:o + (k + 1) * P], HM[:, k, :]) for k in range(DC)])\
                    .then_inc(pe_done, st.one("pe", f"c{c}"))
            wt = unit_here(pe, st.u0 + 10)
            pe.wait_ge(act_done, st.v("act", "c15"))
            for t in range(4):
                ins = dot(pe, ps[:, 4, t * 16:t * 16 + 16], [(HM[:, k, tile(t)], wt[:, k * 16:k * 16 + 16]) for k in range(DC)])
            ins.then_inc(pe_done, st.one("pe", "ab"))
            pe.wait_ge(act_done, st.v("act", "c19"))
            for u in range(2):
                wt = unit_here(pe, st.u0 + 11 + u)
                for t in range(4):
                    for k in range(4):
                        ins = pe.matmul(ps[:, t, :], HM[:, 4 * u + k, tile(t)], wt[:, k * 512:(k + 1) * 512],
                                        start=(u == 0 and k == 0), stop=(u == 1 and k == 3))
            ins.then_inc(pe_done, st.one("pe", "z"))
            pe.drain().then_inc(pe_done, 1)

        def seqs(ap):
            return ap.rearrange("p (s t) -> p s t", s=2)

        def in2_act(act, n):
            st = enter(act, n)
            for c in range(12):
                copy_marked(act, st, c % 8, [(CI[:, c, :, 2:2 + T], seqs(ps[:, c % 8, :]))], f"c{c}")
            for i in range(CCH):
                c = 12 + 2 * i
                copy_marked(act, st, c % 8, [(VAL[:, i, :], ps[:, c % 8, :])], f"c{c}")
                act.wait_ge(pe_done, st.v("pe", f"c{c + 1}"))
                if i:
                    act.wait_ge(dve_done, st.v("dve", f"g{i - 1}"))
                act.activation(SGt, ps[:, (c + 1) % 8, :], ACT.Sigmoid).then_inc(act_done, st.one("act", f"c{c + 1}"))
            copy_marked(act, st, 4, [(AB.rearrange("p a b -> p (a b)"), ps[:, 4, 0:64])], "ab")
            act.wait_ge(pe_done, st.v("pe", "z"))
            act.activation(Zr, ps[:, 0:4, :], ACT.Silu).then_inc(act_done, st.one("act", "z"))
            act.drain().then_inc(act_done, 1)

        def in2_dve(dve, n):
            st = enter(dve, n)
            hc, hl = GCONV // 2, CCONV // 2
            dve.memset(CI[:, :, :, 0:hc].rearrange("p a b c -> p (a b) c"), 0.0)
            dve.memset(CI[:, :, :, hc + T:].rearrange("p a b c -> p (a b) c"), 0.0)
            dve.memset(GL[:, :, :, 0:hl].rearrange("p a b c -> p (a b) c"), 0.0)
            dve.memset(GL[:, :, :, hl + T:].rearrange("p a b c -> p (a b) c"), 0.0)
            for i in range(CCH):
                dve.wait_ge(act_done, st.v("act", f"c{13 + 2 * i}"))
                dve.tensor_tensor(GL[:, i, :, hl:hl + T], seqs(VAL[:, i, :]), seqs(SGt), ALU.mult)\
                   .then_inc(dve_done, st.one("dve", f"g{i}"))
            dve.drain().then_inc(dve_done, 1)

        def conv_dve(dve, link, n):
            st = enter(dve, n)
            for c in range(12):
                o = seqs(QKV[:, c, :])
                link(dve.tensor_scalar(o, CI[:, c, :, 0:T], col("gconv", c * GCONV), None, ALU.mult))
                for k in range(1, GCONV):
                    ins = dve.scalar_tensor_tensor(o, CI[:, c, :, k:k + T], col("gconv", c * GCONV + k), o, ALU.mult, ALU.add)
                    if k < GCONV - 1:
                        link(ins)
                ins.then_inc(dve_done, st.one("dve", f"c{c}"))
            for c in range(CCH):
                o = seqs(CF[:, c, :])
                link(dve.tensor_scalar(o, GL[:, c, :, 0:T], col("cconv", c * CCONV), col("cbias", c), ALU.mult, ALU.add))
                for k in range(1, CCONV):
                    ins = dve.scalar_tensor_tensor(o, GL[:, c, :, k:k + T], col("cconv", c * CCONV + k), o, ALU.mult, ALU.add)
                    if k < CCONV - 1:
                        link(ins)
                if c < CCH - 1:
                    link(ins)
            ins.then_inc(dve_done, st.one("dve", "y"))
            dve.wait_ge(pe_done, st.v("pe", "mean"))
            dve.wait_ge(act_done, st.v("act", "ln"))
            dve.tensor_tensor(CF, CF, outer(row[:, 0, :], CCH), ALU.subtract).then_inc(dve_done, st.one("dve", "centred"))
            dve.wait_ge(pe_done, st.v("pe", "var"))
            dve.tensor_scalar(row[:, 0, :], ps[:, 1, :], 1.0 / (CCH * P), LN_EPS, ALU.mult, ALU.add)\
               .then_inc(dve_done, st.one("dve", "eps"))
            dve.wait_ge(act_done, st.v("act", "root"))
            link(dve.reciprocal(row[:, 0, :], row[:, 1, :]))
            dve.tensor_tensor(CF, CF, outer(row[:, 0, :], CCH), ALU.mult).then_inc(dve_done, st.one("dve", "normed"))
            dve.drain().then_inc(dve_done, 1)

        def conv_act(act, n):
            st = enter(act, n)
            for c in range(12):
                act.wait_ge(dve_done, st.v("dve", f"c{c}"))
                act.activation(QKV[:, c, :], QKV[:, c, :], ACT.Silu).then_inc(act_done, st.one("act", f"silu{c}"))
            act.wait_ge(pe_done, st.v("pe", "mean"))
            act.activation(row[:, 0, :], ps[:, 0, :], ACT.Copy, scale=1.0 / (CCH * P)).then_inc(act_done, st.one("act", "ln"))
            act.wait_ge(dve_done, st.v("dve", "centred"))
            act.activation(Y[:, 0:CCH, :], CF, ACT.Square).then_inc(act_done, st.one("act", "sq"))
            act.wait_ge(dve_done, st.v("dve", "eps"))
            act.activation(row[:, 1, :], row[:, 0, :], ACT.Sqrt).then_inc(act_done, st.one("act", "root"))
            act.wait_ge(dve_done, st.v("dve", "normed"))
            for c in range(CCH):
                act.activation(CF[:, c, :], CF[:, c, :], ACT.Silu, bias=col("clnb", c), scale=col("clng", c))
            act.drain().then_inc(act_done, 1)

        def conv_pe(pe, n):
            st = enter(pe, n)
            pe.wait_ge(dve_done, st.v("dve", "y"))
            dot(pe, ps[:, 0, :], [(ones, CF[:, c, :]) for c in range(CCH)]).then_inc(pe_done, st.one("pe", "mean"))
            pe.wait_ge(act_done, st.v("act", "sq"))
            dot(pe, ps[:, 1, :], [(ones, Y[:, c, :]) for c in range(CCH)]).then_inc(pe_done, st.one("pe", "var"))
            pe.drain().then_inc(pe_done, 1)

        def l2_pe(pe, n):
            st = enter(pe, n)
            pe.wait_ge(act_done, st.v("act", "sq"))
            for c in range(2 * GH):
                ins = pe.matmul(ps[:, c, :], ones, HM[:, c, :], start=True, stop=True)
            ins.then_inc(pe_done, st.one("pe", "sums"))
            pe.drain().then_inc(pe_done, 1)

        def l2_act(act, n):
            st = enter(act, n)
            act.activation(HM[:], QKV[:, 0:8, :], ACT.Square).then_inc(act_done, st.one("act", "sq"))
            act.wait_ge(dve_done, st.v("dve", "eps"))
            act.activation(HM[:], HM[:], ACT.Sqrt).then_inc(act_done, st.one("act", "root"))
            act.drain().then_inc(act_done, 1)

        def l2_dve(dve, link, n):
            st = enter(dve, n)
            dve.wait_ge(pe_done, st.v("pe", "sums"))
            dve.tensor_scalar(HM[:], ps[:], RMS_EPS, None, ALU.add).then_inc(dve_done, st.one("dve", "eps"))
            dve.wait_ge(act_done, st.v("act", "root"))
            link(dve.reciprocal(Y[:], HM[:]))
            link(dve.tensor_scalar(Y[:, 0:GH, :], Y[:, 0:GH, :], GD ** -0.5, None, ALU.mult))
            dve.tensor_tensor(QKV[:, 0:8, :], QKV[:, 0:8, :], Y[:], ALU.mult)
            dve.drain().then_inc(dve_done, 1)

        def rows_pe(pe, n):
            st = enter(pe, n)
            for t in range(4):
                for i, kind in enumerate("kv"):
                    b = 2 * t + i
                    for h in range(GH):
                        ins = pe.transpose(ps[:, b, h * P:(h + 1) * P], QKV[:, GH * (1 + i) + h, tile(t)], ident)
                    ins.then_inc(pe_done, st.one("pe", f"{kind}{t}"))
            pe.drain().then_inc(pe_done, 1)

        def rows_act(act, link, n):
            st = enter(act, n)
            act.activation(gp[:, 0, 32:40], col("alog", 0, 8), ACT.Exp)
            act.activation(AB[:, :, 8:16], AB[:, :, 8:16], ACT.Exp, scale=-1.0)
            act.wait_ge(dve_done, st.v("dve", "dt"))
            act.activation(gp[:, :, 16:24], gp[:, :, 8:16], ACT.Exp).then_inc(act_done, st.one("act", "exp"))
            for t in range(4):
                for i, kind in enumerate("kv"):
                    act.wait_ge(pe_done, st.v("pe", f"{kind}{t}"))
                    dst = (rowK, rowV)[i]
                    act.activation(dst[:, t, :, :].rearrange("p a b -> p (a b)"), ps[:, 2 * t + i, :], ACT.Copy)\
                       .then_inc(act_done, st.one("act", f"{kind}{t}"))
            act.drain().then_inc(act_done, 1)

        def rows_dve(dve, link, n):
            st = enter(dve, n)
            x, neg, e, m = [gp[:, :, 8 * i:8 * i + 8] for i in range(4)]
            link(dve.tensor_tensor(x, AB[:, :, 0:8], outer(col("dtb", 0, 8), 4), ALU.add))
            dve.scalar_tensor_tensor(neg, x, -1.0, x, ALU.mult, ALU.min).then_inc(dve_done, st.one("dve", "dt"))
            dve.tensor_scalar(m, x, 0.0, None, ALU.max)
            dve.memset(St, 0.0)
            dve.wait_ge(act_done, st.v("act", "exp"))
            link(dve.tensor_scalar(neg, e, 2.0, None, ALU.add))
            link(dve.reciprocal(neg, neg))
            link(dve.tensor_tensor(e, e, neg, ALU.mult))
            link(dve.tensor_tensor(x, e, e, ALU.mult))
            link(dve.tensor_scalar(neg, x, 2.0 / (2 * ATANH_TERMS + 1), None, ALU.mult))
            for i in range(ATANH_TERMS - 1, 0, -1):
                link(dve.scalar_tensor_tensor(neg, neg, 2.0 / (2 * i + 1), x, ALU.add, ALU.mult))
            link(dve.scalar_tensor_tensor(e, neg, 2.0, e, ALU.add, ALU.mult))
            link(dve.tensor_scalar(AB[:, :, 8:16], AB[:, :, 8:16], 1.0, None, ALU.add))
            dve.reciprocal(Bb, AB[:, :, 8:16])
            link(dve.tensor_tensor(Gg, m, e, ALU.add))
            dve.scalar_tensor_tensor(Gg, Gg, -1.0, outer(gp[:, 0, 32:40], 4), ALU.mult, ALU.mult)
            dve.drain().then_inc(dve_done, 1)

        ORDER = ((2, 3, 0, 1), (3, 2, 1, 0))

        def fl(ap):
            return ap.rearrange("p h k -> p (h k)")

        def scan_pe(pe, n, step):
            st = enter(pe, n)
            for d in range(2):
                t, b, m = ORDER[d][step], 4 * d, DN[d]
                tri = con(f"tri{d}")
                pe.wait_ge(dve_done, st.v("dve", f"inp.{d}"))
                for h in range(GH):
                    c = slice(h * P, (h + 1) * P)
                    kT = QKV[:, GH + h, tile(t)]
                    pe.matmul(ps[:, b, c], m["gB"][:, h, :], tri, start=True, stop=True)
                    pe.matmul(ps[:, b + 1, c], m["bB"][:, h, :], ident, start=True, stop=True)
                    ins = pe.matmul(ps[:, b + 3, c], kT, kT, start=True, stop=True)
                ins.then_inc(pe_done, st.one("pe", f"A.{d}"))
            for d in range(2):
                t, b = ORDER[d][step], 4 * d
                pe.wait_ge(dve_done, st.v("dve", f"mt.{d}"))
                for h in range(GH):
                    c = slice(h * P, (h + 1) * P)
                    qT, kT, S_h = QKV[:, h, tile(t)], QKV[:, GH + h, tile(t)], St[:, d, c]
                    pe.matmul(ps[:, b, c], kT, qT, start=True, stop=True)
                    pe.matmul(ps[:, b + 1, c], kT, S_h, start=True, stop=True)
                    ins = pe.matmul(ps[:, b + 2, c], qT, S_h, start=True, stop=True)
                ins.then_inc(pe_done, st.one("pe", f"B.{d}"))
            for j in range(LEVELS):
                for d in range(2):
                    b, m = 4 * d, DN[d]
                    pe.wait_ge(dve_done, st.v("dve", f"X{j - 1}.{d}" if j else f"mt.{d}"))
                    for h in range(GH):
                        ins = pe.matmul(ps[:, b + 3, h * P:(h + 1) * P], m[f"ET{j % 2}"][:, h, :], m["Xi"][:, h, :],
                                        start=True, stop=True)
                    ins.then_inc(pe_done, st.one("pe", f"Y{j}.{d}"))
                for d in range(2):
                    b, m = 4 * d, DN[d]
                    pe.wait_ge(act_done, st.v("act", f"Y{j}.{d}"))
                    if j == 0:
                        pe.wait_ge(dve_done, st.v("dve", f"at.{d}"))
                    for h in range(GH):
                        c = slice(h * P, (h + 1) * P)
                        if j < LEVELS - 1:
                            pe.matmul(ps[:, b, c], m["XT"][:, h, :], m["Yv"][:, h, :], start=True, stop=True)
                        ins = pe.matmul(ps[:, b + 1, c], m["Yv"][:, h, :], m["XT"][:, h, :], start=True, stop=True)
                    ins.then_inc(pe_done, st.one("pe", f"Z{j}.{d}"))
            for d in range(2):
                m = DN[d]
                pe.wait_ge(dve_done, st.v("dve", f"X{LEVELS - 1}.{d}"))
                for h in range(GH):
                    ins = pe.matmul(ps[:, 4 * d + 3, h * P:(h + 1) * P], m["XT"][:, h, :], m["R"][:, h, :], start=True, stop=True)
                ins.then_inc(pe_done, st.one("pe", f"V.{d}"))
            for d in range(2):
                b, m = 4 * d, DN[d]
                pe.wait_ge(act_done, st.v("act", f"vn.{d}"))
                for h in range(GH):
                    c = slice(h * P, (h + 1) * P)
                    pe.matmul(ps[:, b, c], m["AT"][:, h, :], m["bB"][:, h, :], start=True, stop=True)
                    ins = pe.matmul(ps[:, b + 1, c], m["gB"][:, h, :], m["bB"][:, h, :], start=True, stop=True)
                ins.then_inc(pe_done, st.one("pe", f"O.{d}"))
            pe.drain().then_inc(pe_done, 1)

        def scan_act(act, link, n):
            st = enter(act, n)
            for d in range(2):
                m = DN[d]
                act.wait_ge(dve_done, st.v("dve", f"dec.{d}"))
                act.activation(m["sm"][:, 12:24], m["sm"][:, 0:12], ACT.Exp)
                act.activation(fl(m["DEC"]), fl(m["DEC"]), ACT.Exp).then_inc(act_done, st.one("act", f"exp.{d}"))
            for d in range(2):
                m = DN[d]
                act.wait_ge(act_done, st.v("act", f"exp.{d}"))
                act.wait_ge(pe_done, st.v("pe", f"B.{d}"))
                for h in range(GH):
                    ins = act.activation(m["QS"][:, h, :], ps[:, 4 * d + 2, h * P:(h + 1) * P], ACT.Copy,
                                         scale=m["sm"][:, 12 + h:13 + h])
                ins.then_inc(act_done, st.one("act", f"qs.{d}"))
            for j in range(LEVELS):
                for d in range(2):
                    act.wait_ge(pe_done, st.v("pe", f"Y{j}.{d}"))
                    act.activation(fl(DN[d]["Yv"]), ps[:, 4 * d + 3, :], ACT.Copy).then_inc(act_done, st.one("act", f"Y{j}.{d}"))
            for d in range(2):
                act.wait_ge(pe_done, st.v("pe", f"V.{d}"))
                act.activation(fl(DN[d]["bB"]), ps[:, 4 * d + 3, :], ACT.Copy).then_inc(act_done, st.one("act", f"vn.{d}"))
            act.drain().then_inc(act_done, 1)

        def scan_dve(dve, link, n, step):
            st = enter(dve, n)
            for d in range(2):
                t, m = ORDER[d][step], DN[d]
                dve.tensor_copy(m["bB"], inner(Bb[:, t, GH * d:GH * d + GH], P))
                dve.tensor_copy(m["gB"], inner(Gg[:, t, GH * d:GH * d + GH], P)).then_inc(dve_done, st.one("dve", f"inp.{d}"))
            for d in range(2):
                t, b, m = ORDER[d][step], 4 * d, DN[d]
                sm = m["sm"]
                dve.wait_ge(pe_done, st.v("pe", f"A.{d}"))
                GC = ps[:, b, :].rearrange("p (h i) -> p h i", h=GH)
                link(dve.tensor_tensor(m["DEC"], GC, outer(ident, GH), ALU.mult))
                link(dve.tensor_reduce(sm[:, 0:4], m["DEC"], AXX, ALU.add))
                link(dve.tensor_copy(sm[:, 4:8], GC[:, :, (P - 1, 0)[d]]))
                dve.tensor_tensor(sm[:, 8:12], sm[:, 4:8], sm[:, 0:4], ALU.subtract)
                for h in range(GH):
                    ins = dve.tensor_scalar(m["DEC"][:, h, :], ps[:, b, h * P:(h + 1) * P], sm[:, h:h + 1], 0.0,
                                            ALU.subtract, ALU.min)
                ins.then_inc(dve_done, st.one("dve", f"dec.{d}"))
            for d in range(2):
                b, m = 4 * d, DN[d]
                dve.tensor_copy(m["Xi"], outer(ident, GH))
                dve.tensor_copy(m["XT"], outer(ident, GH))
                dve.wait_ge(act_done, st.v("act", f"exp.{d}"))
                link(dve.tensor_tensor(fl(m["MT"]), fl(m["DEC"]), ps[:, b + 3, :], ALU.mult))
                link(dve.tensor_tensor(fl(m["MT"]), fl(m["MT"]), ps[:, b + 1, :], ALU.mult))
                dve.tensor_tensor(m["ET0"], m["MT"], outer(con(f"lvl{d}", 0, P), GH), ALU.mult)\
                   .then_inc(dve_done, st.one("dve", f"mt.{d}"))
            for d in range(2):
                t, b, m = ORDER[d][step], 4 * d, DN[d]
                sm = m["sm"]
                link(dve.scalar_tensor_tensor(sm[:, 24:28], sm[:, 12:16], -1.0, Bb[:, t, GH * d:GH * d + GH], ALU.mult, ALU.mult))
                for h in range(GH):
                    dve.tensor_scalar(m["VB"][:, h, :], rowV[:, t, h, :], Bb[:, t, GH * d + h:GH * d + h + 1], None, ALU.mult)
                    ins = dve.tensor_scalar(m["gB"][:, h, :], rowK[:, t, h, :], sm[:, 20 + h:21 + h], None, ALU.mult)
                link(ins)
                dve.wait_ge(pe_done, st.v("pe", f"B.{d}"))
                link(dve.tensor_tensor(fl(m["AT"]), fl(m["DEC"]), ps[:, b, :], ALU.mult))
                dve.tensor_tensor(m["AT"], m["AT"], outer(con(f"tri{d}"), GH), ALU.mult)
                for h in range(GH):
                    ins = dve.scalar_tensor_tensor(m["R"][:, h, :], ps[:, b + 1, h * P:(h + 1) * P], sm[:, 24 + h:25 + h],
                                                   m["VB"][:, h, :], ALU.mult, ALU.add)
                ins.then_inc(dve_done, st.one("dve", f"at.{d}"))
            for j in range(LEVELS):
                for d in range(2):
                    b, m = 4 * d, DN[d]
                    if j < LEVELS - 1:
                        dve.tensor_tensor(m[f"ET{(j + 1) % 2}"], m["MT"], outer(con(f"lvl{d}", (j + 1) * P, P), GH), ALU.mult)
                    dve.wait_ge(pe_done, st.v("pe", f"Z{j}.{d}"))
                    if j < LEVELS - 1:
                        dve.tensor_tensor(fl(m["Xi"]), fl(m["Xi"]), ps[:, b, :], ALU.subtract)
                    dve.tensor_tensor(fl(m["XT"]), fl(m["XT"]), ps[:, b + 1, :], ALU.subtract)\
                       .then_inc(dve_done, st.one("dve", f"X{j}.{d}"))
                    dve.wait_ge(dve_done, st.v("dve", f"X{j}.{d}"))
            for d in range(2):
                t, b, m = ORDER[d][step], 4 * d, DN[d]
                dve.wait_ge(pe_done, st.v("pe", f"O.{d}"))
                dve.wait_ge(act_done, st.v("act", f"qs.{d}"))
                o = fl(OR[:, t, :, :])
                if step in (0, 2):
                    dve.tensor_tensor(o, fl(m["QS"]), ps[:, b, :], ALU.add)
                else:
                    link(dve.tensor_tensor(o, o, fl(m["QS"]), ALU.add))
                    dve.tensor_tensor(o, o, ps[:, b, :], ALU.add)
                for h in range(GH):
                    c = slice(h * P, (h + 1) * P)
                    dve.scalar_tensor_tensor(St[:, d, c], St[:, d, c], m["sm"][:, 16 + h:17 + h], ps[:, b + 1, c], ALU.mult, ALU.add)
            dve.drain().then_inc(dve_done, 1)

        def merge_act(act, n):
            st = enter(act, n)
            flat = OR.rearrange("p a b c -> p (a b c)")
            act.activation(Yf[:, 0:2048], flat, ACT.Square).then_inc(act_done, st.one("act", "sq"))
            act.wait_ge(dve_done, st.v("dve", "eps"))
            act.activation(small2[:, 16:32], small2[:, 0:16], ACT.Sqrt).then_inc(act_done, st.one("act", "root"))
            act.wait_ge(pe_done, st.v("pe", "turned"))
            act.activation(HM[:, 0:GH, :].rearrange("p a b -> p (a b)"), ps[:, 0:4, :].rearrange("p a b -> p (a b)"), ACT.Copy)
            act.drain().then_inc(act_done, 1)

        def merge_dve(dve, link, n):
            st = enter(dve, n)
            o3 = OR.rearrange("p a b c -> p (a b) c")
            dve.wait_ge(act_done, st.v("act", "sq"))
            link(dve.tensor_reduce(small2[:, 0:16], Yf[:, 0:2048].rearrange("p (a c) -> p a c", c=P), AXX, ALU.add))
            dve.tensor_scalar(small2[:, 0:16], small2[:, 0:16], 1.0 / GD, RMS_EPS, ALU.mult, ALU.add)\
               .then_inc(dve_done, st.one("dve", "eps"))
            dve.wait_ge(act_done, st.v("act", "root"))
            link(dve.reciprocal(small2[:, 0:16], small2[:, 16:32]))
            link(dve.tensor_tensor(o3, o3, inner(small2[:, 0:16], P), ALU.mult))
            link(dve.tensor_tensor(o3, o3, outer(col("outn", 0, P), 16), ALU.mult))
            dve.tensor_tensor(OR.rearrange("p a b c -> p a (b c)"), OR.rearrange("p a b c -> p a (b c)"), Zr, ALU.mult)\
               .then_inc(dve_done, st.one("dve", "ready"))
            dve.drain().then_inc(dve_done, 1)

        def merge_pe(pe, n):
            st = enter(pe, n)
            pe.wait_ge(dve_done, st.v("dve", "ready"))
            for h in range(GH):
                for t in range(4):
                    ins = pe.transpose(ps[:, h, tile(t)], OR[:, t, h, :], ident)
            ins.then_inc(pe_done, st.one("pe", "turned"))
            pe.drain().then_inc(pe_done, 1)

        def in3_pe(pe, n):
            st = enter(pe, n)
            for c in range(AH + AKV):
                wt = unit_here(pe, st.u0 + c // 2)
                if c >= 8:
                    pe.wait_ge(act_done, st.v("act", f"q{c - 8}"))
                o = (c % 2) * D
                name, m = (f"q{c}", T) if c < AH else (f"k{c - AH}", N2)
                dot(pe, ps[:, c % 8, 0:m], [(wt[:, o + k * P:o + (k + 1) * P], HM[:, k, 0:m]) for k in range(DC)])\
                    .then_inc(pe_done, st.one("pe", name))
            wt = unit_here(pe, st.u0 + 5)
            pe.wait_ge(act_done, st.v("act", "q5"))
            for t in range(4):
                ins = dot(pe, ps[:, 2 + t, 0:AKV * AD], [(HM[:, k, tile(t)], wt[:, k * 256:(k + 1) * 256]) for k in range(DC)])
            ins.then_inc(pe_done, st.one("pe", "v"))
            pe.drain().then_inc(pe_done, 1)

        def in3_act(act, n):
            st = enter(act, n)
            for c in range(AH):
                copy_marked(act, st, c, [(AQ[:, c, :], ps[:, c, 0:T])], f"q{c}")
            for c in range(AKV):
                copy_marked(act, st, c, [(AK[:, c, :], ps[:, c, :])], f"k{c}")
            copy_marked(act, st, 2, [(AV, ps[:, 2:6, 0:AKV * AD])], "v")
            act.drain().then_inc(act_done, 1)

        def rms3_pe(pe, n):
            st = enter(pe, n)
            pe.wait_ge(act_done, st.v("act", "sq"))
            for c in range(AH):
                pe.matmul(ps[:, c // 2, (c % 2) * T:(c % 2 + 1) * T], ones, SQq[:, c, :], start=True, stop=True)
            for c in range(AKV):
                ins = pe.matmul(ps[:, 4 + c, :], ones, SQk[:, c, :], start=True, stop=True)
            ins.then_inc(pe_done, st.one("pe", "sums"))
            pe.drain().then_inc(pe_done, 1)

        sq_all = area[:, AH * T + AKV * N2:2 * (AH * T + AKV * N2)]

        def rms3_act(act, n):
            st = enter(act, n)
            act.activation(sq_all, area[:, 0:AH * T + AKV * N2], ACT.Square).then_inc(act_done, st.one("act", "sq"))
            act.wait_ge(dve_done, st.v("dve", "eps"))
            act.activation(sq_all, sq_all, ACT.Sqrt).then_inc(act_done, st.one("act", "root"))
            act.drain().then_inc(act_done, 1)

        def rms3_dve(dve, link, n):
            st = enter(dve, n)
            dve.wait_ge(pe_done, st.v("pe", "sums"))
            dve.tensor_scalar(sq_all, ps[:, 0:6, :].rearrange("p a b -> p (a b)"), 1.0 / AD, RMS_EPS, ALU.mult, ALU.add)\
               .then_inc(dve_done, st.one("dve", "eps"))
            dve.wait_ge(act_done, st.v("act", "root"))
            link(dve.reciprocal(sq_all, sq_all))
            dve.scalar_tensor_tensor(AQ, AQ, col("qn"), SQq, ALU.mult, ALU.mult)
            dve.scalar_tensor_tensor(AK, AK, col("kn"), SQk, ALU.mult, ALU.mult)
            dve.drain().then_inc(dve_done, 1)

        def rope3_pe(pe, n):
            st = enter(pe, n)
            for c in range(AH):
                pe.matmul(ps[:, c // 2, (c % 2) * T:(c % 2 + 1) * T], con("permA"), AQ[:, c, :], start=True, stop=True)
            for c in range(AKV):
                ins = pe.matmul(ps[:, 4, c * T:(c + 1) * T], con("permA"), AK[:, c, 0:T], start=True, stop=True)
            ins.then_inc(pe_done, st.one("pe", "swapped"))
            pe.drain().then_inc(pe_done, 1)

        def rope3_dve(dve, link, n):
            st = enter(dve, n)
            dve.wait_ge(pe_done, st.v("pe", "swapped"))
            sw = ps[:, 0:5, :].rearrange("p a (b t) -> p (a b) t", b=2)
            prod = sq_all[:, 0:(AH + AKV) * T].rearrange("p (c t) -> p c t", t=T)
            dve.tensor_tensor(AQ, AQ, outer(con("cosA"), AH), ALU.mult)
            dve.tensor_tensor(AK[:, :, 0:T], AK[:, :, 0:T], outer(con("cosA"), AKV), ALU.mult)
            link(dve.tensor_tensor(prod, sw, outer(con("sinA"), AH + AKV), ALU.mult))
            dve.tensor_tensor(AQ, AQ, prod[:, 0:AH, :], ALU.add)
            dve.tensor_tensor(AK[:, :, 0:T], AK[:, :, 0:T], prod[:, AH:AH + AKV, :], ALU.add)
            dve.drain().then_inc(dve_done, 1)

        def gqa_scores(t, g_):
            return [[(AQ[:, 4 * g_ + h, tile(t)], AK[:, g_, :])] for h in range(4)]

        def gqa_mix(g_):
            return [[(AV[:, s_, g_ * AD:(g_ + 1) * AD], h * 4 + s_) for s_ in range(4)] for h in range(4)]

        block = ctx.enter_context(nc.Block())

        @block.sync
        def _(sp):
            sp.dma_start(X[:, :, 0:T], w["x"]).then_inc(tables_in, 16)
            sp.dma_start(X[:, :, T:N2], w["ctx"]).then_inc(tables_in, 16)
            fill_ring(sp)
            sp.wait_ge(dve_done, now["dve"])
            sp.dma_start(out, X[:, :, 0:T]).then_inc(out_done, 16)
            sp.wait_ge(out_done, 16)

        @block.scalar
        def _(act):
            link = Chain(act, act_step)
            act.dma_start(cols[:], w["cols"]).then_inc(tables_in, 16)
            act.dma_start(cons[:], w["cons"]).then_inc(tables_in, 16)
            act.wait_ge(tables_in, 64)
            link(act.activation(condT[:].rearrange("p a b -> p (a b)"), col("cond", 0, 2 * DC), ACT.Silu))
            for l in range(DEPTH):
                n = f"b1.{l}."
                in1_act(act, n + "in")
                rms1_act(act, n + "rms")
                up1_act(act, n + "up")
                idle(act, act_done, n + "rope")
                for t in range(TT):
                    index_act(act, f"{n}index{t}")
                    attention_act(act, f"{n}mla{t}", S1, PT, OT1[:, 0:4, tile(t)])
                    attention_act(act, f"{n}dsa{t}", S1, PT, OT1[:, 4:8, tile(t)])
                idle(act, act_done, n + "out")
                ln_act(act, n + "ln1", T)
                router_act(act, n + "router")
                ffn_up_act(act, n + "moe.up", MOE_CH, T)
                idle(act, act_done, n + "moe.down")
                ln_act(act, n + "ln2", T)
            for l in range(DEPTH):
                n = f"b2.{l}."
                idle(act, act_done, n + "ada")
                idle(act, act_done, n + "mod0")
                ffn_up_act(act, n + "ffn0.up", FF_CH, N2)
                idle(act, act_done, n + "ffn0.down")
                ln_act(act, n + "ln0", N2)
                idle(act, act_done, n + "mod1")
                if l == 0:
                    in2_act(act, n + "in")
                    conv_act(act, n + "conv")
                    l2_act(act, n + "l2")
                    rows_act(act, link, n + "rows")
                    for i in range(4):
                        scan_act(act, link, f"{n}scan{i}")
                    merge_act(act, n + "merge")
                else:
                    in3_act(act, n + "in")
                    rms3_act(act, n + "rms")
                    idle(act, act_done, n + "rope")
                    for t in range(TT):
                        for h in range(AKV):
                            attention_act(act, f"{n}gqa{t}{h}", S2, PT2, OT2[:, 4 * h:4 * h + 4, tile(t)])
                m = N2 if l < DEPTH - 1 else T
                idle(act, act_done, n + "out")
                ln_act(act, n + "ln1", m)
                idle(act, act_done, n + "mod2")
                ffn_up_act(act, n + "ffn1.up", FF_CH, m)
                idle(act, act_done, n + "ffn1.down")
                ln_act(act, n + "ln2", m)

        @block.vector
        def _(dve):
            link = Chain(dve, dve_step)
            dve.wait_ge(tables_in, 64)
            for l in range(DEPTH):
                n = f"b1.{l}."
                in1_dve(dve, n + "in")
                rms1_dve(dve, link, n + "rms", l)
                idle(dve, dve_done, n + "up")
                rope1_dve(dve, link, n + "rope")
                for t in range(TT):
                    index_dve(dve, link, f"{n}index{t}", t)
                    attention_dve(dve, link, f"{n}mla{t}", H, S1, (NOPE + ROPE_D) ** -0.5, outer(con("causal", t * T, T), H))
                    attention_dve(dve, link, f"{n}dsa{t}", H, S1, VD ** -0.5, SB)
                add_residual(dve, link, enter(dve, n + "out"), DC, None, T)
                ln_dve(dve, link, n + "ln1", T, f"ln1g{l}", f"ln1b{l}")
                router_dve(dve, link, n + "router")
                ffn_up_dve(dve, link, n + "moe.up", MOE_CH, T, hid_moe, True)
                ffn_down_dve(dve, link, n + "moe.down", MOE_CH, None, T)
                ln_dve(dve, link, n + "ln2", T, f"ln2g{l}", f"ln2b{l}")
            for l in range(DEPTH):
                n = f"b2.{l}."
                ada_dve(dve, link, n + "ada", l)
                modulate(dve, n + "mod0", 0, 1)
                ffn_up_dve(dve, link, n + "ffn0.up", FF_CH, N2, hid_ff, False)
                ffn_down_dve(dve, link, n + "ffn0.down", FF_CH, 2, N2)
                ln_dve(dve, link, n + "ln0", N2, f"lng0{l}", f"lnb0{l}")
                modulate(dve, n + "mod1", 3, 4)
                if l == 0:
                    in2_dve(dve, n + "in")
                    conv_dve(dve, link, n + "conv")
                    l2_dve(dve, link, n + "l2")
                    rows_dve(dve, link, n + "rows")
                    for i in range(4):
                        scan_dve(dve, link, f"{n}scan{i}", i)
                    merge_dve(dve, link, n + "merge")
                else:
                    idle(dve, dve_done, n + "in")
                    rms3_dve(dve, link, n + "rms")
                    rope3_dve(dve, link, n + "rope")
                    for t in range(TT):
                        for h in range(AKV):
                            attention_dve(dve, link, f"{n}gqa{t}{h}", 4, S2, AD ** -0.5, None)
                m = N2 if l < DEPTH - 1 else T
                add_residual(dve, link, enter(dve, n + "out"), DC, 5, m)
                ln_dve(dve, link, n + "ln1", m, f"lng1{l}", f"lnb1{l}")
                modulate(dve, n + "mod2", 6, 7)
                ffn_up_dve(dve, link, n + "ffn1.up", FF_CH, m, hid_ff, False)
                ffn_down_dve(dve, link, n + "ffn1.down", FF_CH, 8, m)
                ln_dve(dve, link, n + "ln2", m, f"lng2{l}", f"lnb2{l}")

        @block.tensor
        def _(pe):
            pe.wait_ge(tables_in, 64)
            pe.wait_ge(act_step, 1)
            for l in range(DEPTH):
                n = f"b1.{l}."
                in1_pe(pe, n + "in")
                rms1_pe(pe, n + "rms")
                up1_pe(pe, n + "up")
                rope1_pe(pe, n + "rope")
                for t in range(TT):
                    index_pe(pe, f"{n}index{t}", t)
                    attention_pe(pe, f"{n}mla{t}", mla_scores(t), pair_mix(lambda h, s_: Vz[:, s_, h, :]), S1, PT)
                    attention_pe(pe, f"{n}dsa{t}", dsa_scores(t), pair_mix(lambda h, s_: DVz[:, s_, h % 2, :]), S1, PT)
                out_pe(pe, n + "out", lambda k: OT1[:, k, :], T)
                ln_pe(pe, n + "ln1", T)
                router_pe(pe, n + "router")
                ffn_up_pe(pe, n + "moe.up", MOE_CH, T, X)
                ffn_down_pe(pe, n + "moe.down", MOE_CH, T, hid_moe)
                ln_pe(pe, n + "ln2", T)
            for l in range(DEPTH):
                n = f"b2.{l}."
                ada_pe(pe, n + "ada")
                idle(pe, pe_done, n + "mod0")
                ffn_up_pe(pe, n + "ffn0.up", FF_CH, N2, HM)
                ffn_down_pe(pe, n + "ffn0.down", FF_CH, N2, hid_ff)
                ln_pe(pe, n + "ln0", N2)
                idle(pe, pe_done, n + "mod1")
                if l == 0:
                    in2_pe(pe, n + "in")
                    conv_pe(pe, n + "conv")
                    l2_pe(pe, n + "l2")
                    rows_pe(pe, n + "rows")
                    for i in range(4):
                        scan_pe(pe, f"{n}scan{i}", i)
                    merge_pe(pe, n + "merge")
                else:
                    in3_pe(pe, n + "in")
                    rms3_pe(pe, n + "rms")
                    rope3_pe(pe, n + "rope")
                    for t in range(TT):
                        for h in range(AKV):
                            attention_pe(pe, f"{n}gqa{t}{h}", gqa_scores(t, h), gqa_mix(h), S2, PT2)
                m = N2 if l < DEPTH - 1 else T
                src = (lambda k: HM[:, k, :] if k < GH else CF[:, k - GH, :]) if l == 0 else (lambda k: OT2[:, k, :])
                out_pe(pe, n + "out", src, m)
                ln_pe(pe, n + "ln1", m)
                idle(pe, pe_done, n + "mod2")
                ffn_up_pe(pe, n + "ffn1.up", FF_CH, m, HM)
                ffn_down_pe(pe, n + "ffn1.down", FF_CH, m, hid_ff)
                ln_pe(pe, n + "ln2", m)


def constants():
    f = np.float32
    p = np.arange(P)
    rot = np.arange(T, dtype=f)
    c = {"ident": np.eye(P), "ones": np.ones((P, P)), "perm32": np.eye(P)[p ^ 16], "permA": np.eye(P)[p ^ 1]}
    inv = f(10000.0) ** (-np.arange(16, dtype=f) / f(16))
    ang = (rot[None, :] * inv[p % 16][:, None]).astype(f)
    c["cos32"] = np.cos(ang)
    c["sin32"] = np.sin(ang) * np.where(p % 32 < 16, -1, 1)[:, None]
    inv = f(10000.0) ** (-np.arange(32, dtype=f) / f(32))
    rows_, cols_ = (np.arange(T) // 64).astype(f), (np.arange(T) % 64).astype(f)
    ang = np.concatenate([inv[:, None] * rows_, inv[:, None] * cols_]).astype(f)
    c["cosA"] = np.cos(ang)[p // 2]
    c["sinA"] = np.sin(ang)[p // 2] * np.where(p % 2 == 0, -1, 1)[:, None]
    d = (np.arange(TT)[None, :, None] * P + p[:, None, None] - np.arange(T)[None, None, :]).astype(f)
    c["dist"] = d
    c["causal"] = np.where(d >= 0, 0, NEG)
    c["first4"] = np.broadcast_to(4 - np.arange(4), (P, 4))
    c["first16"] = np.broadcast_to(E_N - np.arange(E_N), (P, E_N))
    j, i = p[:, None], p[None, :]
    for d_, late in enumerate((j < i, j > i)):
        c[f"tri{d_}"] = late | (j == i)
        c[f"lvl{d_}"] = np.stack([late & (j // (2 * b) == i // (2 * b)) & (j // b != i // b)
                                  for b in (1, 2, 4, 8, 16, 32, 64)], axis=1)
    out = np.zeros((P, NCONS), f)
    for name, (a, n) in CONS.items():
        out[:, a:a + n] = np.asarray(c[name]).astype(f).reshape(P, n)
    return out


def chunks_of(wt):
    k, n = wt.shape[0] // P, wt.shape[1] // P
    return wt.reshape(k, P, n, P).transpose(2, 1, 0, 3).reshape(n, P, k * P)


def rows_of(wt):
    k, n = wt.shape[0] // P, wt.shape[1]
    return wt.reshape(k, P, n).transpose(1, 0, 2).reshape(P, k * n)


def grouped(ch, m):
    n, _, wd = ch.shape
    return ch.reshape(n // m, m, P, wd).transpose(0, 2, 1, 3).reshape(n // m, P, m * wd)


def column(v):
    return v.reshape(-1, P).T


def spread(v):
    return np.broadcast_to(v.reshape(1, -1), (P, v.size))


def lay_out(a):
    w = {}
    w["x"] = a["x"][0].reshape(T, DC, P).transpose(2, 1, 0)
    w["ctx"] = a["ctx_2"][0].reshape(T, DC, P).transpose(2, 1, 0)
    cut = np.cumsum([Q_LORA, KV_LORA, ROPE_D, H * VD, VD, VD, H * IDX_DIM, IDX_DIM])
    w_in, rows_, qup, ukv, wo, mu, md = [], [], [], [], [], [], []
    for l in range(DEPTH):
        qa, kva, kr, dq, dk, dv, iq, ik, iw = np.split(a["w_in"][l], cut, axis=1)
        w_in.append(grouped(chunks_of(np.concatenate([qa, kva, dq, iq] + [kr] * 4 + [ik] * 4 + [dk] * 2, axis=1)), 2))
        rows_.append(rows_of(np.concatenate([iw, dv], axis=1))[None])
        q = a["w_q_up"][l].reshape(Q_LORA, H, NOPE + ROPE_D)
        q = np.concatenate([q[:, :, :NOPE].reshape(Q_LORA, -1), q[:, :, NOPE:].reshape(Q_LORA, -1)], axis=1)
        qup.append(grouped(chunks_of(q), 3))
        ukv.append(np.concatenate([grouped(chunks_of(a["w_uk"][l]), 4)[0], rows_of(a["w_uv"][l])], axis=1)[None])
        wo.append(grouped(chunks_of(a["w_o"][l]), 2))
        mu.append(np.concatenate([np.concatenate([chunks_of(a["w_gate"][l, e]) for e in range(E_N)]),
                                  np.concatenate([chunks_of(a["w_up"][l, e]) for e in range(E_N)])], axis=2))
        md.append(grouped(a["w_down"][l].reshape(MOE_CH, P, D), 2))
    w.update(w_in=np.stack(w_in), w_in_rows=np.stack(rows_), w_q_up=np.stack(qup), w_ukv=np.stack(ukv), w_o=np.stack(wo),
             moe_up=np.stack(mu), moe_down=np.stack(md))
    w["ada"] = np.stack([grouped(chunks_of(a["ada_w_2"][l]), 2) for l in range(DEPTH)])
    gu, dn = a["ffn_w_gu_2"], a["ffn_w_down_2"]
    w["ff_up"] = np.stack([np.stack([np.concatenate([chunks_of(gu[l, i][:, :DFF]), chunks_of(gu[l, i][:, DFF:])], axis=2)
                                     for i in range(2)]) for l in range(DEPTH)])
    w["ff_down"] = np.stack([np.stack([grouped(dn[l, i].reshape(FF_CH, P, D), 2) for i in range(2)]) for l in range(DEPTH)])
    qkv, z, ab, val, gate = np.split(a["even_w_in_2"][0], [3 * GH * GD, 4 * GH * GD, 4 * GH * GD + 4 * GH,
                                                            4 * GH * GD + 4 * GH + CCH * P], axis=1)
    glu = np.stack([chunks_of(val), chunks_of(gate)], axis=1).reshape(2 * CCH, P, D)
    w["even_in"] = grouped(np.concatenate([chunks_of(qkv), glu]), 2)
    w["even_ab"] = rows_of(ab)[None]
    w["even_z"] = np.stack([rows_of(z[0:D // 2]), rows_of(z[D // 2:])])
    w["even_out"] = grouped(chunks_of(a["even_w_out_2"][0]), 2)
    ai = a["attn_w_in_2"][0]
    w["attn_in"] = grouped(chunks_of(ai[:, :(AH + AKV) * AD]), 2)
    w["attn_v"] = rows_of(ai[:, (AH + AKV) * AD:])[None]
    w["attn_out"] = grouped(chunks_of(a["attn_w_out_2"][0]), 2)
    c = {}
    for l in range(DEPTH):
        c[f"qg{l}"], c[f"kvg{l}"] = column(a["q_norm_g"][l]), column(a["kv_norm_g"][l])
        for i in (1, 2):
            c[f"ln{i}g{l}"], c[f"ln{i}b{l}"] = column(a[f"ln{i}_g"][l]), column(a[f"ln{i}_b"][l])
        c[f"adab{l}"] = column(a["ada_b_2"][l])
        for i in range(3):
            c[f"lng{i}{l}"], c[f"lnb{i}{l}"] = column(a["ln_g_2"][l, i]), column(a["ln_b_2"][l, i])
    c["cond"] = np.stack([column(a["c_2"][0]), column(a["c_ctx_2"])], axis=2).reshape(P, 2 * DC)
    c["gconv"] = a["even_qkv_conv_2"][0].T.reshape(12, P, GCONV).transpose(1, 0, 2).reshape(P, -1)
    c["cconv"] = a["cf_dw_conv_2"][0].T.reshape(CCH, P, CCONV).transpose(1, 0, 2).reshape(P, -1)
    c["cbias"], c["clng"], c["clnb"] = [column(a[k][0]) for k in ("cf_dw_bias_2", "cf_ln_g_2", "cf_ln_b_2")]
    c["qn"], c["kn"] = column(a["attn_q_norm_2"][0]), column(a["attn_k_norm_2"][0])
    c["rbias"], c["alog"], c["dtb"] = spread(a["router_bias"]), spread(a["gdn_a_log_2"][0]), spread(a["gdn_dt_bias_2"][0])
    c["outn"], c["rw"] = spread(a["gdn_out_norm_2"][0]), rows_of(a["router_w"])
    w["cols"] = np.zeros((P, NCOLS), np.float32)
    for name, (at, n) in COLS.items():
        w["cols"][:, at:at + n] = c[name]
    w["cons"] = constants()
    return {k: np.ascontiguousarray(v) for k, v in w.items()}


def kernel(**inputs):
    import concourse.bacc as bacc
    from concourse.bass_utils import run_bass_kernel_spmd

    nc = bacc.Bacc("TRN2", target_bir_lowering=False, num_devices=1)
    arrays, w = {}, {}
    for name, v in lay_out({k: np.asarray(v) for k, v in inputs.items()}).items():
        arrays[f"in_{name}"] = v
        w[name] = nc.dram_tensor(f"in_{name}", v.shape, F32, kind="ExternalInput").ap()
    out = nc.dram_tensor("out_x", (P, DC, T), F32, kind="ExternalOutput").ap()
    build(nc, w, out)
    r = run_bass_kernel_spmd(nc, [arrays], core_ids=[0])
    got = np.asarray(r.results[0]["out_x"])
    return np.ascontiguousarray(got.transpose(2, 1, 0).reshape(1, T, D))
```

```python
from contextlib import ExitStack

import numpy as np

import concourse.bass as bass
from concourse import mybir

F32 = mybir.dt.float32
F32R = mybir.dt.float32r
ALU = mybir.AluOpType
ACT = mybir.ActivationFunctionType
AXX = mybir.AxisListType.X

P = 128
D = 1024
DC = D // P
T = 256
TT = T // P
N2 = 2 * T
DEPTH = 2
H = 8
Q_LORA, KV_LORA = 384, 256
NOPE, ROPE_D, VD = 64, 32, 64
QC, KVC = Q_LORA // P, KV_LORA // P
IDX_DIM = 32
KEEP = T // 4
E_N, E_F = 16, 512
MOE_CH = E_N * E_F // P
DFF = 2816
FF_CH = DFF // P
GH, GD = 4, 128
GCONV, CCONV = 5, 31
CCH = 4
AH, AKV, AD = 8, 2, 128
N_MOD = 9
LEVELS = 7
ATANH_TERMS = 8
ALPHA = (2.0 * DEPTH) ** 0.25
LN_EPS, RMS_EPS = 1e-5, 1e-6
NEG = -1.0e30
TAKEN = -3.0e38
SLOTS = 4
UNIT = 2048
HALVES = 4
MOE_SEG = 16
FF_SEGS = (12, 10)
SLOPES = [2.0 ** (-8.0 * (h + 1) / H) for h in range(H)]


def columns(parts):
    table, at = {}, 0
    for name, n in parts:
        table[name] = (at, n)
        at += n
    return table, at


PER_LAYER = (("qg", QC), ("kvg", KVC), ("ln1g", DC), ("ln1b", DC), ("ln2g", DC), ("ln2b", DC), ("adab", N_MOD * DC),
             ("lng0", DC), ("lnb0", DC), ("lng1", DC), ("lnb1", DC), ("lng2", DC), ("lnb2", DC))
COLS, NCOLS = columns([(f"{n}{layer}", c) for layer in range(DEPTH) for n, c in PER_LAYER] + [
    ("cond", 2 * DC), ("gconv", 12 * GCONV), ("cconv", CCH * CCONV), ("cbias", CCH), ("clng", CCH), ("clnb", CCH),
    ("qn", 1), ("kn", 1), ("rbias", E_N), ("alog", 2 * GH), ("dtb", 2 * GH), ("outn", GD), ("rw", DC * E_N)])
CONS, NCONS = columns([
    ("ident", P), ("ones", P), ("perm32", P), ("permA", P), ("cos32", T), ("sin32", T), ("cosA", T), ("sinA", T),
    ("causal", TT * T), ("dist", TT * T), ("first4", 4), ("first16", E_N), ("tri0", P), ("tri1", P),
    ("lvl0", LEVELS * P), ("lvl1", LEVELS * P)])


class Stage:

    def __init__(self, name, base, marks):
        self.name, self.base, self.u0 = name, dict(base), None
        self.names, self.total, self.seen = {}, {}, {"pe": 0, "act": 0, "dve": 0}
        for eng in ("pe", "act", "dve"):
            m = marks.get(eng, [])
            self.names[eng] = {} if isinstance(m, int) else {n: i + 1 for i, n in enumerate(m)}
            self.total[eng] = (m if isinstance(m, int) else len(m)) + 1

    def v(self, eng, name):
        return self.base[eng] + (name if isinstance(name, int) else self.names[eng][name])

    def one(self, eng, name):
        self.seen[eng] += 1
        assert self.names[eng][name] == self.seen[eng], (self.name, eng, name, self.seen[eng])
        return 1


class Chain:

    def __init__(self, eng, step):
        self.eng, self.step, self.n = eng, step, 0

    def __call__(self, ins):
        ins.then_inc(self.step, 1)
        self.n += 1
        self.eng.wait_ge(self.step, self.n)

    def inside(self, i, per_turn):
        c = Chain(self.eng, self.step)
        c.n = self.n + i * per_turn
        return c


def outer(ap, n):
    return ap.unsqueeze(1).broadcast_to([P, n, ap.shape[-1]])


def inner(ap, n):
    return ap.unsqueeze(2).broadcast_to([P, ap.shape[-1], n])


def build(nc, w, out):
    with ExitStack() as ctx:
        def sb(name, shape):
            return ctx.enter_context(nc.sbuf_tensor(name, shape, F32))

        def sem(name):
            return ctx.enter_context(nc.semaphore(name))

        ring = sb("ring", [P, SLOTS, UNIT])
        cols = sb("cols", [P, NCOLS])
        cons = sb("cons", [P, NCONS])
        X = sb("X", [P, DC, N2])
        Y = sb("Y", [P, DC, N2])
        MD = sb("MD", [P, DEPTH, N_MOD, DC, 2])
        condT = sb("condT", [P, DC, 2])
        row = sb("row", [P, 2, N2])
        small = sb("small", [P, 32])
        tmp = sb("tmp", [P, 2, N2])
        def part(memory, name, shape, dt=F32R):
            return memory.enter_context(nc.sbuf_tensor(name, shape, dt))

        with ExitStack() as both_:
            w_hi, w_lo = part(both_, "w_hi", [P, HALVES, D]), part(both_, "w_lo", [P, HALVES, D])
            with ExitStack() as one:
                x_hi, x_lo = part(one, "x_hi", [P, DC, N2]), part(one, "x_lo", [P, DC, N2])
                h_hi, h_lo = part(one, "h_hi", [P, FF_SEGS[0], N2]), part(one, "h_lo", [P, FF_SEGS[0], N2])
            with ExitStack() as other:
                m_hi, m_lo = part(other, "m_hi", [P, DC, T]), part(other, "m_lo", [P, DC, T])
                e_hi, e_lo = part(other, "e_hi", [P, MOE_SEG, T]), part(other, "e_lo", [P, MOE_SEG, T])
                gate_b = part(other, "gate_b", [P, E_N, T], F32)
        HM = sb("HM", [P, DC, N2])
        AREA = 24000
        area = sb("area", [P, AREA])
        ps = ctx.enter_context(nc.psum_tensor("ps", [P, 8, 512], F32))

        pe_done, act_done, dve_done = sem("pe_done"), sem("act_done"), sem("dve_done")
        act_step, dve_step = sem("act_step"), sem("dve_step")
        arrived = [sem(f"arrived{i}") for i in range(SLOTS)]
        tables_in, out_done = sem("tables_in"), sem("out_done")
        hi_done, lo_done, half_used = sem("hi_done"), sem("lo_done"), sem("half_used")
        silu_done, hid_done, banks_read = sem("silu_done"), sem("hid_done"), sem("banks_read")
        xin_done, xhi_done, xlo_done = sem("xin_done"), sem("xhi_done"), sem("xlo_done")

        def col(name, i=0, n=1):
            a = COLS[name][0] + i
            return cols[:, a:a + n]

        def con(name, a=0, n=None):
            s, c = CONS[name]
            return cons[:, s + a:s + (c if n is None else a + n)]

        ident, ones = con("ident"), con("ones")

        class Space:

            def __init__(self, at=0, end=AREA, base=area):
                self.at, self.end, self.base = at, end, base

            def take(self, *shape):
                n = int(np.prod(shape))
                v = self.base[:, self.at:self.at + n]
                self.at += n
                assert self.at <= self.end, self.at
                names = "abcd"[:len(shape)]
                if len(shape) > 1:
                    v = v.rearrange(f"p ({' '.join(names)}) -> p {' '.join(names)}", **dict(zip(names, shape)))
                return v

        s = Space()
        selE = s.take(E_N, P)
        G128, gT, R = s.take(TT, P), s.take(TT * P), s.take(16, 2 * E_N)
        s = Space()
        QA, KVA, DQ, IQ, KR = s.take(QC, T), s.take(KVC, T), s.take(4, T), s.take(2, T), s.take(T)
        padded_from = s.at
        IKz, DKz, KRz, KNz = s.take(4, T), s.take(2, T), s.take(4, T), s.take(4, 2, T)
        DVz, Vz = s.take(TT, 2, P), s.take(TT, H, P)
        zero_padded = area[:, padded_from:s.at]
        IW, QN, QR = s.take(TT, H), s.take(4, T), s.take(2, T)
        S1, PT = s.take(2048), s.take(16, P)
        SC, SB, top8 = s.take(2, T), s.take(H, T), s.take(8)
        OT1 = HM[:, :, 0:T]
        s = Space()
        CI = s.take(12, 2, T + GCONV - 1)
        QKV = s.take(12, N2)
        pair_at = s.at
        GL, VAL = s.take(CCH, 2, T + CCONV - 1), s.take(CCH, N2)
        pair_end = s.at
        Zr, AB, Gg, Bb = s.take(4, 512), s.take(4, 16), s.take(4, 8), s.take(4, 8)
        St, CF = s.take(2, GH * P), s.take(CCH, N2)
        gp = s.take(4, 40)
        SGt = s.take(N2)
        small2 = small
        Yf = Y[:].rearrange("p a b -> p (a b)")
        tail_at = s.at
        s = Space()
        rowK, rowV, OR = s.take(4, GH, P), s.take(4, GH, P), s.take(4, GH, P)
        assert s.at <= 12 * 2 * (T + GCONV - 1)
        big = [Y[:].rearrange("p a b -> p (a b)"), HM[:].rearrange("p a b -> p (a b)")]
        half = (pair_end - pair_at) // 2

        def per_direction(d):
            a, b = Space(0, 4096, big[d]), Space(pair_at + d * half, pair_at + (d + 1) * half)
            names = ("gB", "bB", "DEC", "MT", "AT", "XT", "Xi", "R")
            got = {n: a.take(GH, P) for n in names}
            got.update({n: b.take(GH, P) for n in ("Yv", "QS", "ET0", "ET1")})
            got["VB"] = Space(tail_at + d * 544).take(GH, P)
            got["sm"] = Space(tail_at + d * 544 + 512).take(32)
            return got

        DN = [per_direction(0), per_direction(1)]
        s = Space()
        AQ, AK, SQq, SQk = s.take(AH, T), s.take(AKV, N2), s.take(AH, T), s.take(AKV, N2)
        AV, S2, PT2 = s.take(4, AKV * AD), s.take(2048), s.take(16, P)
        OT2 = HM[:, :, 0:T]

        now = {"pe": 0, "act": 0, "dve": 0}
        stages, streams, unit_count = {}, [], [0]

        def stage(name, **marks):
            st = Stage(name, now, marks)
            for k in now:
                now[k] += st.total[k]
            stages[name] = st
            return st

        def stream(st, tensor, n, first, step, width=UNIT, split=False):
            if st.u0 is None:
                st.u0 = unit_count[0]
            if not split:
                first += st.base["pe"]
            streams.append((tensor, n, lo_done if split else pe_done, first, step, width, unit_count[0]))
            unit_count[0] += n

        def ln_stage(name):
            stage(name, pe=["mean", "var"], act=["mean", *[f"sq{k}" for k in range(DC)], "root"], dve=["centred", "eps"])

        def attention_stage(name):
            stage(name, pe=["scores", "turned", "mixed"], act=["exp", "turned", "out"], dve=["ready", "probs"])

        count = {"h": 0, "c": 0, "b": 0, "x": 0, "k": 0}

        def ffn_stage(name, segments, wu, wd, modulated=None):
            st = stage(name)
            st.segments, st.modulated = segments, modulated
            st.h0, st.c0, st.b0, st.x0, st.k0 = count["h"], count["c"], count["b"], count["x"], count["k"]
            c, h = 0, st.h0
            for m in segments:
                for tensor, n in ((wu[c:c + m], m), (wd[c // 2:(c + m) // 2], m // 2)):
                    stream(st, tensor, n, h + 2, 2, split=True)
                    h += 2 * n
                c += m
            count.update(h=h, c=st.c0 + c, b=st.b0 + DC * len(segments), x=st.x0 + 1, k=st.k0 + (DC if modulated else 0))

        for l in range(DEPTH):
            n = f"b1.{l}."
            st = stage(n + "in", pe=[f"c{c}" for c in range(14)] + ["rows"], act=[f"c{c}" for c in range(14)] + ["rows"], dve=["zeroed"])
            stream(st, w["w_in"][l], 7, 2, 2)
            stream(st, w["w_in_rows"][l], 1, 15, 1, DC * 72)
            stage(n + "rms", pe=["sums"], act=["sq", "root"], dve=["eps"])
            st = stage(n + "up", pe=[f"c{c}" for c in range(10)] + ["rows"], act=[f"c{c}" for c in range(10)] + ["rows"])
            stream(st, w["w_q_up"][l], 2, 3, 3, 3 * QC * P)
            stream(st, w["w_ukv"][l], 1, 11, 1)
            stage(n + "rope", pe=["swapped"])
            for t in range(TT):
                stage(f"{n}index{t}", pe=["scores"], act=["relu"])
                attention_stage(f"{n}mla{t}")
                attention_stage(f"{n}dsa{t}")
            stream(stage(n + "out", pe=DC), w["w_o"][l], DC // 2, 2, 2)
            ln_stage(n + "ln1")
            stage(n + "router", pe=["logits", "turned", "spread0", "spread1"], act=["exp", "turned", "spread0", "spread1"], dve=["gates"])
            ffn_stage(n + "moe", (MOE_SEG,) * (MOE_CH // MOE_SEG), w["moe_up"][l], w["moe_down"][l])
            ln_stage(n + "ln2")
        for l in range(DEPTH):
            n = f"b2.{l}."
            stream(stage(n + "ada", pe=4 * N_MOD, dve=2 * N_MOD), w["ada"][l], 4 * N_MOD, 1, 1)
            ffn_stage(n + "ffn0", FF_SEGS, w["ff_up"][l, 0], w["ff_down"][l, 0], (0, 1))
            ln_stage(n + "ln0")
            stage(n + "mod1")
            if l == 0:
                order = [f"c{c}" for c in range(20)]
                st = stage(n + "in", pe=order + ["ab", "z"], act=order + ["ab", "z"], dve=["g0", "g1", "g2", "g3"])
                stream(st, w["even_in"], 10, 2, 2)
                stream(st, w["even_ab"], 1, 21, 1, DC * 16)
                stream(st, w["even_z"], 2, 22, 0)
                stage(n + "conv", act=[f"silu{c}" for c in range(12)] + ["ln", "sq", "root"], pe=["mean", "var"],
                      dve=[f"c{c}" for c in range(12)] + ["y", "centred", "eps", "normed"])
                stage(n + "l2", pe=["sums"], act=["sq", "root"], dve=["eps"])
                stage(n + "rows", pe=["k0", "v0", "k1", "v1", "k2", "v2", "k3", "v3"],
                      act=["exp", "k0", "v0", "k1", "v1", "k2", "v2", "k3", "v3"], dve=["dt"])
                for i in range(4):
                    both = lambda *names: [f"{x}.{d}" for x in names for d in range(2)]
                    lv = [x for j in range(LEVELS) for x in both(f"Y{j}", f"Z{j}")]
                    stage(f"{n}scan{i}", pe=both("A", "B") + lv + both("V", "O"),
                          act=both("exp") + both("qs") + both(*[f"Y{j}" for j in range(LEVELS)]) + both("vn"),
                          dve=both("inp") + both("dec") + both("mt") + both("at") + both(*[f"X{j}" for j in range(LEVELS)]))
                stage(n + "merge", pe=["turned"], act=["sq", "root"], dve=["eps", "ready"])
            else:
                order = [f"q{c}" for c in range(AH)] + [f"k{c}" for c in range(AKV)] + ["v"]
                st = stage(n + "in", pe=order, act=order)
                stream(st, w["attn_in"], 5, 2, 2)
                stream(st, w["attn_v"], 1, 11, 1)
                stage(n + "rms", pe=["sums"], act=["sq", "root"], dve=["eps"])
                stage(n + "rope", pe=["swapped"])
                for t in range(TT):
                    for h in range(AKV):
                        attention_stage(f"{n}gqa{t}{h}")
            stream(stage(n + "out", pe=DC), w["even_out"] if l == 0 else w["attn_out"], DC // 2, 2, 2)
            ln_stage(n + "ln1")
            ffn_stage(n + "ffn1", FF_SEGS, w["ff_up"][l, 1], w["ff_down"][l, 1], (6, 7))
            ln_stage(n + "ln2")

        def enter(eng, name):
            st = stages[name]
            if st.base["pe"]:
                eng.wait_ge(pe_done, st.base["pe"])
                eng.wait_ge(act_done, st.base["act"])
                eng.wait_ge(dve_done, st.base["dve"])
            return st

        def fill_ring(sp):
            released = []
            for tensor, n, done, first, step, width, u0 in streams:
                released += [(done, first + c * step) for c in range(n)]
            for tensor, n, done, first, step, width, u0 in streams:
                turns = max(0, n - SLOTS) // SLOTS
                head = SLOTS if turns > 1 else n
                if turns <= 1:
                    turns = 0

                def load(c, j, free):
                    if free is not None:
                        sp.wait_ge(*free)
                    sp.dma_start(ring[:, (u0 + j) % SLOTS, 0:width], tensor[c]).then_inc(arrived[(u0 + j) % SLOTS], 16)

                for c in range(head):
                    u = u0 + c
                    load(c, c, released[u - SLOTS] if u >= SLOTS else None)
                if turns:
                    with sp.Fori(0, turns) as i:
                        for j in range(SLOTS):
                            load(SLOTS * i + SLOTS + j, j, (done, first + j * step + SLOTS * step * i))
                for c in range(head + SLOTS * turns, n):
                    load(c, c, released[u0 + c - SLOTS])

        def unit_here(pe, u, i=None):
            value = 16 * (u // SLOTS + 1)
            pe.wait_ge(arrived[u % SLOTS], value if i is None else value + 16 * i)
            return ring[:, u % SLOTS, :]

        def dot(pe, dst, pairs):
            for n, (a, b) in enumerate(pairs):
                ins = pe.matmul(dst, a, b, start=(n == 0), stop=(n == len(pairs) - 1))
            return ins

        def three(pe, dst, hi, lo, xh, xl, start, stop):
            pe.matmul(dst, hi, xh, start=start, stop=False, skip_group_check=True)
            pe.matmul(dst, hi, xl, start=False, stop=False, skip_group_check=True)
            return pe.matmul(dst, lo, xh, start=False, stop=stop, skip_group_check=True)

        def ffn_pe(pe, name, n, xh, xl, hh, hl):
            st = enter(pe, name)
            pe.wait_ge(xlo_done, st.x0 + 1)

            def half(j, i):
                value = st.h0 + j + 1
                pe.wait_ge(lo_done, value if i is None else value + HALVES * i)
                return w_hi[:, j % HALVES, :], w_lo[:, j % HALVES, :]

            def up(j, c, i, free):
                if free is not None:
                    pe.wait_ge(hid_done, free)
                for e in range(2):
                    hi, lo = half(j + e, i)
                    for k in range(DC):
                        ins = three(pe, ps[:, 2 * (c % 2) + e, 0:n], hi[:, k * P:(k + 1) * P], lo[:, k * P:(k + 1) * P],
                                    xh[:, k, 0:n], xl[:, k, 0:n], k == 0, k == DC - 1)
                    ins.then_inc(half_used, 1)

            def down(j, f, i, first, last):
                hi, lo = half(j, i)
                for d in range(DC):
                    ins = three(pe, ps[:, d, 0:n], hi[:, d * P:(d + 1) * P], lo[:, d * P:(d + 1) * P],
                                hh[:, f, 0:n], hl[:, f, 0:n], first, last)
                ins.then_inc(half_used, 1)

            j = c = 0
            for seg, m in enumerate(st.segments):
                if seg:
                    pe.wait_ge(banks_read, st.b0 + DC * seg - 4)
                up(j, 0, None, None)
                up(j + 2, 1, None, None)
                with pe.Fori(0, m // 2 - 1) as i:
                    for e in range(2):
                        up(j + 4 + 2 * e, e, i, st.c0 + c + 1 + e + 2 * i)
                j, c = j + 2 * m, c + m
                pe.wait_ge(hid_done, st.c0 + c)
                if seg:
                    pe.wait_ge(banks_read, st.b0 + DC * seg)
                for f in range(HALVES):
                    down(j + f, f, None, f == 0, False)
                turns = (m - HALVES - 1) // HALVES
                with pe.Fori(0, turns) as i:
                    for f in range(HALVES):
                        down(j + HALVES + f, HALVES * i + HALVES + f, i, False, False)
                for f in range(HALVES * (turns + 1), m):
                    down(j + f, f, None, False, f == m - 1)
                j += m
            pe.drain().then_inc(pe_done, 1)

        def steps(eng, count, body, turn, first=0):
            for s_ in range(first):
                body(s_, None)
            turns = (count - first) // turn
            if turns:
                with eng.Fori(0, turns) as i:
                    for s_ in range(turn):
                        body(first + s_, i)
            for s_ in range(first + turns * turn, count):
                body(s_, None)

        def ffn_act(act, name, n, src, xh):
            st = enter(act, name)
            total = 3 * sum(st.segments)

            def split(j, i):
                u = st.u0 + j // 2
                if j % 2 == 0:
                    value = 16 * (u // SLOTS + 1)
                    act.wait_ge(arrived[u % SLOTS], value if i is None else value + 16 * i)
                if j >= HALVES:
                    value = st.h0 + j - HALVES + 1
                    act.wait_ge(half_used, value if i is None else value + 2 * SLOTS * i)
                act.activation(w_hi[:, j % HALVES, :], ring[:, u % SLOTS, (j % 2) * D:(j % 2 + 1) * D], ACT.Copy)\
                   .then_inc(hi_done, 1)

            for j in range(HALVES):
                split(j, None)
            for k in range(DC):
                if st.modulated:
                    act.wait_ge(xin_done, st.k0 + k + 1)
                ins = act.activation(xh[:, k, 0:n], src[:, k, 0:n], ACT.Copy)
            ins.then_inc(xhi_done, 1)
            j = c = 0
            for m in st.segments:
                def chunk(s_, i):
                    value = st.h0 + j + 2 * s_ + 1
                    act.wait_ge(half_used, value if i is None else value + 2 * SLOTS * i)
                    if c + s_ >= 2:
                        value = st.c0 + c + s_ - 1
                        act.wait_ge(hid_done, value if i is None else value + SLOTS * i)
                    act.activation(row[:, s_ % 2, 0:n], ps[:, 2 * (s_ % 2), 0:n], ACT.Silu).then_inc(silu_done, 1)
                    split(j + HALVES + 2 * s_, i)
                    split(j + HALVES + 2 * s_ + 1, i)

                steps(act, m, chunk, SLOTS, 0 if c else SLOTS)
                j, c = j + 2 * m, c + m
                ahead = m if j + m < total else m - HALVES
                steps(act, ahead, lambda s_, i: split(j + HALVES + s_, i), 2 * SLOTS)
                j += m
            act.drain().then_inc(act_done, 1)

        def ffn_dve(dve, link, name, l, n, src, xh, xl, hh, hl, gate):
            st = enter(dve, name)
            total = 3 * sum(st.segments)

            def split(j, i):
                u = st.u0 + j // 2
                value = st.h0 + j + 1
                dve.wait_ge(hi_done, value if i is None else value + 2 * SLOTS * i)
                dve.tensor_tensor(w_lo[:, j % HALVES, :], ring[:, u % SLOTS, (j % 2) * D:(j % 2 + 1) * D],
                                  w_hi[:, j % HALVES, :].bitcast(F32), ALU.subtract).then_inc(lo_done, 1)

            if st.modulated:
                shift, scale = st.modulated
                for k in range(DC):
                    for part_ in range(n // T):
                        c = slice(part_ * T, (part_ + 1) * T)
                        ins = dve.tensor_scalar(Y[:, k, c], X[:, k, c], MD[:, l, scale, k, part_:part_ + 1],
                                                MD[:, l, shift, k, part_:part_ + 1], ALU.mult, ALU.add)
                    ins.then_inc(xin_done, 1)
            dve.wait_ge(xhi_done, st.x0 + 1)
            if st.modulated:
                dve.wait_ge(xin_done, st.k0 + DC)
            dve.tensor_tensor(xl[:, :, 0:n], src[:, :, 0:n], xh[:, :, 0:n].bitcast(F32), ALU.subtract).then_inc(xlo_done, 1)
            for j in range(HALVES):
                split(j, None)
            dve.wait_ge(xlo_done, st.x0 + 1)
            link(dve.tensor_scalar(Y[:, :, 0:n], X[:, :, 0:n], ALPHA, None, ALU.mult))
            j = c = 0
            for seg, m in enumerate(st.segments):
                links = 3 if gate is None else 2

                def chunk(s_, i):
                    split(j + HALVES + 2 * s_, i)
                    chain = link if i is None else link.inside(i, SLOTS * links)
                    if i is not None:
                        chain.n = chain.n + links * ((s_ - (0 if c else SLOTS)) % SLOTS)
                    value = st.c0 + c + s_ + 1
                    dve.wait_ge(silu_done, value if i is None else value + SLOTS * i)
                    value = st.h0 + j + 2 * s_ + 2
                    dve.wait_ge(half_used, value if i is None else value + 2 * SLOTS * i)
                    f = s_ if i is None else SLOTS * i + s_
                    t = tmp[:, s_ % 2, 0:n]
                    chain(dve.tensor_tensor(t, row[:, s_ % 2, 0:n], ps[:, 2 * (s_ % 2) + 1, 0:n], ALU.mult))
                    if gate is None:
                        e = c // 4 + s_ // 4
                        chain(dve.tensor_tensor(t, t, gate_b[:, e if i is None else e + i, :], ALU.mult))
                    chain(dve.tensor_copy(hh[:, f, 0:n], t))
                    dve.tensor_tensor(hl[:, f, 0:n], t, hh[:, f, 0:n].bitcast(F32), ALU.subtract).then_inc(hid_done, 1)
                    split(j + HALVES + 2 * s_ + 1, i)

                first = 0 if c else SLOTS
                turns = (m - first) // SLOTS
                for s_ in range(first):
                    chunk(s_, None)
                with dve.Fori(0, turns) as i:
                    for s_ in range(first, first + SLOTS):
                        chunk(s_, i)
                link.n += links * SLOTS * turns
                for s_ in range(first + SLOTS * turns, m):
                    chunk(s_, None)
                j, c = j + 2 * m, c + m
                ahead = m if j + m < total else m - HALVES
                steps(dve, ahead, lambda s_, i: split(j + HALVES + s_, i), 2 * SLOTS)
                j += m
                dve.wait_ge(half_used, st.h0 + j)
                if seg:
                    dve.wait_ge(banks_read, st.b0 + DC * seg)
                for d in range(DC):
                    for part_ in range(n // T):
                        cc = slice(part_ * T, (part_ + 1) * T)
                        if gate is None:
                            ins = dve.tensor_tensor(Y[:, d, cc], ps[:, d, cc], Y[:, d, cc], ALU.add)
                        else:
                            ins = dve.scalar_tensor_tensor(Y[:, d, cc], ps[:, d, cc], MD[:, l, gate, d, part_:part_ + 1],
                                                           Y[:, d, cc], ALU.mult, ALU.add)
                    ins.then_inc(banks_read, 1)
            dve.drain().then_inc(dve_done, 1)

        def add_residual(dve, link, st, last_mark, l, gate, n):
            link(dve.tensor_scalar(Y[:, :, 0:n], X[:, :, 0:n], ALPHA, None, ALU.mult))
            if isinstance(last_mark, int):
                dve.wait_ge(pe_done, st.v("pe", last_mark))
            for d in range(DC):
                for part in range(n // T):
                    c = slice(part * T, (part + 1) * T)
                    if gate is None:
                        dve.tensor_tensor(Y[:, d, c], ps[:, d, c], Y[:, d, c], ALU.add)
                    else:
                        dve.scalar_tensor_tensor(Y[:, d, c], ps[:, d, c], MD[:, l, gate, d, part:part + 1], Y[:, d, c],
                                                 ALU.mult, ALU.add)
            dve.drain().then_inc(dve_done, 1)

        def out_pe(pe, name, src, n):
            st = enter(pe, name)
            for d in range(DC):
                wt = unit_here(pe, st.u0 + d // 2)
                o = (d % 2) * D
                dot(pe, ps[:, d, 0:n], [(wt[:, o + k * P:o + (k + 1) * P], src(k)) for k in range(DC)]).then_inc(pe_done, 1)
            pe.drain().then_inc(pe_done, 1)

        def ln_pe(pe, name, n):
            st = enter(pe, name)
            dot(pe, ps[:, 0, 0:n], [(ones, Y[:, k, 0:n]) for k in range(DC)]).then_inc(pe_done, st.one("pe", "mean"))
            for k in range(DC):
                pe.wait_ge(act_done, st.v("act", f"sq{k}"))
                ins = pe.matmul(ps[:, 1, 0:n], ones, HM[:, k, 0:n], start=(k == 0), stop=(k == DC - 1))
            ins.then_inc(pe_done, st.one("pe", "var"))
            pe.drain().then_inc(pe_done, 1)

        def ln_act(act, name, n):
            st = enter(act, name)
            act.wait_ge(pe_done, st.v("pe", "mean"))
            act.activation(row[:, 0, 0:n], ps[:, 0, 0:n], ACT.Copy, scale=1.0 / D).then_inc(act_done, st.one("act", "mean"))
            act.wait_ge(dve_done, st.v("dve", "centred"))
            for k in range(DC):
                act.activation(HM[:, k, 0:n], Y[:, k, 0:n], ACT.Square).then_inc(act_done, st.one("act", f"sq{k}"))
            act.wait_ge(dve_done, st.v("dve", "eps"))
            act.activation(row[:, 1, 0:n], row[:, 0, 0:n], ACT.Sqrt).then_inc(act_done, st.one("act", "root"))
            act.drain().then_inc(act_done, 1)

        def ln_dve(dve, link, name, n, g, b):
            st = enter(dve, name)
            dve.wait_ge(act_done, st.v("act", "mean"))
            dve.tensor_tensor(Y[:, :, 0:n], Y[:, :, 0:n], outer(row[:, 0, 0:n], DC), ALU.subtract)\
               .then_inc(dve_done, st.one("dve", "centred"))
            dve.wait_ge(pe_done, st.v("pe", "var"))
            dve.tensor_scalar(row[:, 0, 0:n], ps[:, 1, 0:n], 1.0 / D, LN_EPS, ALU.mult, ALU.add)\
               .then_inc(dve_done, st.one("dve", "eps"))
            dve.wait_ge(act_done, st.v("act", "root"))
            link(dve.reciprocal(row[:, 0, 0:n], row[:, 1, 0:n]))
            link(dve.tensor_tensor(Y[:, :, 0:n], Y[:, :, 0:n], outer(row[:, 0, 0:n], DC), ALU.mult))
            for k in range(DC):
                dve.tensor_scalar(X[:, k, 0:n], Y[:, k, 0:n], col(g, k), col(b, k), ALU.mult, ALU.add)
            dve.drain().then_inc(dve_done, 1)

        def modulate(dve, name, l, shift, scale):
            enter(dve, name)
            for k in range(DC):
                for part in range(2):
                    c = slice(part * T, (part + 1) * T)
                    dve.tensor_scalar(HM[:, k, c], X[:, k, c], MD[:, l, scale, k, part:part + 1],
                                      MD[:, l, shift, k, part:part + 1], ALU.mult, ALU.add)
            dve.drain().then_inc(dve_done, 1)

        def idle(eng, done, name):
            enter(eng, name)
            eng.drain().then_inc(done, 1)

        def attention_pe(pe, name, scores, mix, probs, turned):
            st = enter(pe, name)
            width = 2048 // len(scores)
            flat = ps[:].rearrange("p a b -> p (a b)")
            for h, pairs in enumerate(scores):
                ins = dot(pe, flat[:, h * width:(h + 1) * width], pairs)
            ins.then_inc(pe_done, st.one("pe", "scores"))
            pe.wait_ge(dve_done, st.v("dve", "probs"))
            for b in range(16):
                ins = pe.transpose(flat[:, 2048 + b * P:2048 + (b + 1) * P], probs[:, b * P:(b + 1) * P], ident)
            ins.then_inc(pe_done, st.one("pe", "turned"))
            pe.wait_ge(act_done, st.v("act", "turned"))
            for i, terms in enumerate(mix):
                ins = dot(pe, ps[:, 0, i * P:(i + 1) * P], [(v, turned[:, b, :]) for v, b in terms])
            ins.then_inc(pe_done, st.one("pe", "mixed"))
            pe.drain().then_inc(pe_done, 1)

        def attention_act(act, name, probs, turned, dst):
            st = enter(act, name)
            act.wait_ge(dve_done, st.v("dve", "ready"))
            act.activation(probs, probs, ACT.Exp).then_inc(act_done, st.one("act", "exp"))
            act.wait_ge(pe_done, st.v("pe", "turned"))
            act.activation(turned.rearrange("p a b -> p (a b)"), ps[:, 4:8, :].rearrange("p a b -> p (a b)"), ACT.Copy)\
               .then_inc(act_done, st.one("act", "turned"))
            act.wait_ge(pe_done, st.v("pe", "mixed"))
            act.activation(dst, ps[:, 0, :].rearrange("p (a b) -> p a b", a=4), ACT.Copy)\
               .then_inc(act_done, st.one("act", "out"))
            act.drain().then_inc(act_done, 1)

        def attention_dve(dve, link, name, heads, probs, scale, mask):
            st = enter(dve, name)
            keys = 2048 // heads
            s3 = probs.rearrange("p (h k) -> p h k", h=heads)
            p3 = ps[:, 0:4, :].rearrange("p a b -> p (a b)").rearrange("p (h k) -> p h k", h=heads)
            mx, total = small[:, 0:heads], small[:, 8:8 + heads]
            dve.wait_ge(pe_done, st.v("pe", "scores"))
            if mask is None:
                link(dve.tensor_scalar(s3, p3, scale, None, ALU.mult))
            else:
                link(dve.scalar_tensor_tensor(s3, p3, scale, mask, ALU.mult, ALU.add))
            link(dve.tensor_reduce(mx, s3, AXX, ALU.max))
            dve.tensor_tensor(s3, s3, inner(mx, keys), ALU.subtract).then_inc(dve_done, st.one("dve", "ready"))
            dve.wait_ge(act_done, st.v("act", "exp"))
            link(dve.tensor_reduce(total, s3, AXX, ALU.add))
            link(dve.reciprocal(mx, total))
            dve.tensor_tensor(s3, s3, inner(mx, keys), ALU.mult).then_inc(dve_done, st.one("dve", "probs"))
            dve.drain().then_inc(dve_done, 1)

        def in1_pe(pe, n):
            st = enter(pe, n)
            for c in range(14):
                wt = unit_here(pe, st.u0 + c // 2)
                if c >= 8:
                    pe.wait_ge(act_done, st.v("act", f"c{c - 8}"))
                o = (c % 2) * D
                dot(pe, ps[:, c % 8, 0:T], [(wt[:, o + k * P:o + (k + 1) * P], X[:, k, 0:T]) for k in range(DC)])\
                    .then_inc(pe_done, st.one("pe", f"c{c}"))
            wt = unit_here(pe, st.u0 + 7)
            pe.wait_ge(act_done, st.v("act", "c7"))
            for t in range(TT):
                ins = dot(pe, ps[:, 6 + t, 0:72], [(X[:, k, t * P:(t + 1) * P], wt[:, k * 72:(k + 1) * 72]) for k in range(DC)])
            ins.then_inc(pe_done, st.one("pe", "rows"))
            pe.drain().then_inc(pe_done, 1)

        def copy_marked(act, st, bank, pairs, mark):
            act.wait_ge(pe_done, st.v("pe", mark))
            for dst, src in pairs:
                ins = act.activation(dst, src, ACT.Copy)
            ins.then_inc(act_done, st.one("act", mark))

        def in1_act(act, n):
            st = enter(act, n)
            plain = [QA[:, 0, :], QA[:, 1, :], QA[:, 2, :], KVA[:, 0, :], KVA[:, 1, :],
                     *[DQ[:, i, :] for i in range(4)], IQ[:, 0, :], IQ[:, 1, :], KR]
            for c, dst in enumerate(plain):
                copy_marked(act, st, c % 8, [(dst, ps[:, c % 8, 0:T])], f"c{c}")
            act.wait_ge(dve_done, st.v("dve", "zeroed"))
            copy_marked(act, st, 4, [(IKz[32 * j:32 * j + 32, j, :], ps[32 * j:32 * j + 32, 4, 0:T]) for j in range(4)], "c12")
            copy_marked(act, st, 5, [(DKz[64 * j:64 * j + 64, j, :], ps[64 * j:64 * j + 64, 5, 0:T]) for j in range(2)], "c13")
            act.wait_ge(pe_done, st.v("pe", "rows"))
            for t in range(TT):
                act.activation(IW[:, t, :], ps[:, 6 + t, 0:H], ACT.Copy, scale=H ** -0.5)
                for e in range(2):
                    ins = act.activation(DVz[:, t, e, e * VD:(e + 1) * VD], ps[:, 6 + t, H:H + VD], ACT.Copy)
            ins.then_inc(act_done, st.one("act", "rows"))
            act.drain().then_inc(act_done, 1)

        def in1_dve(dve, n):
            st = enter(dve, n)
            dve.memset(zero_padded, 0.0).then_inc(dve_done, st.one("dve", "zeroed"))
            dve.drain().then_inc(dve_done, 1)

        def rms1_pe(pe, n):
            st = enter(pe, n)
            pe.wait_ge(act_done, st.v("act", "sq"))
            dot(pe, ps[:, 0, 0:T], [(ones, HM[:, k, 0:T]) for k in range(QC)])
            dot(pe, ps[:, 1, 0:T], [(ones, HM[:, QC + k, 0:T]) for k in range(KVC)]).then_inc(pe_done, st.one("pe", "sums"))
            pe.drain().then_inc(pe_done, 1)

        def rms1_act(act, n):
            st = enter(act, n)
            act.activation(HM[:, 0:QC, 0:T], QA, ACT.Square)
            act.activation(HM[:, QC:QC + KVC, 0:T], KVA, ACT.Square).then_inc(act_done, st.one("act", "sq"))
            act.wait_ge(dve_done, st.v("dve", "eps"))
            act.activation(row[:, 1, :], row[:, 0, :], ACT.Sqrt).then_inc(act_done, st.one("act", "root"))
            act.drain().then_inc(act_done, 1)

        def rms1_dve(dve, link, n, l):
            st = enter(dve, n)
            dve.wait_ge(pe_done, st.v("pe", "sums"))
            dve.tensor_scalar(row[:, 0, 0:T], ps[:, 0, 0:T], 1.0 / Q_LORA, RMS_EPS, ALU.mult, ALU.add)
            dve.tensor_scalar(row[:, 0, T:N2], ps[:, 1, 0:T], 1.0 / KV_LORA, RMS_EPS, ALU.mult, ALU.add)\
               .then_inc(dve_done, st.one("dve", "eps"))
            dve.wait_ge(act_done, st.v("act", "root"))
            link(dve.reciprocal(row[:, 0, :], row[:, 1, :]))
            for k in range(QC):
                dve.scalar_tensor_tensor(QA[:, k, :], QA[:, k, :], col(f"qg{l}", k), row[:, 0, 0:T], ALU.mult, ALU.mult)
            for k in range(KVC):
                dve.scalar_tensor_tensor(KVA[:, k, :], KVA[:, k, :], col(f"kvg{l}", k), row[:, 0, T:N2], ALU.mult, ALU.mult)
            dve.drain().then_inc(dve_done, 1)

        def up1_pe(pe, n):
            st = enter(pe, n)
            for c in range(6):
                wt = unit_here(pe, st.u0 + c // 3)
                o = (c % 3) * QC * P
                dot(pe, ps[:, c, 0:T], [(wt[:, o + k * P:o + (k + 1) * P], QA[:, k, :]) for k in range(QC)])\
                    .then_inc(pe_done, st.one("pe", f"c{c}"))
            wt = unit_here(pe, st.u0 + 2)
            for c in range(6, 10):
                if c >= 8:
                    pe.wait_ge(act_done, st.v("act", f"c{c - 8}"))
                o = (c - 6) * KVC * P
                dot(pe, ps[:, c % 8, 0:T], [(wt[:, o + k * P:o + (k + 1) * P], KVA[:, k, :]) for k in range(KVC)])\
                    .then_inc(pe_done, st.one("pe", f"c{c}"))
            pe.wait_ge(act_done, st.v("act", "c3"))
            for t in range(TT):
                ins = dot(pe, ps[:, 2 + t, :], [(KVA[:, k, t * P:(t + 1) * P], wt[:, 1024 + k * 512:1024 + (k + 1) * 512])
                                                for k in range(KVC)])
            ins.then_inc(pe_done, st.one("pe", "rows"))
            pe.drain().then_inc(pe_done, 1)

        def up1_act(act, n):
            st = enter(act, n)
            for c in range(6):
                copy_marked(act, st, c, [(QN[:, c, :] if c < 4 else QR[:, c - 4, :], ps[:, c, 0:T])], f"c{c}")
            for c in range(4):
                b = (c + 6) % 8
                copy_marked(act, st, b, [(KNz[64 * e:64 * e + 64, c, e, :], ps[64 * e:64 * e + 64, b, 0:T]) for e in range(2)], f"c{c + 6}")
            act.wait_ge(pe_done, st.v("pe", "rows"))
            for t in range(TT):
                v4 = ps[:, 2 + t, :].rearrange("p (h e d) -> p h e d", h=H // 2, e=2)
                z4 = Vz[:, t, :, :].rearrange("p (h e) d -> p h e d", e=2)
                for e in range(2):
                    ins = act.activation(z4[:, :, e, e * VD:(e + 1) * VD], v4[:, :, e, :], ACT.Copy)
            ins.then_inc(act_done, st.one("act", "rows"))
            act.drain().then_inc(act_done, 1)

        def rope1_pe(pe, n):
            st = enter(pe, n)
            for c, src in enumerate((QR[:, 0, :], QR[:, 1, :], KR)):
                ins = pe.matmul(ps[:, c, 0:T], con("perm32"), src, start=True, stop=True)
            ins.then_inc(pe_done, st.one("pe", "swapped"))
            pe.drain().then_inc(pe_done, 1)

        def rope1_dve(dve, link, n):
            st = enter(dve, n)
            dve.wait_ge(pe_done, st.v("pe", "swapped"))
            dve.tensor_tensor(QR, QR, outer(con("cos32"), 2), ALU.mult)
            dve.tensor_tensor(KR, KR, con("cos32"), ALU.mult)
            link(dve.tensor_tensor(HM[:, 0:3, 0:T], ps[:, 0:3, 0:T], outer(con("sin32"), 3), ALU.mult))
            dve.tensor_tensor(QR, QR, HM[:, 0:2, 0:T], ALU.add)
            for j in range(4):
                r = slice(32 * j, 32 * j + 32)
                dve.tensor_tensor(KRz[r, j, :], KR[r, :], HM[r, 2, 0:T], ALU.add)
            dve.drain().then_inc(dve_done, 1)

        def index_pe(pe, n, t):
            st = enter(pe, n)
            for h in range(H):
                ins = pe.matmul(ps[:, h // 2, (h % 2) * T:(h % 2 + 1) * T], IQ[:, h // 4, t * P:(t + 1) * P], IKz[:, h % 4, :],
                                start=True, stop=True)
            ins.then_inc(pe_done, st.one("pe", "scores"))
            pe.drain().then_inc(pe_done, 1)

        def index_act(act, n):
            st = enter(act, n)
            act.wait_ge(pe_done, st.v("pe", "scores"))
            act.activation(S1, ps[:, 0:4, :].rearrange("p a b -> p (a b)"), ACT.Relu, scale=IDX_DIM ** -0.5)\
               .then_inc(act_done, st.one("act", "relu"))
            act.drain().then_inc(act_done, 1)

        def index_dve(dve, link, n, t):
            st = enter(dve, n)
            rel = S1.rearrange("p (h k) -> p h k", h=H)
            score, left = SC[:, 0, :], SC[:, 1, :]
            dve.wait_ge(act_done, st.v("act", "relu"))
            link(dve.tensor_scalar(score, rel[:, 0, :], IW[:, t, 0:1], None, ALU.mult))
            for h in range(1, H):
                link(dve.scalar_tensor_tensor(score, rel[:, h, :], IW[:, t, h:h + 1], score, ALU.mult, ALU.add))
            link(dve.tensor_tensor(left, score, con("causal", t * T, T), ALU.add))
            for r in range(KEEP // 8):
                link(dve.max(top8, left))
                link(dve.match_replace(left, top8, left, TAKEN))
            link(dve.tensor_scalar(score, left, TAKEN, None, ALU.is_equal))
            link(dve.tensor_scalar(score, score, 1.0, -NEG, ALU.subtract, ALU.mult))
            link(dve.tensor_tensor(score, score, con("causal", t * T, T), ALU.add))
            for h in range(H):
                dve.scalar_tensor_tensor(SB[:, h, :], con("dist", t * T, T), -SLOPES[h], score, ALU.mult, ALU.add)
            dve.drain().then_inc(dve_done, 1)

        def tile(t):
            return slice(t * P, (t + 1) * P)

        def mla_scores(t):
            return [[(QN[:, h // 2, tile(t)], KNz[:, h // 2, h % 2, :]), (QR[:, h // 4, tile(t)], KRz[:, h % 4, :])] for h in range(H)]

        def dsa_scores(t):
            return [[(DQ[:, h // 2, tile(t)], DKz[:, h % 2, :])] for h in range(H)]

        def pair_mix(value):
            return [[(value(h, s_), h * TT + s_) for h in (2 * p_, 2 * p_ + 1) for s_ in range(TT)] for p_ in range(4)]

        def router_pe(pe, n):
            st = enter(pe, n)
            rw = cols[:, COLS["rw"][0]:COLS["rw"][0] + DC * E_N].rearrange("p (k e) -> p k e", k=DC)
            for t in range(TT):
                ins = dot(pe, ps[:, t, 0:E_N], [(X[:, k, tile(t)], rw[:, k, :]) for k in range(DC)])
            ins.then_inc(pe_done, st.one("pe", "logits"))
            pe.wait_ge(dve_done, st.v("dve", "gates"))
            for t in range(TT):
                ins = pe.transpose(ps[:, 2, tile(t)], G128[:, t, :], ident)
            ins.then_inc(pe_done, st.one("pe", "turned"))
            pe.wait_ge(act_done, st.v("act", "turned"))
            for r in range(2):
                if r:
                    pe.wait_ge(act_done, st.v("act", "spread0"))
                for e in range(8):
                    ins = pe.matmul(ps[:, e, 0:T], selE[:, 8 * r + e, :], gT, start=True, stop=True)
                ins.then_inc(pe_done, st.one("pe", f"spread{r}"))
            pe.drain().then_inc(pe_done, 1)

        def router_act(act, n):
            st = enter(act, n)
            act.wait_ge(pe_done, st.v("pe", "logits"))
            act.activation(R[:, 0, :].rearrange("p (t e) -> p t e", t=TT), ps[:, 0:TT, 0:E_N], ACT.Exp, scale=-1.0)\
               .then_inc(act_done, st.one("act", "exp"))
            act.wait_ge(pe_done, st.v("pe", "turned"))
            act.activation(gT, ps[:, 2, 0:T], ACT.Copy).then_inc(act_done, st.one("act", "turned"))
            for r in range(2):
                act.wait_ge(pe_done, st.v("pe", f"spread{r}"))
                act.activation(gate_b[:, 8 * r:8 * r + 8, :], ps[:, :, 0:T], ACT.Copy).then_inc(act_done, st.one("act", f"spread{r}"))
            act.drain().then_inc(act_done, 1)

        def router_dve(dve, link, n):
            st = enter(dve, n)
            link(dve.memset(G128, 0.0))
            dve.tensor_copy(selE, inner(con("ident", 0, E_N), P))
            dve.wait_ge(act_done, st.v("act", "exp"))
            flat = lambda i: R[:, i, :]
            te = lambda i: R[:, i, :].rearrange("p (t e) -> p t e", t=TT)
            ge = lambda i: R[:, i, :].rearrange("p (g e) -> p g e", e=4)
            tg = lambda i: R[:, i, 0:8].rearrange("p (t g) -> p t g", t=TT)
            link(dve.tensor_scalar(flat(0), flat(0), 1.0, None, ALU.add))
            link(dve.reciprocal(flat(1), flat(0)))
            link(dve.tensor_tensor(te(2), te(1), outer(col("rbias", 0, E_N), TT), ALU.add))
            a, b, c, d = [ge(2)[:, :, i] for i in range(4)]
            m = lambda i: R[:, 3 + i, 0:8]
            dve.tensor_tensor(m(0), a, b, ALU.max)
            dve.tensor_tensor(m(1), a, b, ALU.min)
            dve.tensor_tensor(m(2), c, d, ALU.max)
            link(dve.tensor_tensor(m(3), c, d, ALU.min))
            dve.tensor_tensor(m(4), m(0), m(2), ALU.max)
            dve.tensor_tensor(m(5), m(0), m(2), ALU.min)
            link(dve.tensor_tensor(m(6), m(1), m(3), ALU.max))
            link(dve.tensor_tensor(m(5), m(5), m(6), ALU.max))
            link(dve.tensor_tensor(m(0), m(4), m(5), ALU.add))
            best = R[:, 10, 0:TT]

            def first_best(values, weights, onehot, n_):
                link(dve.tensor_reduce(best, values, AXX, ALU.max))
                link(dve.tensor_tensor(onehot, values, inner(best, n_), ALU.is_equal))
                link(dve.tensor_tensor(onehot, onehot, outer(weights, TT), ALU.mult))
                link(dve.tensor_reduce(best, onehot, AXX, ALU.max))
                link(dve.tensor_tensor(onehot, onehot, inner(best, n_), ALU.is_equal))

            first_best(tg(3), con("first4"), tg(4), 4)
            ing = R[:, 4, 0:8]
            link(dve.tensor_scalar(R[:, 5, 0:8], ing, 1.0, -NEG, ALU.subtract, ALU.mult))
            link(dve.tensor_tensor(ge(2), ge(2), inner(ing, 4), ALU.mult))
            link(dve.tensor_tensor(ge(2), ge(2), inner(R[:, 5, 0:8], 4), ALU.add))
            first_best(te(2), con("first16"), te(6), E_N)
            link(dve.scalar_tensor_tensor(flat(2), flat(6), NEG, flat(2), ALU.mult, ALU.add))
            first_best(te(2), con("first16"), te(7), E_N)
            link(dve.tensor_tensor(flat(6), flat(6), flat(7), ALU.add))
            link(dve.tensor_tensor(flat(6), flat(6), flat(1), ALU.mult))
            link(dve.tensor_reduce(best, te(6), AXX, ALU.add))
            link(dve.reciprocal(R[:, 11, 0:TT], best))
            dve.tensor_tensor(G128[:, :, 0:E_N], te(6), inner(R[:, 11, 0:TT], E_N), ALU.mult)\
               .then_inc(dve_done, st.one("dve", "gates"))
            dve.drain().then_inc(dve_done, 1)

        def ada_pe(pe, n):
            st = enter(pe, n)

            def half_mod(hm, i, free):
                if free is not None:
                    pe.wait_ge(dve_done, free)
                for j in (2 * hm, 2 * hm + 1):
                    wt = unit_here(pe, st.u0 + j, i)
                    for e in range(2):
                        c = 2 * (j % 2) + e
                        ins = dot(pe, ps[:, hm % 2, 2 * c:2 * c + 2],
                                  [(wt[:, e * D + k * P:e * D + (k + 1) * P], condT[:, k, :]) for k in range(DC)])
                    ins.then_inc(pe_done, 1)

            half_mod(0, None, None)
            half_mod(1, None, None)
            with pe.Fori(0, N_MOD - 1) as i:
                for hm in range(2):
                    half_mod(2 + hm, i, st.v("dve", hm + 1) + 2 * i)
            pe.drain().then_inc(pe_done, 1)

        def ada_dve(dve, link, n, l):
            st = enter(dve, n)
            a = COLS[f"adab{l}"][0]
            bias = cols[:, a:a + N_MOD * DC].rearrange("p (m k) -> p m k", m=N_MOD)
            with dve.Fori(0, N_MOD) as i:
                for hm in range(2):
                    dve.wait_ge(pe_done, st.v("pe", 2 * hm + 2) + 4 * i)
                    dve.tensor_tensor(MD[:, l, i, 4 * hm:4 * hm + 4, :], ps[:, hm, 0:8].rearrange("p (c b) -> p c b", b=2),
                                      inner(bias[:, i, 4 * hm:4 * hm + 4], 2), ALU.add).then_inc(dve_done, 1)
            dve.wait_ge(dve_done, st.v("dve", 2 * N_MOD))
            for m in (1, 4, 7):
                dve.tensor_scalar(MD[:, l, m, :, :], MD[:, l, m, :, :], 1.0, None, ALU.add)
            for m in (2, 8):
                dve.tensor_scalar(MD[:, l, m, :, :], MD[:, l, m, :, :], 0.5, None, ALU.mult)
            dve.drain().then_inc(dve_done, 1)

        def in2_pe(pe, n):
            st = enter(pe, n)
            for c in range(20):
                wt = unit_here(pe, st.u0 + c // 2)
                if c >= 8:
                    pe.wait_ge(act_done, st.v("act", f"c{c - 8}"))
                o = (c % 2) * D
                dot(pe, ps[:, c % 8, :], [(wt[:, o + k * P:o + (k + 1) * P], HM[:, k, :]) for k in range(DC)])\
                    .then_inc(pe_done, st.one("pe", f"c{c}"))
            wt = unit_here(pe, st.u0 + 10)
            pe.wait_ge(act_done, st.v("act", "c15"))
            for t in range(4):
                ins = dot(pe, ps[:, 4, t * 16:t * 16 + 16], [(HM[:, k, tile(t)], wt[:, k * 16:k * 16 + 16]) for k in range(DC)])
            ins.then_inc(pe_done, st.one("pe", "ab"))
            pe.wait_ge(act_done, st.v("act", "c19"))
            for u in range(2):
                wt = unit_here(pe, st.u0 + 11 + u)
                for t in range(4):
                    for k in range(4):
                        ins = pe.matmul(ps[:, t, :], HM[:, 4 * u + k, tile(t)], wt[:, k * 512:(k + 1) * 512],
                                        start=(u == 0 and k == 0), stop=(u == 1 and k == 3))
            ins.then_inc(pe_done, st.one("pe", "z"))
            pe.drain().then_inc(pe_done, 1)

        def seqs(ap):
            return ap.rearrange("p (s t) -> p s t", s=2)

        def in2_act(act, n):
            st = enter(act, n)
            for c in range(12):
                copy_marked(act, st, c % 8, [(CI[:, c, :, 2:2 + T], seqs(ps[:, c % 8, :]))], f"c{c}")
            for i in range(CCH):
                c = 12 + 2 * i
                copy_marked(act, st, c % 8, [(VAL[:, i, :], ps[:, c % 8, :])], f"c{c}")
                act.wait_ge(pe_done, st.v("pe", f"c{c + 1}"))
                if i:
                    act.wait_ge(dve_done, st.v("dve", f"g{i - 1}"))
                act.activation(SGt, ps[:, (c + 1) % 8, :], ACT.Sigmoid).then_inc(act_done, st.one("act", f"c{c + 1}"))
            copy_marked(act, st, 4, [(AB.rearrange("p a b -> p (a b)"), ps[:, 4, 0:64])], "ab")
            act.wait_ge(pe_done, st.v("pe", "z"))
            act.activation(Zr, ps[:, 0:4, :], ACT.Silu).then_inc(act_done, st.one("act", "z"))
            act.drain().then_inc(act_done, 1)

        def in2_dve(dve, n):
            st = enter(dve, n)
            hc, hl = GCONV // 2, CCONV // 2
            dve.memset(CI[:, :, :, 0:hc].rearrange("p a b c -> p (a b) c"), 0.0)
            dve.memset(CI[:, :, :, hc + T:].rearrange("p a b c -> p (a b) c"), 0.0)
            dve.memset(GL[:, :, :, 0:hl].rearrange("p a b c -> p (a b) c"), 0.0)
            dve.memset(GL[:, :, :, hl + T:].rearrange("p a b c -> p (a b) c"), 0.0)
            for i in range(CCH):
                dve.wait_ge(act_done, st.v("act", f"c{13 + 2 * i}"))
                dve.tensor_tensor(GL[:, i, :, hl:hl + T], seqs(VAL[:, i, :]), seqs(SGt), ALU.mult)\
                   .then_inc(dve_done, st.one("dve", f"g{i}"))
            dve.drain().then_inc(dve_done, 1)

        def conv_dve(dve, link, n):
            st = enter(dve, n)
            for c in range(12):
                o = seqs(QKV[:, c, :])
                link(dve.tensor_scalar(o, CI[:, c, :, 0:T], col("gconv", c * GCONV), None, ALU.mult))
                for k in range(1, GCONV):
                    ins = dve.scalar_tensor_tensor(o, CI[:, c, :, k:k + T], col("gconv", c * GCONV + k), o, ALU.mult, ALU.add)
                    if k < GCONV - 1:
                        link(ins)
                ins.then_inc(dve_done, st.one("dve", f"c{c}"))
            for c in range(CCH):
                o = seqs(CF[:, c, :])
                link(dve.tensor_scalar(o, GL[:, c, :, 0:T], col("cconv", c * CCONV), col("cbias", c), ALU.mult, ALU.add))
                for k in range(1, CCONV):
                    ins = dve.scalar_tensor_tensor(o, GL[:, c, :, k:k + T], col("cconv", c * CCONV + k), o, ALU.mult, ALU.add)
                    if k < CCONV - 1:
                        link(ins)
                if c < CCH - 1:
                    link(ins)
            ins.then_inc(dve_done, st.one("dve", "y"))
            dve.wait_ge(pe_done, st.v("pe", "mean"))
            dve.wait_ge(act_done, st.v("act", "ln"))
            dve.tensor_tensor(CF, CF, outer(row[:, 0, :], CCH), ALU.subtract).then_inc(dve_done, st.one("dve", "centred"))
            dve.wait_ge(pe_done, st.v("pe", "var"))
            dve.tensor_scalar(row[:, 0, :], ps[:, 1, :], 1.0 / (CCH * P), LN_EPS, ALU.mult, ALU.add)\
               .then_inc(dve_done, st.one("dve", "eps"))
            dve.wait_ge(act_done, st.v("act", "root"))
            link(dve.reciprocal(row[:, 0, :], row[:, 1, :]))
            dve.tensor_tensor(CF, CF, outer(row[:, 0, :], CCH), ALU.mult).then_inc(dve_done, st.one("dve", "normed"))
            dve.drain().then_inc(dve_done, 1)

        def conv_act(act, n):
            st = enter(act, n)
            for c in range(12):
                act.wait_ge(dve_done, st.v("dve", f"c{c}"))
                act.activation(QKV[:, c, :], QKV[:, c, :], ACT.Silu).then_inc(act_done, st.one("act", f"silu{c}"))
            act.wait_ge(pe_done, st.v("pe", "mean"))
            act.activation(row[:, 0, :], ps[:, 0, :], ACT.Copy, scale=1.0 / (CCH * P)).then_inc(act_done, st.one("act", "ln"))
            act.wait_ge(dve_done, st.v("dve", "centred"))
            act.activation(Y[:, 0:CCH, :], CF, ACT.Square).then_inc(act_done, st.one("act", "sq"))
            act.wait_ge(dve_done, st.v("dve", "eps"))
            act.activation(row[:, 1, :], row[:, 0, :], ACT.Sqrt).then_inc(act_done, st.one("act", "root"))
            act.wait_ge(dve_done, st.v("dve", "normed"))
            for c in range(CCH):
                act.activation(CF[:, c, :], CF[:, c, :], ACT.Silu, bias=col("clnb", c), scale=col("clng", c))
            act.drain().then_inc(act_done, 1)

        def conv_pe(pe, n):
            st = enter(pe, n)
            pe.wait_ge(dve_done, st.v("dve", "y"))
            dot(pe, ps[:, 0, :], [(ones, CF[:, c, :]) for c in range(CCH)]).then_inc(pe_done, st.one("pe", "mean"))
            pe.wait_ge(act_done, st.v("act", "sq"))
            dot(pe, ps[:, 1, :], [(ones, Y[:, c, :]) for c in range(CCH)]).then_inc(pe_done, st.one("pe", "var"))
            pe.drain().then_inc(pe_done, 1)

        def l2_pe(pe, n):
            st = enter(pe, n)
            pe.wait_ge(act_done, st.v("act", "sq"))
            for c in range(2 * GH):
                ins = pe.matmul(ps[:, c, :], ones, HM[:, c, :], start=True, stop=True)
            ins.then_inc(pe_done, st.one("pe", "sums"))
            pe.drain().then_inc(pe_done, 1)

        def l2_act(act, n):
            st = enter(act, n)
            act.activation(HM[:], QKV[:, 0:8, :], ACT.Square).then_inc(act_done, st.one("act", "sq"))
            act.wait_ge(dve_done, st.v("dve", "eps"))
            act.activation(HM[:], HM[:], ACT.Sqrt).then_inc(act_done, st.one("act", "root"))
            act.drain().then_inc(act_done, 1)

        def l2_dve(dve, link, n):
            st = enter(dve, n)
            dve.wait_ge(pe_done, st.v("pe", "sums"))
            dve.tensor_scalar(HM[:], ps[:], RMS_EPS, None, ALU.add).then_inc(dve_done, st.one("dve", "eps"))
            dve.wait_ge(act_done, st.v("act", "root"))
            link(dve.reciprocal(Y[:], HM[:]))
            link(dve.tensor_scalar(Y[:, 0:GH, :], Y[:, 0:GH, :], GD ** -0.5, None, ALU.mult))
            dve.tensor_tensor(QKV[:, 0:8, :], QKV[:, 0:8, :], Y[:], ALU.mult)
            dve.drain().then_inc(dve_done, 1)

        def rows_pe(pe, n):
            st = enter(pe, n)
            for t in range(4):
                for i, kind in enumerate("kv"):
                    b = 2 * t + i
                    for h in range(GH):
                        ins = pe.transpose(ps[:, b, h * P:(h + 1) * P], QKV[:, GH * (1 + i) + h, tile(t)], ident)
                    ins.then_inc(pe_done, st.one("pe", f"{kind}{t}"))
            pe.drain().then_inc(pe_done, 1)

        def rows_act(act, link, n):
            st = enter(act, n)
            act.activation(gp[:, 0, 32:40], col("alog", 0, 8), ACT.Exp)
            act.activation(AB[:, :, 8:16], AB[:, :, 8:16], ACT.Exp, scale=-1.0)
            act.wait_ge(dve_done, st.v("dve", "dt"))
            act.activation(gp[:, :, 16:24], gp[:, :, 8:16], ACT.Exp).then_inc(act_done, st.one("act", "exp"))
            for t in range(4):
                for i, kind in enumerate("kv"):
                    act.wait_ge(pe_done, st.v("pe", f"{kind}{t}"))
                    dst = (rowK, rowV)[i]
                    act.activation(dst[:, t, :, :].rearrange("p a b -> p (a b)"), ps[:, 2 * t + i, :], ACT.Copy)\
                       .then_inc(act_done, st.one("act", f"{kind}{t}"))
            act.drain().then_inc(act_done, 1)

        def rows_dve(dve, link, n):
            st = enter(dve, n)
            x, neg, e, m = [gp[:, :, 8 * i:8 * i + 8] for i in range(4)]
            link(dve.tensor_tensor(x, AB[:, :, 0:8], outer(col("dtb", 0, 8), 4), ALU.add))
            dve.scalar_tensor_tensor(neg, x, -1.0, x, ALU.mult, ALU.min).then_inc(dve_done, st.one("dve", "dt"))
            dve.tensor_scalar(m, x, 0.0, None, ALU.max)
            dve.memset(St, 0.0)
            dve.wait_ge(act_done, st.v("act", "exp"))
            link(dve.tensor_scalar(neg, e, 2.0, None, ALU.add))
            link(dve.reciprocal(neg, neg))
            link(dve.tensor_tensor(e, e, neg, ALU.mult))
            link(dve.tensor_tensor(x, e, e, ALU.mult))
            link(dve.tensor_scalar(neg, x, 2.0 / (2 * ATANH_TERMS + 1), None, ALU.mult))
            for i in range(ATANH_TERMS - 1, 0, -1):
                link(dve.scalar_tensor_tensor(neg, neg, 2.0 / (2 * i + 1), x, ALU.add, ALU.mult))
            link(dve.scalar_tensor_tensor(e, neg, 2.0, e, ALU.add, ALU.mult))
            link(dve.tensor_scalar(AB[:, :, 8:16], AB[:, :, 8:16], 1.0, None, ALU.add))
            dve.reciprocal(Bb, AB[:, :, 8:16])
            link(dve.tensor_tensor(Gg, m, e, ALU.add))
            dve.scalar_tensor_tensor(Gg, Gg, -1.0, outer(gp[:, 0, 32:40], 4), ALU.mult, ALU.mult)
            dve.drain().then_inc(dve_done, 1)

        ORDER = ((2, 3, 0, 1), (3, 2, 1, 0))

        def fl(ap):
            return ap.rearrange("p h k -> p (h k)")

        def scan_pe(pe, n, step):
            st = enter(pe, n)
            for d in range(2):
                t, b, m = ORDER[d][step], 4 * d, DN[d]
                tri = con(f"tri{d}")
                pe.wait_ge(dve_done, st.v("dve", f"inp.{d}"))
                for h in range(GH):
                    c = slice(h * P, (h + 1) * P)
                    kT = QKV[:, GH + h, tile(t)]
                    pe.matmul(ps[:, b, c], m["gB"][:, h, :], tri, start=True, stop=True)
                    pe.matmul(ps[:, b + 1, c], m["bB"][:, h, :], ident, start=True, stop=True)
                    ins = pe.matmul(ps[:, b + 3, c], kT, kT, start=True, stop=True)
                ins.then_inc(pe_done, st.one("pe", f"A.{d}"))
            for d in range(2):
                t, b = ORDER[d][step], 4 * d
                pe.wait_ge(dve_done, st.v("dve", f"mt.{d}"))
                for h in range(GH):
                    c = slice(h * P, (h + 1) * P)
                    qT, kT, S_h = QKV[:, h, tile(t)], QKV[:, GH + h, tile(t)], St[:, d, c]
                    pe.matmul(ps[:, b, c], kT, qT, start=True, stop=True)
                    pe.matmul(ps[:, b + 1, c], kT, S_h, start=True, stop=True)
                    ins = pe.matmul(ps[:, b + 2, c], qT, S_h, start=True, stop=True)
                ins.then_inc(pe_done, st.one("pe", f"B.{d}"))
            for j in range(LEVELS):
                for d in range(2):
                    b, m = 4 * d, DN[d]
                    pe.wait_ge(dve_done, st.v("dve", f"X{j - 1}.{d}" if j else f"mt.{d}"))
                    for h in range(GH):
                        ins = pe.matmul(ps[:, b + 3, h * P:(h + 1) * P], m[f"ET{j % 2}"][:, h, :], m["Xi"][:, h, :],
                                        start=True, stop=True)
                    ins.then_inc(pe_done, st.one("pe", f"Y{j}.{d}"))
                for d in range(2):
                    b, m = 4 * d, DN[d]
                    pe.wait_ge(act_done, st.v("act", f"Y{j}.{d}"))
                    if j == 0:
                        pe.wait_ge(dve_done, st.v("dve", f"at.{d}"))
                    for h in range(GH):
                        c = slice(h * P, (h + 1) * P)
                        if j < LEVELS - 1:
                            pe.matmul(ps[:, b, c], m["XT"][:, h, :], m["Yv"][:, h, :], start=True, stop=True)
                        ins = pe.matmul(ps[:, b + 1, c], m["Yv"][:, h, :], m["XT"][:, h, :], start=True, stop=True)
                    ins.then_inc(pe_done, st.one("pe", f"Z{j}.{d}"))
            for d in range(2):
                m = DN[d]
                pe.wait_ge(dve_done, st.v("dve", f"X{LEVELS - 1}.{d}"))
                for h in range(GH):
                    ins = pe.matmul(ps[:, 4 * d + 3, h * P:(h + 1) * P], m["XT"][:, h, :], m["R"][:, h, :], start=True, stop=True)
                ins.then_inc(pe_done, st.one("pe", f"V.{d}"))
            for d in range(2):
                b, m = 4 * d, DN[d]
                pe.wait_ge(act_done, st.v("act", f"vn.{d}"))
                for h in range(GH):
                    c = slice(h * P, (h + 1) * P)
                    pe.matmul(ps[:, b, c], m["AT"][:, h, :], m["bB"][:, h, :], start=True, stop=True)
                    ins = pe.matmul(ps[:, b + 1, c], m["gB"][:, h, :], m["bB"][:, h, :], start=True, stop=True)
                ins.then_inc(pe_done, st.one("pe", f"O.{d}"))
            pe.drain().then_inc(pe_done, 1)

        def scan_act(act, link, n):
            st = enter(act, n)
            for d in range(2):
                m = DN[d]
                act.wait_ge(dve_done, st.v("dve", f"dec.{d}"))
                act.activation(m["sm"][:, 12:24], m["sm"][:, 0:12], ACT.Exp)
                act.activation(fl(m["DEC"]), fl(m["DEC"]), ACT.Exp).then_inc(act_done, st.one("act", f"exp.{d}"))
            for d in range(2):
                m = DN[d]
                act.wait_ge(act_done, st.v("act", f"exp.{d}"))
                act.wait_ge(pe_done, st.v("pe", f"B.{d}"))
                for h in range(GH):
                    ins = act.activation(m["QS"][:, h, :], ps[:, 4 * d + 2, h * P:(h + 1) * P], ACT.Copy,
                                         scale=m["sm"][:, 12 + h:13 + h])
                ins.then_inc(act_done, st.one("act", f"qs.{d}"))
            for j in range(LEVELS):
                for d in range(2):
                    act.wait_ge(pe_done, st.v("pe", f"Y{j}.{d}"))
                    act.activation(fl(DN[d]["Yv"]), ps[:, 4 * d + 3, :], ACT.Copy).then_inc(act_done, st.one("act", f"Y{j}.{d}"))
            for d in range(2):
                act.wait_ge(pe_done, st.v("pe", f"V.{d}"))
                act.activation(fl(DN[d]["bB"]), ps[:, 4 * d + 3, :], ACT.Copy).then_inc(act_done, st.one("act", f"vn.{d}"))
            act.drain().then_inc(act_done, 1)

        def scan_dve(dve, link, n, step):
            st = enter(dve, n)
            for d in range(2):
                t, m = ORDER[d][step], DN[d]
                dve.tensor_copy(m["bB"], inner(Bb[:, t, GH * d:GH * d + GH], P))
                dve.tensor_copy(m["gB"], inner(Gg[:, t, GH * d:GH * d + GH], P)).then_inc(dve_done, st.one("dve", f"inp.{d}"))
            for d in range(2):
                t, b, m = ORDER[d][step], 4 * d, DN[d]
                sm = m["sm"]
                dve.wait_ge(pe_done, st.v("pe", f"A.{d}"))
                GC = ps[:, b, :].rearrange("p (h i) -> p h i", h=GH)
                link(dve.tensor_tensor(m["DEC"], GC, outer(ident, GH), ALU.mult))
                link(dve.tensor_reduce(sm[:, 0:4], m["DEC"], AXX, ALU.add))
                link(dve.tensor_copy(sm[:, 4:8], GC[:, :, (P - 1, 0)[d]]))
                dve.tensor_tensor(sm[:, 8:12], sm[:, 4:8], sm[:, 0:4], ALU.subtract)
                for h in range(GH):
                    ins = dve.tensor_scalar(m["DEC"][:, h, :], ps[:, b, h * P:(h + 1) * P], sm[:, h:h + 1], 0.0,
                                            ALU.subtract, ALU.min)
                ins.then_inc(dve_done, st.one("dve", f"dec.{d}"))
            for d in range(2):
                b, m = 4 * d, DN[d]
                dve.tensor_copy(m["Xi"], outer(ident, GH))
                dve.tensor_copy(m["XT"], outer(ident, GH))
                dve.wait_ge(act_done, st.v("act", f"exp.{d}"))
                link(dve.tensor_tensor(fl(m["MT"]), fl(m["DEC"]), ps[:, b + 3, :], ALU.mult))
                link(dve.tensor_tensor(fl(m["MT"]), fl(m["MT"]), ps[:, b + 1, :], ALU.mult))
                dve.tensor_tensor(m["ET0"], m["MT"], outer(con(f"lvl{d}", 0, P), GH), ALU.mult)\
                   .then_inc(dve_done, st.one("dve", f"mt.{d}"))
            for d in range(2):
                t, b, m = ORDER[d][step], 4 * d, DN[d]
                sm = m["sm"]
                link(dve.scalar_tensor_tensor(sm[:, 24:28], sm[:, 12:16], -1.0, Bb[:, t, GH * d:GH * d + GH], ALU.mult, ALU.mult))
                for h in range(GH):
                    dve.tensor_scalar(m["VB"][:, h, :], rowV[:, t, h, :], Bb[:, t, GH * d + h:GH * d + h + 1], None, ALU.mult)
                    ins = dve.tensor_scalar(m["gB"][:, h, :], rowK[:, t, h, :], sm[:, 20 + h:21 + h], None, ALU.mult)
                link(ins)
                dve.wait_ge(pe_done, st.v("pe", f"B.{d}"))
                link(dve.tensor_tensor(fl(m["AT"]), fl(m["DEC"]), ps[:, b, :], ALU.mult))
                dve.tensor_tensor(m["AT"], m["AT"], outer(con(f"tri{d}"), GH), ALU.mult)
                for h in range(GH):
                    ins = dve.scalar_tensor_tensor(m["R"][:, h, :], ps[:, b + 1, h * P:(h + 1) * P], sm[:, 24 + h:25 + h],
                                                   m["VB"][:, h, :], ALU.mult, ALU.add)
                ins.then_inc(dve_done, st.one("dve", f"at.{d}"))
            for j in range(LEVELS):
                for d in range(2):
                    b, m = 4 * d, DN[d]
                    if j < LEVELS - 1:
                        dve.tensor_tensor(m[f"ET{(j + 1) % 2}"], m["MT"], outer(con(f"lvl{d}", (j + 1) * P, P), GH), ALU.mult)
                    dve.wait_ge(pe_done, st.v("pe", f"Z{j}.{d}"))
                    if j < LEVELS - 1:
                        dve.tensor_tensor(fl(m["Xi"]), fl(m["Xi"]), ps[:, b, :], ALU.subtract)
                    dve.tensor_tensor(fl(m["XT"]), fl(m["XT"]), ps[:, b + 1, :], ALU.subtract)\
                       .then_inc(dve_done, st.one("dve", f"X{j}.{d}"))
                    dve.wait_ge(dve_done, st.v("dve", f"X{j}.{d}"))
            for d in range(2):
                t, b, m = ORDER[d][step], 4 * d, DN[d]
                dve.wait_ge(pe_done, st.v("pe", f"O.{d}"))
                dve.wait_ge(act_done, st.v("act", f"qs.{d}"))
                o = fl(OR[:, t, :, :])
                if step in (0, 2):
                    dve.tensor_tensor(o, fl(m["QS"]), ps[:, b, :], ALU.add)
                else:
                    link(dve.tensor_tensor(o, o, fl(m["QS"]), ALU.add))
                    dve.tensor_tensor(o, o, ps[:, b, :], ALU.add)
                for h in range(GH):
                    c = slice(h * P, (h + 1) * P)
                    dve.scalar_tensor_tensor(St[:, d, c], St[:, d, c], m["sm"][:, 16 + h:17 + h], ps[:, b + 1, c], ALU.mult, ALU.add)
            dve.drain().then_inc(dve_done, 1)

        def merge_act(act, n):
            st = enter(act, n)
            flat = OR.rearrange("p a b c -> p (a b c)")
            act.activation(Yf[:, 0:2048], flat, ACT.Square).then_inc(act_done, st.one("act", "sq"))
            act.wait_ge(dve_done, st.v("dve", "eps"))
            act.activation(small2[:, 16:32], small2[:, 0:16], ACT.Sqrt).then_inc(act_done, st.one("act", "root"))
            act.wait_ge(pe_done, st.v("pe", "turned"))
            act.activation(HM[:, 0:GH, :].rearrange("p a b -> p (a b)"), ps[:, 0:4, :].rearrange("p a b -> p (a b)"), ACT.Copy)
            act.drain().then_inc(act_done, 1)

        def merge_dve(dve, link, n):
            st = enter(dve, n)
            o3 = OR.rearrange("p a b c -> p (a b) c")
            dve.wait_ge(act_done, st.v("act", "sq"))
            link(dve.tensor_reduce(small2[:, 0:16], Yf[:, 0:2048].rearrange("p (a c) -> p a c", c=P), AXX, ALU.add))
            dve.tensor_scalar(small2[:, 0:16], small2[:, 0:16], 1.0 / GD, RMS_EPS, ALU.mult, ALU.add)\
               .then_inc(dve_done, st.one("dve", "eps"))
            dve.wait_ge(act_done, st.v("act", "root"))
            link(dve.reciprocal(small2[:, 0:16], small2[:, 16:32]))
            link(dve.tensor_tensor(o3, o3, inner(small2[:, 0:16], P), ALU.mult))
            link(dve.tensor_tensor(o3, o3, outer(col("outn", 0, P), 16), ALU.mult))
            dve.tensor_tensor(OR.rearrange("p a b c -> p a (b c)"), OR.rearrange("p a b c -> p a (b c)"), Zr, ALU.mult)\
               .then_inc(dve_done, st.one("dve", "ready"))
            dve.drain().then_inc(dve_done, 1)

        def merge_pe(pe, n):
            st = enter(pe, n)
            pe.wait_ge(dve_done, st.v("dve", "ready"))
            for h in range(GH):
                for t in range(4):
                    ins = pe.transpose(ps[:, h, tile(t)], OR[:, t, h, :], ident)
            ins.then_inc(pe_done, st.one("pe", "turned"))
            pe.drain().then_inc(pe_done, 1)

        def in3_pe(pe, n):
            st = enter(pe, n)
            for c in range(AH + AKV):
                wt = unit_here(pe, st.u0 + c // 2)
                if c >= 8:
                    pe.wait_ge(act_done, st.v("act", f"q{c - 8}"))
                o = (c % 2) * D
                name, m = (f"q{c}", T) if c < AH else (f"k{c - AH}", N2)
                dot(pe, ps[:, c % 8, 0:m], [(wt[:, o + k * P:o + (k + 1) * P], HM[:, k, 0:m]) for k in range(DC)])\
                    .then_inc(pe_done, st.one("pe", name))
            wt = unit_here(pe, st.u0 + 5)
            pe.wait_ge(act_done, st.v("act", "q5"))
            for t in range(4):
                ins = dot(pe, ps[:, 2 + t, 0:AKV * AD], [(HM[:, k, tile(t)], wt[:, k * 256:(k + 1) * 256]) for k in range(DC)])
            ins.then_inc(pe_done, st.one("pe", "v"))
            pe.drain().then_inc(pe_done, 1)

        def in3_act(act, n):
            st = enter(act, n)
            for c in range(AH):
                copy_marked(act, st, c, [(AQ[:, c, :], ps[:, c, 0:T])], f"q{c}")
            for c in range(AKV):
                copy_marked(act, st, c, [(AK[:, c, :], ps[:, c, :])], f"k{c}")
            copy_marked(act, st, 2, [(AV, ps[:, 2:6, 0:AKV * AD])], "v")
            act.drain().then_inc(act_done, 1)

        def rms3_pe(pe, n):
            st = enter(pe, n)
            pe.wait_ge(act_done, st.v("act", "sq"))
            for c in range(AH):
                pe.matmul(ps[:, c // 2, (c % 2) * T:(c % 2 + 1) * T], ones, SQq[:, c, :], start=True, stop=True)
            for c in range(AKV):
                ins = pe.matmul(ps[:, 4 + c, :], ones, SQk[:, c, :], start=True, stop=True)
            ins.then_inc(pe_done, st.one("pe", "sums"))
            pe.drain().then_inc(pe_done, 1)

        sq_all = area[:, AH * T + AKV * N2:2 * (AH * T + AKV * N2)]

        def rms3_act(act, n):
            st = enter(act, n)
            act.activation(sq_all, area[:, 0:AH * T + AKV * N2], ACT.Square).then_inc(act_done, st.one("act", "sq"))
            act.wait_ge(dve_done, st.v("dve", "eps"))
            act.activation(sq_all, sq_all, ACT.Sqrt).then_inc(act_done, st.one("act", "root"))
            act.drain().then_inc(act_done, 1)

        def rms3_dve(dve, link, n):
            st = enter(dve, n)
            dve.wait_ge(pe_done, st.v("pe", "sums"))
            dve.tensor_scalar(sq_all, ps[:, 0:6, :].rearrange("p a b -> p (a b)"), 1.0 / AD, RMS_EPS, ALU.mult, ALU.add)\
               .then_inc(dve_done, st.one("dve", "eps"))
            dve.wait_ge(act_done, st.v("act", "root"))
            link(dve.reciprocal(sq_all, sq_all))
            dve.scalar_tensor_tensor(AQ, AQ, col("qn"), SQq, ALU.mult, ALU.mult)
            dve.scalar_tensor_tensor(AK, AK, col("kn"), SQk, ALU.mult, ALU.mult)
            dve.drain().then_inc(dve_done, 1)

        def rope3_pe(pe, n):
            st = enter(pe, n)
            for c in range(AH):
                pe.matmul(ps[:, c // 2, (c % 2) * T:(c % 2 + 1) * T], con("permA"), AQ[:, c, :], start=True, stop=True)
            for c in range(AKV):
                ins = pe.matmul(ps[:, 4, c * T:(c + 1) * T], con("permA"), AK[:, c, 0:T], start=True, stop=True)
            ins.then_inc(pe_done, st.one("pe", "swapped"))
            pe.drain().then_inc(pe_done, 1)

        def rope3_dve(dve, link, n):
            st = enter(dve, n)
            dve.wait_ge(pe_done, st.v("pe", "swapped"))
            sw = ps[:, 0:5, :].rearrange("p a (b t) -> p (a b) t", b=2)
            prod = sq_all[:, 0:(AH + AKV) * T].rearrange("p (c t) -> p c t", t=T)
            dve.tensor_tensor(AQ, AQ, outer(con("cosA"), AH), ALU.mult)
            dve.tensor_tensor(AK[:, :, 0:T], AK[:, :, 0:T], outer(con("cosA"), AKV), ALU.mult)
            link(dve.tensor_tensor(prod, sw, outer(con("sinA"), AH + AKV), ALU.mult))
            dve.tensor_tensor(AQ, AQ, prod[:, 0:AH, :], ALU.add)
            dve.tensor_tensor(AK[:, :, 0:T], AK[:, :, 0:T], prod[:, AH:AH + AKV, :], ALU.add)
            dve.drain().then_inc(dve_done, 1)

        def gqa_scores(t, g_):
            return [[(AQ[:, 4 * g_ + h, tile(t)], AK[:, g_, :])] for h in range(4)]

        def gqa_mix(g_):
            return [[(AV[:, s_, g_ * AD:(g_ + 1) * AD], h * 4 + s_) for s_ in range(4)] for h in range(4)]

        block = ctx.enter_context(nc.Block())

        @block.sync
        def _(sp):
            sp.dma_start(X[:, :, 0:T], w["x"]).then_inc(tables_in, 16)
            sp.dma_start(X[:, :, T:N2], w["ctx"]).then_inc(tables_in, 16)
            fill_ring(sp)
            sp.wait_ge(dve_done, now["dve"])
            sp.dma_start(out, X[:, :, 0:T]).then_inc(out_done, 16)
            sp.wait_ge(out_done, 16)

        @block.scalar
        def _(act):
            link = Chain(act, act_step)
            act.dma_start(cols[:], w["cols"]).then_inc(tables_in, 16)
            act.dma_start(cons[:], w["cons"]).then_inc(tables_in, 16)
            act.wait_ge(tables_in, 64)
            link(act.activation(condT[:].rearrange("p a b -> p (a b)"), col("cond", 0, 2 * DC), ACT.Silu))
            for l in range(DEPTH):
                n = f"b1.{l}."
                in1_act(act, n + "in")
                rms1_act(act, n + "rms")
                up1_act(act, n + "up")
                idle(act, act_done, n + "rope")
                for t in range(TT):
                    index_act(act, f"{n}index{t}")
                    attention_act(act, f"{n}mla{t}", S1, PT, OT1[:, 0:4, tile(t)])
                    attention_act(act, f"{n}dsa{t}", S1, PT, OT1[:, 4:8, tile(t)])
                idle(act, act_done, n + "out")
                ln_act(act, n + "ln1", T)
                router_act(act, n + "router")
                ffn_act(act, n + "moe", T, X, m_hi)
                ln_act(act, n + "ln2", T)
            for l in range(DEPTH):
                n = f"b2.{l}."
                idle(act, act_done, n + "ada")
                ffn_act(act, n + "ffn0", N2, Y, x_hi)
                ln_act(act, n + "ln0", N2)
                idle(act, act_done, n + "mod1")
                if l == 0:
                    in2_act(act, n + "in")
                    conv_act(act, n + "conv")
                    l2_act(act, n + "l2")
                    rows_act(act, link, n + "rows")
                    for i in range(4):
                        scan_act(act, link, f"{n}scan{i}")
                    merge_act(act, n + "merge")
                else:
                    in3_act(act, n + "in")
                    rms3_act(act, n + "rms")
                    idle(act, act_done, n + "rope")
                    for t in range(TT):
                        for h in range(AKV):
                            attention_act(act, f"{n}gqa{t}{h}", S2, PT2, OT2[:, 4 * h:4 * h + 4, tile(t)])
                m = N2 if l < DEPTH - 1 else T
                idle(act, act_done, n + "out")
                ln_act(act, n + "ln1", m)
                ffn_act(act, n + "ffn1", m, Y, x_hi)
                ln_act(act, n + "ln2", m)

        @block.vector
        def _(dve):
            link = Chain(dve, dve_step)
            dve.wait_ge(tables_in, 64)
            for l in range(DEPTH):
                n = f"b1.{l}."
                in1_dve(dve, n + "in")
                rms1_dve(dve, link, n + "rms", l)
                idle(dve, dve_done, n + "up")
                rope1_dve(dve, link, n + "rope")
                for t in range(TT):
                    index_dve(dve, link, f"{n}index{t}", t)
                    attention_dve(dve, link, f"{n}mla{t}", H, S1, (NOPE + ROPE_D) ** -0.5, outer(con("causal", t * T, T), H))
                    attention_dve(dve, link, f"{n}dsa{t}", H, S1, VD ** -0.5, SB)
                add_residual(dve, link, enter(dve, n + "out"), DC, l, None, T)
                ln_dve(dve, link, n + "ln1", T, f"ln1g{l}", f"ln1b{l}")
                router_dve(dve, link, n + "router")
                ffn_dve(dve, link, n + "moe", l, T, X, m_hi, m_lo, e_hi, e_lo, None)
                ln_dve(dve, link, n + "ln2", T, f"ln2g{l}", f"ln2b{l}")
            for l in range(DEPTH):
                n = f"b2.{l}."
                ada_dve(dve, link, n + "ada", l)
                ffn_dve(dve, link, n + "ffn0", l, N2, Y, x_hi, x_lo, h_hi, h_lo, 2)
                ln_dve(dve, link, n + "ln0", N2, f"lng0{l}", f"lnb0{l}")
                modulate(dve, n + "mod1", l, 3, 4)
                if l == 0:
                    in2_dve(dve, n + "in")
                    conv_dve(dve, link, n + "conv")
                    l2_dve(dve, link, n + "l2")
                    rows_dve(dve, link, n + "rows")
                    for i in range(4):
                        scan_dve(dve, link, f"{n}scan{i}", i)
                    merge_dve(dve, link, n + "merge")
                else:
                    idle(dve, dve_done, n + "in")
                    rms3_dve(dve, link, n + "rms")
                    rope3_dve(dve, link, n + "rope")
                    for t in range(TT):
                        for h in range(AKV):
                            attention_dve(dve, link, f"{n}gqa{t}{h}", 4, S2, AD ** -0.5, None)
                m = N2 if l < DEPTH - 1 else T
                add_residual(dve, link, enter(dve, n + "out"), DC, l, 5, m)
                ln_dve(dve, link, n + "ln1", m, f"lng1{l}", f"lnb1{l}")
                ffn_dve(dve, link, n + "ffn1", l, m, Y, x_hi, x_lo, h_hi, h_lo, 8)
                ln_dve(dve, link, n + "ln2", m, f"lng2{l}", f"lnb2{l}")

        @block.tensor
        def _(pe):
            pe.wait_ge(tables_in, 64)
            pe.wait_ge(act_step, 1)
            for l in range(DEPTH):
                n = f"b1.{l}."
                in1_pe(pe, n + "in")
                rms1_pe(pe, n + "rms")
                up1_pe(pe, n + "up")
                rope1_pe(pe, n + "rope")
                for t in range(TT):
                    index_pe(pe, f"{n}index{t}", t)
                    attention_pe(pe, f"{n}mla{t}", mla_scores(t), pair_mix(lambda h, s_: Vz[:, s_, h, :]), S1, PT)
                    attention_pe(pe, f"{n}dsa{t}", dsa_scores(t), pair_mix(lambda h, s_: DVz[:, s_, h % 2, :]), S1, PT)
                out_pe(pe, n + "out", lambda k: OT1[:, k, :], T)
                ln_pe(pe, n + "ln1", T)
                router_pe(pe, n + "router")
                ffn_pe(pe, n + "moe", T, m_hi, m_lo, e_hi, e_lo)
                ln_pe(pe, n + "ln2", T)
            for l in range(DEPTH):
                n = f"b2.{l}."
                ada_pe(pe, n + "ada")
                ffn_pe(pe, n + "ffn0", N2, x_hi, x_lo, h_hi, h_lo)
                ln_pe(pe, n + "ln0", N2)
                idle(pe, pe_done, n + "mod1")
                if l == 0:
                    in2_pe(pe, n + "in")
                    conv_pe(pe, n + "conv")
                    l2_pe(pe, n + "l2")
                    rows_pe(pe, n + "rows")
                    for i in range(4):
                        scan_pe(pe, f"{n}scan{i}", i)
                    merge_pe(pe, n + "merge")
                else:
                    in3_pe(pe, n + "in")
                    rms3_pe(pe, n + "rms")
                    rope3_pe(pe, n + "rope")
                    for t in range(TT):
                        for h in range(AKV):
                            attention_pe(pe, f"{n}gqa{t}{h}", gqa_scores(t, h), gqa_mix(h), S2, PT2)
                m = N2 if l < DEPTH - 1 else T
                src = (lambda k: HM[:, k, :] if k < GH else CF[:, k - GH, :]) if l == 0 else (lambda k: OT2[:, k, :])
                out_pe(pe, n + "out", src, m)
                ln_pe(pe, n + "ln1", m)
                ffn_pe(pe, n + "ffn1", m, x_hi, x_lo, h_hi, h_lo)
                ln_pe(pe, n + "ln2", m)


def constants():
    f = np.float32
    p = np.arange(P)
    rot = np.arange(T, dtype=f)
    c = {"ident": np.eye(P), "ones": np.ones((P, P)), "perm32": np.eye(P)[p ^ 16], "permA": np.eye(P)[p ^ 1]}
    inv = f(10000.0) ** (-np.arange(16, dtype=f) / f(16))
    ang = (rot[None, :] * inv[p % 16][:, None]).astype(f)
    c["cos32"] = np.cos(ang)
    c["sin32"] = np.sin(ang) * np.where(p % 32 < 16, -1, 1)[:, None]
    inv = f(10000.0) ** (-np.arange(32, dtype=f) / f(32))
    rows_, cols_ = (np.arange(T) // 64).astype(f), (np.arange(T) % 64).astype(f)
    ang = np.concatenate([inv[:, None] * rows_, inv[:, None] * cols_]).astype(f)
    c["cosA"] = np.cos(ang)[p // 2]
    c["sinA"] = np.sin(ang)[p // 2] * np.where(p % 2 == 0, -1, 1)[:, None]
    d = (np.arange(TT)[None, :, None] * P + p[:, None, None] - np.arange(T)[None, None, :]).astype(f)
    c["dist"] = d
    c["causal"] = np.where(d >= 0, 0, NEG)
    c["first4"] = np.broadcast_to(4 - np.arange(4), (P, 4))
    c["first16"] = np.broadcast_to(E_N - np.arange(E_N), (P, E_N))
    j, i = p[:, None], p[None, :]
    for d_, late in enumerate((j < i, j > i)):
        c[f"tri{d_}"] = late | (j == i)
        c[f"lvl{d_}"] = np.stack([late & (j // (2 * b) == i // (2 * b)) & (j // b != i // b)
                                  for b in (1, 2, 4, 8, 16, 32, 64)], axis=1)
    out = np.zeros((P, NCONS), f)
    for name, (a, n) in CONS.items():
        out[:, a:a + n] = np.asarray(c[name]).astype(f).reshape(P, n)
    return out


def chunks_of(wt):
    k, n = wt.shape[0] // P, wt.shape[1] // P
    return wt.reshape(k, P, n, P).transpose(2, 1, 0, 3).reshape(n, P, k * P)


def rows_of(wt):
    k, n = wt.shape[0] // P, wt.shape[1]
    return wt.reshape(k, P, n).transpose(1, 0, 2).reshape(P, k * n)


def grouped(ch, m):
    n, _, wd = ch.shape
    return ch.reshape(n // m, m, P, wd).transpose(0, 2, 1, 3).reshape(n // m, P, m * wd)


def column(v):
    return v.reshape(-1, P).T


def spread(v):
    return np.broadcast_to(v.reshape(1, -1), (P, v.size))


def lay_out(a):
    w = {}
    w["x"] = a["x"][0].reshape(T, DC, P).transpose(2, 1, 0)
    w["ctx"] = a["ctx_2"][0].reshape(T, DC, P).transpose(2, 1, 0)
    cut = np.cumsum([Q_LORA, KV_LORA, ROPE_D, H * VD, VD, VD, H * IDX_DIM, IDX_DIM])
    w_in, rows_, qup, ukv, wo, mu, md = [], [], [], [], [], [], []
    for l in range(DEPTH):
        qa, kva, kr, dq, dk, dv, iq, ik, iw = np.split(a["w_in"][l], cut, axis=1)
        w_in.append(grouped(chunks_of(np.concatenate([qa, kva, dq, iq] + [kr] * 4 + [ik] * 4 + [dk] * 2, axis=1)), 2))
        rows_.append(rows_of(np.concatenate([iw, dv], axis=1))[None])
        q = a["w_q_up"][l].reshape(Q_LORA, H, NOPE + ROPE_D)
        q = np.concatenate([q[:, :, :NOPE].reshape(Q_LORA, -1), q[:, :, NOPE:].reshape(Q_LORA, -1)], axis=1)
        qup.append(grouped(chunks_of(q), 3))
        ukv.append(np.concatenate([grouped(chunks_of(a["w_uk"][l]), 4)[0], rows_of(a["w_uv"][l])], axis=1)[None])
        wo.append(grouped(chunks_of(a["w_o"][l]), 2))
        mu.append(np.concatenate([np.concatenate([chunks_of(a["w_gate"][l, e]) for e in range(E_N)]),
                                  np.concatenate([chunks_of(a["w_up"][l, e]) for e in range(E_N)])], axis=2))
        md.append(grouped(a["w_down"][l].reshape(MOE_CH, P, D), 2))
    w.update(w_in=np.stack(w_in), w_in_rows=np.stack(rows_), w_q_up=np.stack(qup), w_ukv=np.stack(ukv), w_o=np.stack(wo),
             moe_up=np.stack(mu), moe_down=np.stack(md))
    w["ada"] = np.stack([grouped(chunks_of(a["ada_w_2"][l]), 2) for l in range(DEPTH)])
    gu, dn = a["ffn_w_gu_2"], a["ffn_w_down_2"]
    w["ff_up"] = np.stack([np.stack([np.concatenate([chunks_of(gu[l, i][:, :DFF]), chunks_of(gu[l, i][:, DFF:])], axis=2)
                                     for i in range(2)]) for l in range(DEPTH)])
    w["ff_down"] = np.stack([np.stack([grouped(dn[l, i].reshape(FF_CH, P, D), 2) for i in range(2)]) for l in range(DEPTH)])
    qkv, z, ab, val, gate = np.split(a["even_w_in_2"][0], [3 * GH * GD, 4 * GH * GD, 4 * GH * GD + 4 * GH,
                                                            4 * GH * GD + 4 * GH + CCH * P], axis=1)
    glu = np.stack([chunks_of(val), chunks_of(gate)], axis=1).reshape(2 * CCH, P, D)
    w["even_in"] = grouped(np.concatenate([chunks_of(qkv), glu]), 2)
    w["even_ab"] = rows_of(ab)[None]
    w["even_z"] = np.stack([rows_of(z[0:D // 2]), rows_of(z[D // 2:])])
    w["even_out"] = grouped(chunks_of(a["even_w_out_2"][0]), 2)
    ai = a["attn_w_in_2"][0]
    w["attn_in"] = grouped(chunks_of(ai[:, :(AH + AKV) * AD]), 2)
    w["attn_v"] = rows_of(ai[:, (AH + AKV) * AD:])[None]
    w["attn_out"] = grouped(chunks_of(a["attn_w_out_2"][0]), 2)
    c = {}
    for l in range(DEPTH):
        c[f"qg{l}"], c[f"kvg{l}"] = column(a["q_norm_g"][l]), column(a["kv_norm_g"][l])
        for i in (1, 2):
            c[f"ln{i}g{l}"], c[f"ln{i}b{l}"] = column(a[f"ln{i}_g"][l]), column(a[f"ln{i}_b"][l])
        c[f"adab{l}"] = column(a["ada_b_2"][l])
        for i in range(3):
            c[f"lng{i}{l}"], c[f"lnb{i}{l}"] = column(a["ln_g_2"][l, i]), column(a["ln_b_2"][l, i])
    c["cond"] = np.stack([column(a["c_2"][0]), column(a["c_ctx_2"])], axis=2).reshape(P, 2 * DC)
    c["gconv"] = a["even_qkv_conv_2"][0].T.reshape(12, P, GCONV).transpose(1, 0, 2).reshape(P, -1)
    c["cconv"] = a["cf_dw_conv_2"][0].T.reshape(CCH, P, CCONV).transpose(1, 0, 2).reshape(P, -1)
    c["cbias"], c["clng"], c["clnb"] = [column(a[k][0]) for k in ("cf_dw_bias_2", "cf_ln_g_2", "cf_ln_b_2")]
    c["qn"], c["kn"] = column(a["attn_q_norm_2"][0]), column(a["attn_k_norm_2"][0])
    c["rbias"], c["alog"], c["dtb"] = spread(a["router_bias"]), spread(a["gdn_a_log_2"][0]), spread(a["gdn_dt_bias_2"][0])
    c["outn"], c["rw"] = spread(a["gdn_out_norm_2"][0]), rows_of(a["router_w"])
    w["cols"] = np.zeros((P, NCOLS), np.float32)
    for name, (at, n) in COLS.items():
        w["cols"][:, at:at + n] = c[name]
    w["cons"] = constants()
    return {k: np.ascontiguousarray(v) for k, v in w.items()}


def kernel(**inputs):
    import concourse.bacc as bacc
    from concourse.bass_utils import run_bass_kernel_spmd

    nc = bacc.Bacc("TRN2", target_bir_lowering=False, num_devices=1)
    arrays, w = {}, {}
    for name, v in lay_out({k: np.asarray(v) for k, v in inputs.items()}).items():
        arrays[f"in_{name}"] = v
        w[name] = nc.dram_tensor(f"in_{name}", v.shape, F32, kind="ExternalInput").ap()
    out = nc.dram_tensor("out_x", (P, DC, T), F32, kind="ExternalOutput").ap()
    build(nc, w, out)
    r = run_bass_kernel_spmd(nc, [arrays], core_ids=[0])
    got = np.asarray(r.results[0]["out_x"])
    return np.ascontiguousarray(got.transpose(2, 1, 0).reshape(1, T, D))
```

```python
from contextlib import ExitStack

import numpy as np

import concourse.bass as bass
from concourse import mybir

F32 = mybir.dt.float32
F32R = mybir.dt.float32r
ALU = mybir.AluOpType
ACT = mybir.ActivationFunctionType
AXX = mybir.AxisListType.X

P = 128
D = 1024
DC = D // P
T = 256
TT = T // P
N2 = 2 * T
DEPTH = 2
H = 8
Q_LORA, KV_LORA = 384, 256
NOPE, ROPE_D, VD = 64, 32, 64
QC, KVC = Q_LORA // P, KV_LORA // P
IDX_DIM = 32
KEEP = T // 4
E_N, E_F = 16, 512
MOE_CH = E_N * E_F // P
DFF = 2816
FF_CH = DFF // P
GH, GD = 4, 128
GCONV, CCONV = 5, 31
CCH = 4
AH, AKV, AD = 8, 2, 128
N_MOD = 9
LEVELS = 7
ATANH_TERMS = 8
ALPHA = (2.0 * DEPTH) ** 0.25
LN_EPS, RMS_EPS = 1e-5, 1e-6
NEG = -1.0e30
TAKEN = -3.0e38
SLOTS = 4
UNIT = 2048
HALVES = 4
MOE_SEG = 16
FF_SEGS = (12, 10)
PE_ORDER1 = "I0 I1 Q0 Q1 T0 M0 Q2 T1 M1 Q3 T2 M2 T3 M3".split()
ACT_ORDER1 = "R0 R1 E0 P0 O0 E1 E2 P1 O1 P2 O2 E3 P3 O3".split()
DVE_ORDER1 = "H0 H1 A0 s0 N0 A1 A2 N1 s1 N2 A3 N3".split()
PE_ORDER2 = "Q0 Q1 T0 Q2 M0 T1 Q3 M1 T2 M2 T3 M3".split()
ACT_ORDER2 = "E0 E1 P0 O0 E2 P1 O1 E3 P2 O2 P3 O3".split()
DVE_ORDER2 = "A0 A1 N0 A2 N1 A3 N2 N3".split()
SLOPES = [2.0 ** (-8.0 * (h + 1) / H) for h in range(H)]


def columns(parts):
    table, at = {}, 0
    for name, n in parts:
        table[name] = (at, n)
        at += n
    return table, at


PER_LAYER = (("qg", QC), ("kvg", KVC), ("ln1g", DC), ("ln1b", DC), ("ln2g", DC), ("ln2b", DC), ("adab", N_MOD * DC),
             ("lng0", DC), ("lnb0", DC), ("lng1", DC), ("lnb1", DC), ("lng2", DC), ("lnb2", DC))
COLS, NCOLS = columns([(f"{n}{layer}", c) for layer in range(DEPTH) for n, c in PER_LAYER] + [
    ("cond", 2 * DC), ("gconv", 12 * GCONV), ("cconv", CCH * CCONV), ("cbias", CCH), ("clng", CCH), ("clnb", CCH),
    ("qn", 1), ("kn", 1), ("rbias", E_N), ("alog", 2 * GH), ("dtb", 2 * GH), ("outn", GD), ("rw", DC * E_N)])
CONS, NCONS = columns([
    ("ident", P), ("ones", P), ("perm32", P), ("permA", P), ("cos32", T), ("sin32", T), ("cosA", T), ("sinA", T),
    ("causal", TT * T), ("dist", TT * T), ("first4", 4), ("first16", E_N), ("pick", 23), ("tri0", P), ("tri1", P),
    ("lvl0", LEVELS * P), ("lvl1", LEVELS * P)])


class Stage:

    def __init__(self, name, base, marks):
        self.name, self.base, self.u0 = name, dict(base), None
        self.names, self.total, self.seen = {}, {}, {"pe": 0, "act": 0, "dve": 0}
        for eng in ("pe", "act", "dve"):
            m = marks.get(eng, [])
            self.names[eng] = {} if isinstance(m, int) else {n: i + 1 for i, n in enumerate(m)}
            self.total[eng] = (m if isinstance(m, int) else len(m)) + 1

    def v(self, eng, name):
        return self.base[eng] + (name if isinstance(name, int) else self.names[eng][name])

    def one(self, eng, name):
        self.seen[eng] += 1
        assert self.names[eng][name] == self.seen[eng], (self.name, eng, name, self.seen[eng])
        return 1


class Chain:

    def __init__(self, eng, step):
        self.eng, self.step, self.n = eng, step, 0

    def __call__(self, ins):
        ins.then_inc(self.step, 1)
        self.n += 1
        self.eng.wait_ge(self.step, self.n)

    def inside(self, i, per_turn):
        c = Chain(self.eng, self.step)
        c.n = self.n + i * per_turn
        return c


def outer(ap, n):
    return ap.unsqueeze(1).broadcast_to([P, n, ap.shape[-1]])


def inner(ap, n):
    return ap.unsqueeze(2).broadcast_to([P, ap.shape[-1], n])


def build(nc, w, out):
    with ExitStack() as ctx:
        def sb(name, shape):
            return ctx.enter_context(nc.sbuf_tensor(name, shape, F32))

        def sem(name):
            return ctx.enter_context(nc.semaphore(name))

        ring = sb("ring", [P, SLOTS, UNIT])
        cols = sb("cols", [P, NCOLS])
        cons = sb("cons", [P, NCONS])
        X = sb("X", [P, DC, N2])
        Y = sb("Y", [P, DC, N2])
        MD = sb("MD", [P, DEPTH, N_MOD, DC, 2])
        condT = sb("condT", [P, DC, 2])
        row = sb("row", [P, 2, N2])
        small = sb("small", [P, 32])
        comb = sb("comb", [P, 2])
        tmp = sb("tmp", [P, 2, N2])
        def part(memory, name, shape, dt=F32R):
            return memory.enter_context(nc.sbuf_tensor(name, shape, dt))

        cond4 = part(ctx, "cond4", [P, DC, 4])
        with ExitStack() as both_:
            w_hi, w_lo = part(both_, "w_hi", [P, HALVES, D]), part(both_, "w_lo", [P, HALVES, D])
            with ExitStack() as one:
                x_hi, x_lo = part(one, "x_hi", [P, DC, N2]), part(one, "x_lo", [P, DC, N2])
                h_hi, h_lo = part(one, "h_hi", [P, FF_SEGS[0], N2]), part(one, "h_lo", [P, FF_SEGS[0], N2])
            with ExitStack() as other:
                m_hi, m_lo = part(other, "m_hi", [P, DC, T]), part(other, "m_lo", [P, DC, T])
                e_hi, e_lo = part(other, "e_hi", [P, MOE_SEG, T]), part(other, "e_lo", [P, MOE_SEG, T])
                gate_b = part(other, "gate_b", [P, E_N, T], F32)
        HM = sb("HM", [P, DC, N2])
        AREA = 24000
        area = sb("area", [P, AREA])
        ps = ctx.enter_context(nc.psum_tensor("ps", [P, 8, 512], F32))

        pe_done, act_done, dve_done = sem("pe_done"), sem("act_done"), sem("dve_done")
        act_step, dve_step = sem("act_step"), sem("dve_step")
        arrived = [sem(f"arrived{i}") for i in range(SLOTS)]
        x_in, ctx_in, tables_in, out_done = sem("x_in"), sem("ctx_in"), sem("tables_in"), sem("out_done")
        hi_done, lo_done, half_used = sem("hi_done"), sem("lo_done"), sem("half_used")
        silu_done, hid_done = sem("silu_done"), sem("hid_done")
        banks_full, banks_read = sem("banks_full"), sem("banks_read")
        xin_done, xhi_done, xlo_done = sem("xin_done"), sem("xhi_done"), sem("xlo_done")

        def col(name, i=0, n=1):
            a = COLS[name][0] + i
            return cols[:, a:a + n]

        def con(name, a=0, n=None):
            s, c = CONS[name]
            return cons[:, s + a:s + (c if n is None else a + n)]

        ident, ones = con("ident"), con("ones")

        class Space:

            def __init__(self, at=0, end=AREA, base=area):
                self.at, self.end, self.base = at, end, base

            def take(self, *shape):
                n = int(np.prod(shape))
                v = self.base[:, self.at:self.at + n]
                self.at += n
                assert self.at <= self.end, self.at
                names = "abcd"[:len(shape)]
                if len(shape) > 1:
                    v = v.rearrange(f"p ({' '.join(names)}) -> p {' '.join(names)}", **dict(zip(names, shape)))
                return v

        SQ = Space(4096).take(DC, N2)
        s = Space(8192)
        selE = s.take(E_N, P)
        G128, gT, R = s.take(TT, P), s.take(TT * P), s.take(16, 2 * E_N)
        s = Space()
        QA, KVA, DQ, IQ, KR = s.take(QC, T), s.take(KVC, T), s.take(4, T), s.take(2, T), s.take(T)
        padded_from = s.at
        IKz, DKz, KRz, KNz = s.take(4, T), s.take(2, T), s.take(4, T), s.take(4, 2, T)
        DVz, Vz = s.take(TT, 2, P), s.take(TT, H, P)
        zero_padded = area[:, padded_from:s.at]
        IW, QN, QR = s.take(TT, H), s.take(4, T), s.take(2, T)
        S1, PT1 = [s.take(2048), s.take(2048)], [s.take(16, P), s.take(16, P)]
        SC, SB, top8 = s.take(TT, 2, T), s.take(H, T), s.take(8)
        OT1 = HM[:, :, 0:T]
        s = Space()
        CI = s.take(12, 2, T + GCONV - 1)
        QKV = s.take(12, N2)
        pair_at = s.at
        GL, VAL = s.take(CCH, 2, T + CCONV - 1), s.take(CCH, N2)
        pair_end = s.at
        SGt = tmp
        Zr, AB, Gg, Bb = s.take(4, 512), s.take(4, 16), s.take(4, 8), s.take(4, 8)
        St, CF = s.take(2, GH * P), s.take(CCH, N2)
        gp = s.take(4, 40)
        small2 = small
        Yf = Y[:].rearrange("p a b -> p (a b)")
        tail_at = s.at
        s = Space()
        rowK, rowV, OR = s.take(4, GH, P), s.take(4, GH, P), s.take(4, GH, P)
        assert s.at <= 12 * 2 * (T + GCONV - 1)
        big = [Y[:].rearrange("p a b -> p (a b)"), HM[:].rearrange("p a b -> p (a b)")]
        half = (pair_end - pair_at) // 2

        def per_direction(d):
            a, b = Space(0, 4096, big[d]), Space(pair_at + d * half, pair_at + (d + 1) * half)
            names = ("gB", "bB", "DEC", "MT", "AT", "XT", "Xi", "R")
            got = {n: a.take(GH, P) for n in names}
            got.update({n: b.take(GH, P) for n in ("Yv", "QS", "ET0", "ET1")})
            got["VB"] = Space(tail_at + d * 544).take(GH, P)
            got["sm"] = Space(tail_at + d * 544 + 512).take(32)
            return got

        DN = [per_direction(0), per_direction(1)]
        s = Space()
        AQ, AK, SQq, SQk = s.take(AH, T), s.take(AKV, N2), s.take(AH, T), s.take(AKV, N2)
        AV, S2, PT2 = s.take(4, AKV * AD), [s.take(2048), s.take(2048)], [s.take(16, P), s.take(16, P)]
        OT2 = HM[:, :, 0:T]

        now = {"pe": 0, "act": 0, "dve": 0}
        stages, streams, unit_count = {}, [], [0]

        def stage(name, **marks):
            st = Stage(name, now, marks)
            for k in now:
                now[k] += st.total[k]
            stages[name] = st
            return st

        def stream(st, tensor, n, first, step, width=UNIT, split=False):
            if st.u0 is None:
                st.u0 = unit_count[0]
            if not split:
                first += st.base["pe"]
            streams.append((tensor, n, lo_done if split else pe_done, first, step, width, unit_count[0]))
            unit_count[0] += n

        def out_stage(name, tensor):
            stream(stage(name, pe=DC), tensor, DC // 2, 2, 2)
            count["b"] += DC

        def ln_stage(name):
            st = stage(name, pe=["mean", "var"], act=["mean", *[f"sq{k}" for k in range(DC)], "root"],
                       dve=[*[f"centred{k}" for k in range(DC)], "eps", *[f"scaled{k}" for k in range(DC)]])
            st.b0 = count["b"] - DC

        count = {"h": 0, "c": 0, "b": 0, "x": 0, "k": 0, "f": 0}

        def ffn_stage(name, segments, wu, wd, modulated=None):
            st = stage(name)
            st.segments, st.modulated = segments, modulated
            st.h0, st.c0, st.b0, st.x0, st.k0 = count["h"], count["c"], count["b"], count["x"], count["k"]
            st.f0 = count["f"]
            count["f"] += (DC - 1) * len(segments)
            c, h = 0, st.h0
            for m in segments:
                for tensor, n in ((wu[c:c + m], m), (wd[c // 2:(c + m) // 2], m // 2)):
                    stream(st, tensor, n, h + 2, 2, split=True)
                    h += 2 * n
                c += m
            count.update(h=h, c=st.c0 + c, b=st.b0 + DC * len(segments), x=st.x0 + DC, k=st.k0 + (DC if modulated else 0))

        def ada_stage(name, tensor):
            st = stage(name, pe=2 * N_MOD, act=2 * N_MOD, dve=2 * N_MOD)
            st.h0 = count["h"]
            stream(st, tensor, 4 * N_MOD, st.h0 + 2, 2, split=True)
            count["h"] += 8 * N_MOD

        for l in range(DEPTH):
            n = f"b1.{l}."
            st = stage(n + "in", pe=[f"c{c}" for c in range(14)] + ["rows"], act=[f"c{c}" for c in range(14)] + ["rows"], dve=["zeroed"])
            stream(st, w["w_in"][l], 7, 2, 2)
            stream(st, w["w_in_rows"][l], 1, 15, 1, DC * 72)
            stage(n + "rms", pe=["sums"], act=["sq", "root"], dve=["eps"])
            st = stage(n + "up", pe=[f"c{c}" for c in range(10)] + ["rows"], act=[f"c{c}" for c in range(10)] + ["rows"])
            stream(st, w["w_q_up"][l], 2, 3, 3, 3 * QC * P)
            stream(st, w["w_ukv"][l], 1, 11, 1)
            stage(n + "rope", pe=["swapped"])
            stage(n + "attend", pe=PE_ORDER1, act=ACT_ORDER1, dve=[x for x in DVE_ORDER1 if x[0] != "s"])
            out_stage(n + "out", w["w_o"][l])
            ln_stage(n + "ln1")
            stage(n + "router", pe=["logits", "turned", "spread0", "spread1"], act=["exp", "turned", "spread0", "spread1"], dve=["gates"])
            ffn_stage(n + "moe", (MOE_SEG,) * (MOE_CH // MOE_SEG), w["moe_up"][l], w["moe_down"][l])
            ln_stage(n + "ln2")
        for l in range(DEPTH):
            n = f"b2.{l}."
            ada_stage(n + "ada", w["ada"][l])
            ffn_stage(n + "ffn0", FF_SEGS, w["ff_up"][l, 0], w["ff_down"][l, 0], (0, 1))
            ln_stage(n + "ln0")
            stage(n + "mod1")
            if l == 0:
                order = [f"c{c}" for c in range(20)]
                st = stage(n + "in", pe=order + ["ab", "z"], act=order + ["ab"] + [f"silu{c}" for c in range(12)] + ["z"],
                           dve=["g0", "g1", "g2", "g3"] + [f"conv{c}" for c in range(12)])
                stream(st, w["even_in"], 10, 2, 2)
                stream(st, w["even_ab"], 1, 21, 1, DC * 16)
                stream(st, w["even_z"], 2, 22, 0)
                stage(n + "conv", act=["ln", "sq", "root"], pe=["mean", "var"], dve=["centred", "eps", "normed"])
                stage(n + "l2", pe=["sums"] + [f"spread{c}" for c in range(2 * GH)], act=[f"sq{c}" for c in range(2 * GH)] + ["root"],
                      dve=["eps", "inverse"])
                stage(n + "rows", pe=["k0", "v0", "k1", "v1", "k2", "v2", "k3", "v3"],
                      act=["exp", "k0", "v0", "k1", "v1", "k2", "v2", "k3", "v3"], dve=["dt"])
                for i in range(4):
                    both = lambda *names: [f"{x}.{d}" for x in names for d in range(2)]
                    lv = both("Y0") + [x for j in range(1, LEVELS) for x in both(f"Y{j}", f"Z{j}")]
                    stage(f"{n}scan{i}", pe=both("A", "B") + lv + both("V", "O"),
                          act=both("exp") + both("qs") + both(*[f"Y{j}" for j in range(1, LEVELS)]) + both("vn"),
                          dve=both("inp") + both("dec") + both("mt") + both("at") + both(*[f"X{j}" for j in range(LEVELS)]))
                stage(n + "merge", pe=["turned"], act=["sq", "root"], dve=["eps", "ready"])
            else:
                order = [f"q{c}" for c in range(AH)] + [f"k{c}" for c in range(AKV)] + ["v"]
                st = stage(n + "in", pe=order, act=order)
                stream(st, w["attn_in"], 5, 2, 2)
                stream(st, w["attn_v"], 1, 11, 1)
                stage(n + "rms", pe=["sums"] + [f"spread{b}" for b in range(6)], act=[f"sq{b}" for b in range(6)] + ["root"],
                      dve=["eps", "inverse"])
                stage(n + "rope", pe=["swapped"])
                stage(n + "attend", pe=PE_ORDER2, act=ACT_ORDER2, dve=DVE_ORDER2)
            out_stage(n + "out", w["even_out"] if l == 0 else w["attn_out"])
            ln_stage(n + "ln1")
            ffn_stage(n + "ffn1", FF_SEGS, w["ff_up"][l, 1], w["ff_down"][l, 1], (6, 7))
            ln_stage(n + "ln2")

        def enter(eng, name):
            st = stages[name]
            if st.base["pe"]:
                eng.wait_ge(pe_done, st.base["pe"])
                eng.wait_ge(act_done, st.base["act"])
                eng.wait_ge(dve_done, st.base["dve"])
            return st

        def fl(ap):
            return ap.rearrange("p h k -> p (h k)")

        def fill_ring(sp):
            released = []
            for tensor, n, done, first, step, width, u0 in streams:
                released += [(done, first + c * step) for c in range(n)]
            for tensor, n, done, first, step, width, u0 in streams:
                turns = max(0, n - SLOTS) // SLOTS
                head = SLOTS if turns > 1 else n
                if turns <= 1:
                    turns = 0

                def load(c, j, free):
                    if free is not None:
                        sp.wait_ge(*free)
                    sp.dma_start(ring[:, (u0 + j) % SLOTS, 0:width], tensor[c]).then_inc(arrived[(u0 + j) % SLOTS], 16)

                for c in range(head):
                    u = u0 + c
                    load(c, c, released[u - SLOTS] if u >= SLOTS else None)
                if turns:
                    with sp.Fori(0, turns) as i:
                        for j in range(SLOTS):
                            load(SLOTS * i + SLOTS + j, j, (done, first + j * step + SLOTS * step * i))
                for c in range(head + SLOTS * turns, n):
                    load(c, c, released[u0 + c - SLOTS])

        def unit_here(pe, u, i=None):
            value = 16 * (u // SLOTS + 1)
            pe.wait_ge(arrived[u % SLOTS], value if i is None else value + 16 * i)
            return ring[:, u % SLOTS, :]

        def dot(pe, dst, pairs):
            for n, (a, b) in enumerate(pairs):
                ins = pe.matmul(dst, a, b, start=(n == 0), stop=(n == len(pairs) - 1))
            return ins

        def three(pe, dst, hi, lo, xh, xl, start, stop):
            pe.matmul(dst, hi, xh, start=start, stop=False, skip_group_check=True)
            pe.matmul(dst, hi, xl, start=False, stop=False, skip_group_check=True)
            return pe.matmul(dst, lo, xh, start=False, stop=stop, skip_group_check=True)

        def split_hi(act, st, j, i):
            u = st.u0 + j // 2
            if j % 2 == 0:
                value = 16 * (u // SLOTS + 1)
                act.wait_ge(arrived[u % SLOTS], value if i is None else value + 16 * i)
            value = st.h0 + j - HALVES + 1
            if value > 0:
                act.wait_ge(half_used, value if i is None else value + 2 * SLOTS * i)
            act.activation(w_hi[:, j % HALVES, :], ring[:, u % SLOTS, (j % 2) * D:(j % 2 + 1) * D], ACT.Copy)\
               .then_inc(hi_done, 1)

        def split_lo(dve, st, j, i):
            u = st.u0 + j // 2
            value = st.h0 + j + 1
            dve.wait_ge(hi_done, value if i is None else value + 2 * SLOTS * i)
            dve.tensor_tensor(w_lo[:, j % HALVES, :], ring[:, u % SLOTS, (j % 2) * D:(j % 2 + 1) * D],
                              w_hi[:, j % HALVES, :].bitcast(F32), ALU.subtract).then_inc(lo_done, 1)

        def split_first(eng, split, follows, first=0, last=HALVES):
            if follows:
                for j in range(first, last):
                    split(eng, stages[follows], j, None)

        def ffn_pe(pe, name, n, xh, xl, hh, hl):
            st = enter(pe, name)

            def half(j, i):
                value = st.h0 + j + 1
                pe.wait_ge(lo_done, value if i is None else value + HALVES * i)
                return w_hi[:, j % HALVES, :], w_lo[:, j % HALVES, :]

            def up(j, c, i, free):
                if free is not None:
                    pe.wait_ge(hid_done, free)
                for e in range(2):
                    hi, lo = half(j + e, i)
                    for k in range(DC):
                        if j == e == 0:
                            pe.wait_ge(xlo_done, st.x0 + k + 1)
                        ins = three(pe, ps[:, 2 * (c % 2) + e, 0:n], hi[:, k * P:(k + 1) * P], lo[:, k * P:(k + 1) * P],
                                    xh[:, k, 0:n], xl[:, k, 0:n], k == 0, k == DC - 1)
                    ins.then_inc(half_used, 1)

            def down(j, f, i, hidden, last):
                hi, lo = half(j, i)
                for at, d in enumerate((4, 5, 6, 7, 0, 1, 2, 3) if hidden else range(DC)):
                    if hidden and d in (0, 2):
                        pe.wait_ge(hid_done, hidden - 1 + d // 2)
                    ins = three(pe, ps[:, d, 0:n], hi[:, d * P:(d + 1) * P], lo[:, d * P:(d + 1) * P],
                                hh[:, f, 0:n], hl[:, f, 0:n], bool(hidden), last)
                    if last and d < DC - 1:
                        ins.then_inc(banks_full, 1)
                ins.then_inc(half_used, 1)

            j = c = 0
            for seg, m in enumerate(st.segments):
                if seg:
                    pe.wait_ge(banks_read, st.b0 + DC * seg - 4)
                up(j, 0, None, None)
                up(j + 2, 1, None, None)
                with pe.Fori(0, m // 2 - 1) as i:
                    for e in range(2):
                        up(j + 4 + 2 * e, e, i, st.c0 + c + 1 + e + 2 * i)
                j, c = j + 2 * m, c + m
                if seg:
                    pe.wait_ge(banks_read, st.b0 + DC * seg)
                for f in range(HALVES):
                    down(j + f, f, None, st.c0 + c if f == 0 else None, False)
                turns = (m - HALVES - 1) // HALVES
                with pe.Fori(0, turns) as i:
                    for f in range(HALVES):
                        down(j + HALVES + f, HALVES * i + HALVES + f, i, None, False)
                for f in range(HALVES * (turns + 1), m):
                    down(j + f, f, None, None, f == m - 1)
                j += m
            pe.drain().then_inc(pe_done, 1)

        def steps(eng, count, body, turn, first=0):
            for s_ in range(first):
                body(s_, None)
            turns = (count - first) // turn
            if turns:
                with eng.Fori(0, turns) as i:
                    for s_ in range(turn):
                        body(first + s_, i)
            for s_ in range(first + turns * turn, count):
                body(s_, None)

        def ffn_act(act, name, n, src, xh):
            st = enter(act, name)
            total = 3 * sum(st.segments)

            split = lambda j, i: split_hi(act, st, j, i)
            for k in range(DC):
                if st.modulated:
                    act.wait_ge(xin_done, st.k0 + k + 1)
                act.activation(xh[:, k, 0:n], src[:, k, 0:n], ACT.Copy).then_inc(xhi_done, 1)
            j = c = 0
            for m in st.segments:
                def chunk(s_, i):
                    value = st.h0 + j + 2 * s_ + 1
                    act.wait_ge(half_used, value if i is None else value + 2 * SLOTS * i)
                    if c + s_ >= 2:
                        value = st.c0 + c + s_ - 1
                        act.wait_ge(hid_done, value if i is None else value + SLOTS * i)
                    act.activation(row[:, s_ % 2, 0:n], ps[:, 2 * (s_ % 2), 0:n], ACT.Silu).then_inc(silu_done, 1)
                    split(j + HALVES + 2 * s_, i)
                    split(j + HALVES + 2 * s_ + 1, i)

                steps(act, m, chunk, SLOTS, 0 if c else SLOTS)
                j, c = j + 2 * m, c + m
                ahead = m if j + m < total else m - HALVES
                steps(act, ahead, lambda s_, i: split(j + HALVES + s_, i), 2 * SLOTS)
                j += m
            act.drain().then_inc(act_done, 1)

        def ffn_dve(dve, link, name, l, n, src, xh, xl, hh, hl, gate):
            st = enter(dve, name)
            total = 3 * sum(st.segments)

            split = lambda j, i: split_lo(dve, st, j, i)

            def low(k):
                dve.wait_ge(xhi_done, st.x0 + k + 1)
                if st.modulated:
                    dve.wait_ge(xin_done, st.k0 + k + 1)
                dve.tensor_tensor(xl[:, k, 0:n], src[:, k, 0:n], xh[:, k, 0:n].bitcast(F32), ALU.subtract).then_inc(xlo_done, 1)

            for k in range(DC):
                if st.modulated:
                    shift, scale = st.modulated
                    for part_ in range(n // T):
                        c = slice(part_ * T, (part_ + 1) * T)
                        ins = dve.tensor_scalar(Y[:, k, c], X[:, k, c], MD[:, l, scale, k, part_:part_ + 1],
                                                MD[:, l, shift, k, part_:part_ + 1], ALU.mult, ALU.add)
                    ins.then_inc(xin_done, 1)
                if k:
                    low(k - 1)
            low(DC - 1)
            dve.wait_ge(xlo_done, st.x0 + DC)
            link(dve.tensor_scalar(Y[:, :, 0:n], X[:, :, 0:n], ALPHA, None, ALU.mult))
            j = c = 0
            for seg, m in enumerate(st.segments):
                links = 3 if gate is None else 2

                def chunk(s_, i):
                    split(j + HALVES + 2 * s_, i)
                    chain = link if i is None else link.inside(i, SLOTS * links)
                    if i is not None:
                        chain.n = chain.n + links * ((s_ - (0 if c else SLOTS)) % SLOTS)
                    value = st.c0 + c + s_ + 1
                    dve.wait_ge(silu_done, value if i is None else value + SLOTS * i)
                    value = st.h0 + j + 2 * s_ + 2
                    dve.wait_ge(half_used, value if i is None else value + 2 * SLOTS * i)
                    f = s_ if i is None else SLOTS * i + s_
                    t = tmp[:, s_ % 2, 0:n]
                    chain(dve.tensor_tensor(t, row[:, s_ % 2, 0:n], ps[:, 2 * (s_ % 2) + 1, 0:n], ALU.mult))
                    if gate is None:
                        e = c // 4 + s_ // 4
                        chain(dve.tensor_tensor(t, t, gate_b[:, e if i is None else e + i, :], ALU.mult))
                    chain(dve.tensor_copy(hh[:, f, 0:n], t))
                    dve.tensor_tensor(hl[:, f, 0:n], t, hh[:, f, 0:n].bitcast(F32), ALU.subtract).then_inc(hid_done, 1)
                    split(j + HALVES + 2 * s_ + 1, i)

                first = 0 if c else SLOTS
                turns = (m - first) // SLOTS
                for s_ in range(first):
                    chunk(s_, None)
                with dve.Fori(0, turns) as i:
                    for s_ in range(first, first + SLOTS):
                        chunk(s_, i)
                link.n += links * SLOTS * turns
                for s_ in range(first + SLOTS * turns, m):
                    chunk(s_, None)
                j, c = j + 2 * m, c + m
                ahead = m - 1 if j + m < total else m - HALVES
                steps(dve, ahead, lambda s_, i: split(j + HALVES + s_, i), 2 * SLOTS)
                j += m
                if seg:
                    dve.wait_ge(banks_read, st.b0 + DC * seg)
                for d in range(DC):
                    if d < DC - 1:
                        dve.wait_ge(banks_full, st.f0 + (DC - 1) * seg + d + 1)
                    else:
                        dve.wait_ge(half_used, st.h0 + j)
                    for part_ in range(n // T):
                        cc = slice(part_ * T, (part_ + 1) * T)
                        if gate is None:
                            ins = dve.tensor_tensor(Y[:, d, cc], ps[:, d, cc], Y[:, d, cc], ALU.add)
                        else:
                            ins = dve.scalar_tensor_tensor(Y[:, d, cc], ps[:, d, cc], MD[:, l, gate, d, part_:part_ + 1],
                                                           Y[:, d, cc], ALU.mult, ALU.add)
                    ins.then_inc(banks_read, 1)
                if j < total:
                    split(j + HALVES - 1, None)
            dve.drain().then_inc(dve_done, 1)

        def add_residual(dve, link, st, l, gate, n):
            link(dve.tensor_scalar(Y[:, :, 0:n], X[:, :, 0:n], ALPHA, None, ALU.mult))
            for d in range(DC):
                dve.wait_ge(pe_done, st.v("pe", d + 1))
                for part in range(n // T):
                    c = slice(part * T, (part + 1) * T)
                    if gate is None:
                        ins = dve.tensor_tensor(Y[:, d, c], ps[:, d, c], Y[:, d, c], ALU.add)
                    else:
                        ins = dve.scalar_tensor_tensor(Y[:, d, c], ps[:, d, c], MD[:, l, gate, d, part:part + 1], Y[:, d, c],
                                                       ALU.mult, ALU.add)
                ins.then_inc(banks_read, 1)
            dve.drain().then_inc(dve_done, 1)

        def out_pe(pe, name, src, n):
            st = enter(pe, name)
            for d in range(DC):
                wt = unit_here(pe, st.u0 + d // 2)
                o = (d % 2) * D
                dot(pe, ps[:, d, 0:n], [(wt[:, o + k * P:o + (k + 1) * P], src(k)) for k in range(DC)]).then_inc(pe_done, 1)
            pe.drain().then_inc(pe_done, 1)

        def ln_pe(pe, name, n):
            st = stages[name]
            for k in range(DC):
                pe.wait_ge(banks_read, st.b0 + k + 1)
                ins = pe.matmul(ps[:, 0, 0:n], ones, Y[:, k, 0:n], start=(k == 0), stop=(k == DC - 1))
            ins.then_inc(pe_done, st.one("pe", "mean"))
            for k in range(DC):
                pe.wait_ge(act_done, st.v("act", f"sq{k}"))
                ins = pe.matmul(ps[:, 1, 0:n], ones, SQ[:, k, 0:n], start=(k == 0), stop=(k == DC - 1))
            ins.then_inc(pe_done, st.one("pe", "var"))
            pe.drain().then_inc(pe_done, 1)

        def ln_act(act, name, n, g, b, follows=None):
            st = enter(act, name)
            split_first(act, split_hi, follows)
            act.wait_ge(pe_done, st.v("pe", "mean"))
            act.activation(row[:, 0, 0:n], ps[:, 0, 0:n], ACT.Copy, scale=1.0 / D).then_inc(act_done, st.one("act", "mean"))
            for k in range(DC):
                act.wait_ge(dve_done, st.v("dve", f"centred{k}"))
                act.activation(SQ[:, k, 0:n], Y[:, k, 0:n], ACT.Square).then_inc(act_done, st.one("act", f"sq{k}"))
            act.wait_ge(dve_done, st.v("dve", "eps"))
            act.activation(row[:, 1, 0:n], row[:, 0, 0:n], ACT.Sqrt).then_inc(act_done, st.one("act", "root"))
            for k in range(DC):
                act.wait_ge(dve_done, st.v("dve", f"scaled{k}"))
                act.activation(X[:, k, 0:n], Y[:, k, 0:n], ACT.Identity, scale=col(g, k), bias=col(b, k))
            act.drain().then_inc(act_done, 1)

        def ln_dve(dve, link, name, n, follows=None):
            st = enter(dve, name)
            split_first(dve, split_lo, follows, 0, 2)
            dve.wait_ge(act_done, st.v("act", "mean"))
            for k in range(DC):
                dve.tensor_tensor(Y[:, k, 0:n], Y[:, k, 0:n], row[:, 0, 0:n], ALU.subtract)\
                   .then_inc(dve_done, st.one("dve", f"centred{k}"))
            split_first(dve, split_lo, follows, 2)
            dve.wait_ge(pe_done, st.v("pe", "var"))
            dve.tensor_scalar(row[:, 0, 0:n], ps[:, 1, 0:n], 1.0 / D, LN_EPS, ALU.mult, ALU.add)\
               .then_inc(dve_done, st.one("dve", "eps"))
            dve.wait_ge(act_done, st.v("act", "root"))
            link(dve.reciprocal(row[:, 0, 0:n], row[:, 1, 0:n]))
            for k in range(DC):
                dve.tensor_tensor(Y[:, k, 0:n], Y[:, k, 0:n], row[:, 0, 0:n], ALU.mult)\
                   .then_inc(dve_done, st.one("dve", f"scaled{k}"))
            dve.drain().then_inc(dve_done, 1)

        def modulate(dve, name, l, shift, scale):
            enter(dve, name)
            for k in range(DC):
                for part in range(2):
                    c = slice(part * T, (part + 1) * T)
                    dve.tensor_scalar(HM[:, k, c], X[:, k, c], MD[:, l, scale, k, part:part + 1],
                                      MD[:, l, shift, k, part:part + 1], ALU.mult, ALU.add)
            dve.drain().then_inc(dve_done, 1)

        def idle(eng, done, name):
            enter(eng, name)
            eng.drain().then_inc(done, 1)

        def attend_pe(pe, name, order, units_, S, PT):
            st = enter(pe, name)
            flat = ps[:].rearrange("p a b -> p (a b)")
            for step in order:
                kind, u = step[0], int(step[1])
                if kind == "I":
                    for h in range(H):
                        ins = pe.matmul(flat[:, 2048 * u + h * T:2048 * u + (h + 1) * T], IQ[:, h // 4, tile(u)], IKz[:, h % 4, :],
                                        start=True, stop=True)
                elif kind == "Q":
                    scores = units_[u][0]
                    width = 2048 // len(scores)
                    if u:
                        pe.wait_ge(dve_done, st.v("dve", f"A{u - 1}"))
                    elif "R0" in st.names["act"]:
                        pe.wait_ge(act_done, st.v("act", "R0"))
                    for h, pairs in enumerate(scores):
                        ins = dot(pe, flat[:, h * width:(h + 1) * width], pairs)
                elif kind == "T":
                    pe.wait_ge(dve_done, st.v("dve", f"N{u}"))
                    if u:
                        pe.wait_ge(act_done, st.v("act", f"O{u - 1}"))
                    elif "R1" in st.names["act"]:
                        pe.wait_ge(act_done, st.v("act", "R1"))
                    for b in range(16):
                        ins = pe.transpose(flat[:, 2048 + b * P:2048 + (b + 1) * P], S[u % 2][:, b * P:(b + 1) * P], ident)
                else:
                    pe.wait_ge(act_done, st.v("act", f"P{u}"))
                    for i, terms in enumerate(units_[u][1]):
                        ins = dot(pe, ps[:, 4, i * P:(i + 1) * P], [(v, PT[u % 2][:, b, :]) for v, b in terms])
                ins.then_inc(pe_done, st.one("pe", step))
            pe.drain().then_inc(pe_done, 1)

        def less_max(u, h=0, n=1):
            return small[:, 16 + 8 * (u % 2) + h:16 + 8 * (u % 2) + h + n]

        def attend_act(act, name, order, heads, S, PT, outs):
            st = enter(act, name)
            flat = ps[:].rearrange("p a b -> p (a b)")
            for step in order:
                kind, u = step[0], int(step[1])
                if kind == "R":
                    act.wait_ge(pe_done, st.v("pe", f"I{u}"))
                    ins = act.activation(fl(PT[u]), flat[:, 2048 * u:2048 * (u + 1)], ACT.Relu, scale=IDX_DIM ** -0.5)
                elif kind == "E":
                    act.wait_ge(dve_done, st.v("dve", f"A{u}"))
                    keys = 2048 // heads
                    for h in range(heads):
                        s_h = S[u % 2][:, h * keys:(h + 1) * keys]
                        ins = act.activation(s_h, s_h, ACT.Exp, bias=less_max(u, h))
                elif kind == "P":
                    act.wait_ge(pe_done, st.v("pe", f"T{u}"))
                    if "H1" in st.names["dve"] and u < 2:
                        act.wait_ge(dve_done, st.v("dve", f"H{u}"))
                    ins = act.activation(fl(PT[u % 2]), flat[:, 2048:4096], ACT.Copy)
                else:
                    act.wait_ge(pe_done, st.v("pe", f"M{u}"))
                    ins = act.activation(outs[u], ps[:, 4, :].rearrange("p (a b) -> p a b", a=4), ACT.Copy)
                ins.then_inc(act_done, st.one("act", step))
            act.drain().then_inc(act_done, 1)

        def attend_dve(dve, link, name, order, S, heads, scales, masks):
            st = enter(dve, name)
            keys = 2048 // heads
            p3 = ps[:, 0:4, :].rearrange("p a b -> p (a b)").rearrange("p (h k) -> p h k", h=heads)
            mx, total = small[:, 0:heads], small[:, 8:8 + heads]
            for step in order:
                kind, u = step[0], int(step[1])
                if kind == "H":
                    dve.wait_ge(act_done, st.v("act", f"R{u}"))
                    head_sum(dve, link, u).then_inc(dve_done, st.one("dve", step))
                elif kind == "s":
                    dve.wait_ge(dve_done, st.v("dve", f"H{u}"))
                    select_keys(dve, link, u)
                elif kind == "A":
                    s3 = S[u % 2].rearrange("p (h k) -> p h k", h=heads)
                    dve.wait_ge(pe_done, st.v("pe", f"Q{u}"))
                    if u >= 2:
                        dve.wait_ge(pe_done, st.v("pe", f"T{u - 2}"))
                    if masks[u] is None:
                        link(dve.tensor_scalar(s3, p3, scales[u], None, ALU.mult))
                    else:
                        link(dve.scalar_tensor_tensor(s3, p3, scales[u], masks[u], ALU.mult, ALU.add))
                    link(dve.tensor_reduce(mx, s3, AXX, ALU.max))
                    dve.tensor_scalar(less_max(u, 0, heads), mx, -1.0, None, ALU.mult).then_inc(dve_done, st.one("dve", step))
                else:
                    s3 = S[u % 2].rearrange("p (h k) -> p h k", h=heads)
                    dve.wait_ge(act_done, st.v("act", f"E{u}"))
                    link(dve.tensor_reduce(total, s3, AXX, ALU.add))
                    link(dve.reciprocal(mx, total))
                    dve.tensor_tensor(s3, s3, inner(mx, keys), ALU.mult).then_inc(dve_done, st.one("dve", step))
            dve.drain().then_inc(dve_done, 1)

        def in1_pe(pe, n):
            st = enter(pe, n)
            for c in range(14):
                wt = unit_here(pe, st.u0 + c // 2)
                if c >= 8:
                    pe.wait_ge(act_done, st.v("act", f"c{c - 8}"))
                o = (c % 2) * D
                dot(pe, ps[:, c % 8, 0:T], [(wt[:, o + k * P:o + (k + 1) * P], X[:, k, 0:T]) for k in range(DC)])\
                    .then_inc(pe_done, st.one("pe", f"c{c}"))
            wt = unit_here(pe, st.u0 + 7)
            pe.wait_ge(act_done, st.v("act", "c7"))
            for t in range(TT):
                ins = dot(pe, ps[:, 6 + t, 0:72], [(X[:, k, t * P:(t + 1) * P], wt[:, k * 72:(k + 1) * 72]) for k in range(DC)])
            ins.then_inc(pe_done, st.one("pe", "rows"))
            pe.drain().then_inc(pe_done, 1)

        def copy_marked(act, st, bank, pairs, mark):
            act.wait_ge(pe_done, st.v("pe", mark))
            for dst, src in pairs:
                ins = act.activation(dst, src, ACT.Copy)
            ins.then_inc(act_done, st.one("act", mark))

        def in1_act(act, n):
            st = enter(act, n)
            plain = [QA[:, 0, :], QA[:, 1, :], QA[:, 2, :], KVA[:, 0, :], KVA[:, 1, :],
                     *[DQ[:, i, :] for i in range(4)], IQ[:, 0, :], IQ[:, 1, :], KR]
            for c, dst in enumerate(plain):
                copy_marked(act, st, c % 8, [(dst, ps[:, c % 8, 0:T])], f"c{c}")
            act.wait_ge(dve_done, st.v("dve", "zeroed"))
            copy_marked(act, st, 4, [(IKz[32 * j:32 * j + 32, j, :], ps[32 * j:32 * j + 32, 4, 0:T]) for j in range(4)], "c12")
            copy_marked(act, st, 5, [(DKz[64 * j:64 * j + 64, j, :], ps[64 * j:64 * j + 64, 5, 0:T]) for j in range(2)], "c13")
            act.wait_ge(pe_done, st.v("pe", "rows"))
            for t in range(TT):
                act.activation(IW[:, t, :], ps[:, 6 + t, 0:H], ACT.Copy, scale=H ** -0.5)
                for e in range(2):
                    ins = act.activation(DVz[:, t, e, e * VD:(e + 1) * VD], ps[:, 6 + t, H:H + VD], ACT.Copy)
            ins.then_inc(act_done, st.one("act", "rows"))
            act.drain().then_inc(act_done, 1)

        def in1_dve(dve, n):
            st = enter(dve, n)
            dve.memset(zero_padded, 0.0).then_inc(dve_done, st.one("dve", "zeroed"))
            dve.drain().then_inc(dve_done, 1)

        def rms1_pe(pe, n):
            st = enter(pe, n)
            pe.wait_ge(act_done, st.v("act", "sq"))
            dot(pe, ps[:, 0, 0:T], [(ones, HM[:, k, 0:T]) for k in range(QC)])
            dot(pe, ps[:, 1, 0:T], [(ones, HM[:, QC + k, 0:T]) for k in range(KVC)]).then_inc(pe_done, st.one("pe", "sums"))
            pe.drain().then_inc(pe_done, 1)

        def rms1_act(act, n):
            st = enter(act, n)
            act.activation(HM[:, 0:QC, 0:T], QA, ACT.Square)
            act.activation(HM[:, QC:QC + KVC, 0:T], KVA, ACT.Square).then_inc(act_done, st.one("act", "sq"))
            act.wait_ge(dve_done, st.v("dve", "eps"))
            act.activation(row[:, 1, :], row[:, 0, :], ACT.Sqrt).then_inc(act_done, st.one("act", "root"))
            act.drain().then_inc(act_done, 1)

        def rms1_dve(dve, link, n, l):
            st = enter(dve, n)
            dve.wait_ge(pe_done, st.v("pe", "sums"))
            dve.tensor_scalar(row[:, 0, 0:T], ps[:, 0, 0:T], 1.0 / Q_LORA, RMS_EPS, ALU.mult, ALU.add)
            dve.tensor_scalar(row[:, 0, T:N2], ps[:, 1, 0:T], 1.0 / KV_LORA, RMS_EPS, ALU.mult, ALU.add)\
               .then_inc(dve_done, st.one("dve", "eps"))
            dve.wait_ge(act_done, st.v("act", "root"))
            link(dve.reciprocal(row[:, 0, :], row[:, 1, :]))
            for k in range(QC):
                dve.scalar_tensor_tensor(QA[:, k, :], QA[:, k, :], col(f"qg{l}", k), row[:, 0, 0:T], ALU.mult, ALU.mult)
            for k in range(KVC):
                dve.scalar_tensor_tensor(KVA[:, k, :], KVA[:, k, :], col(f"kvg{l}", k), row[:, 0, T:N2], ALU.mult, ALU.mult)
            dve.drain().then_inc(dve_done, 1)

        def up1_pe(pe, n):
            st = enter(pe, n)
            for c in range(6):
                wt = unit_here(pe, st.u0 + c // 3)
                o = (c % 3) * QC * P
                dot(pe, ps[:, c, 0:T], [(wt[:, o + k * P:o + (k + 1) * P], QA[:, k, :]) for k in range(QC)])\
                    .then_inc(pe_done, st.one("pe", f"c{c}"))
            wt = unit_here(pe, st.u0 + 2)
            for c in range(6, 10):
                if c >= 8:
                    pe.wait_ge(act_done, st.v("act", f"c{c - 8}"))
                o = (c - 6) * KVC * P
                dot(pe, ps[:, c % 8, 0:T], [(wt[:, o + k * P:o + (k + 1) * P], KVA[:, k, :]) for k in range(KVC)])\
                    .then_inc(pe_done, st.one("pe", f"c{c}"))
            pe.wait_ge(act_done, st.v("act", "c3"))
            for t in range(TT):
                ins = dot(pe, ps[:, 2 + t, :], [(KVA[:, k, t * P:(t + 1) * P], wt[:, 1024 + k * 512:1024 + (k + 1) * 512])
                                                for k in range(KVC)])
            ins.then_inc(pe_done, st.one("pe", "rows"))
            pe.drain().then_inc(pe_done, 1)

        def up1_act(act, n):
            st = enter(act, n)
            for c in range(6):
                copy_marked(act, st, c, [(QN[:, c, :] if c < 4 else QR[:, c - 4, :], ps[:, c, 0:T])], f"c{c}")
            for c in range(4):
                b = (c + 6) % 8
                copy_marked(act, st, b, [(KNz[64 * e:64 * e + 64, c, e, :], ps[64 * e:64 * e + 64, b, 0:T]) for e in range(2)], f"c{c + 6}")
            act.wait_ge(pe_done, st.v("pe", "rows"))
            for t in range(TT):
                v4 = ps[:, 2 + t, :].rearrange("p (h e d) -> p h e d", h=H // 2, e=2)
                z4 = Vz[:, t, :, :].rearrange("p (h e) d -> p h e d", e=2)
                for e in range(2):
                    ins = act.activation(z4[:, :, e, e * VD:(e + 1) * VD], v4[:, :, e, :], ACT.Copy)
            ins.then_inc(act_done, st.one("act", "rows"))
            act.drain().then_inc(act_done, 1)

        def rope1_pe(pe, n):
            st = enter(pe, n)
            for c, src in enumerate((QR[:, 0, :], QR[:, 1, :], KR)):
                ins = pe.matmul(ps[:, c, 0:T], con("perm32"), src, start=True, stop=True)
            ins.then_inc(pe_done, st.one("pe", "swapped"))
            pe.drain().then_inc(pe_done, 1)

        def rope1_dve(dve, link, n):
            st = enter(dve, n)
            dve.wait_ge(pe_done, st.v("pe", "swapped"))
            dve.tensor_tensor(QR, QR, outer(con("cos32"), 2), ALU.mult)
            dve.tensor_tensor(KR, KR, con("cos32"), ALU.mult)
            link(dve.tensor_tensor(HM[:, 0:3, 0:T], ps[:, 0:3, 0:T], outer(con("sin32"), 3), ALU.mult))
            dve.tensor_tensor(QR, QR, HM[:, 0:2, 0:T], ALU.add)
            for j in range(4):
                r = slice(32 * j, 32 * j + 32)
                dve.tensor_tensor(KRz[r, j, :], KR[r, :], HM[r, 2, 0:T], ALU.add)
            dve.drain().then_inc(dve_done, 1)

        def head_sum(dve, link, t):
            rel = fl(PT1[t]).rearrange("p (h k) -> p h k", h=H)
            score, left = SC[:, t, 0, :], SC[:, t, 1, :]
            link(dve.tensor_scalar(score, rel[:, 0, :], IW[:, t, 0:1], None, ALU.mult))
            for h in range(1, H):
                link(dve.scalar_tensor_tensor(score, rel[:, h, :], IW[:, t, h:h + 1], score, ALU.mult, ALU.add))
            return dve.tensor_tensor(left, score, con("causal", t * T, T), ALU.add)

        def select_keys(dve, link, t):
            score, left = SC[:, t, 0, :], SC[:, t, 1, :]
            for r in range(KEEP // 8):
                link(dve.max(top8, left))
                link(dve.match_replace(left, top8, left, TAKEN))
            link(dve.tensor_scalar(score, left, TAKEN, None, ALU.is_equal))
            link(dve.tensor_scalar(score, score, 1.0, -NEG, ALU.subtract, ALU.mult))
            link(dve.tensor_tensor(score, score, con("causal", t * T, T), ALU.add))
            for h in range(H):
                ins = dve.scalar_tensor_tensor(SB[:, h, :], con("dist", t * T, T), -SLOPES[h], score, ALU.mult, ALU.add)
            link(ins)

        def tile(t):
            return slice(t * P, (t + 1) * P)

        def mla_scores(t):
            return [[(QN[:, h // 2, tile(t)], KNz[:, h // 2, h % 2, :]), (QR[:, h // 4, tile(t)], KRz[:, h % 4, :])] for h in range(H)]

        def dsa_scores(t):
            return [[(DQ[:, h // 2, tile(t)], DKz[:, h % 2, :])] for h in range(H)]

        def pair_mix(value):
            return [[(value(h, s_), h * TT + s_) for h in (2 * p_, 2 * p_ + 1) for s_ in range(TT)] for p_ in range(4)]

        def router_pe(pe, n):
            st = enter(pe, n)
            rw = cols[:, COLS["rw"][0]:COLS["rw"][0] + DC * E_N].rearrange("p (k e) -> p k e", k=DC)
            for t in range(TT):
                ins = dot(pe, ps[:, t, 0:E_N], [(X[:, k, tile(t)], rw[:, k, :]) for k in range(DC)])
            ins.then_inc(pe_done, st.one("pe", "logits"))
            pe.wait_ge(dve_done, st.v("dve", "gates"))
            for t in range(TT):
                ins = pe.transpose(ps[:, 2, tile(t)], G128[:, t, :], ident)
            ins.then_inc(pe_done, st.one("pe", "turned"))
            pe.wait_ge(act_done, st.v("act", "turned"))
            for r in range(2):
                if r:
                    pe.wait_ge(act_done, st.v("act", "spread0"))
                for e in range(8):
                    ins = pe.matmul(ps[:, e, 0:T], selE[:, 8 * r + e, :], gT, start=True, stop=True)
                ins.then_inc(pe_done, st.one("pe", f"spread{r}"))
            pe.drain().then_inc(pe_done, 1)

        def router_act(act, n):
            st = enter(act, n)
            act.wait_ge(pe_done, st.v("pe", "logits"))
            act.activation(R[:, 0, :].rearrange("p (t e) -> p t e", t=TT), ps[:, 0:TT, 0:E_N], ACT.Exp, scale=-1.0)\
               .then_inc(act_done, st.one("act", "exp"))
            act.wait_ge(pe_done, st.v("pe", "turned"))
            act.activation(gT, ps[:, 2, 0:T], ACT.Copy).then_inc(act_done, st.one("act", "turned"))
            for r in range(2):
                act.wait_ge(pe_done, st.v("pe", f"spread{r}"))
                act.activation(gate_b[:, 8 * r:8 * r + 8, :], ps[:, :, 0:T], ACT.Copy).then_inc(act_done, st.one("act", f"spread{r}"))
            act.drain().then_inc(act_done, 1)

        def router_dve(dve, link, n):
            st = enter(dve, n)
            link(dve.memset(G128, 0.0))
            dve.tensor_copy(selE, inner(con("ident", 0, E_N), P))
            dve.wait_ge(act_done, st.v("act", "exp"))
            flat = lambda i: R[:, i, :]
            te = lambda i: R[:, i, :].rearrange("p (t e) -> p t e", t=TT)
            ge = lambda i: R[:, i, :].rearrange("p (g e) -> p g e", e=4)
            tg = lambda i: R[:, i, 0:8].rearrange("p (t g) -> p t g", t=TT)
            link(dve.tensor_scalar(flat(0), flat(0), 1.0, None, ALU.add))
            link(dve.reciprocal(flat(1), flat(0)))
            link(dve.tensor_tensor(te(2), te(1), outer(col("rbias", 0, E_N), TT), ALU.add))
            a, b, c, d = [ge(2)[:, :, i] for i in range(4)]
            m = lambda i: R[:, 3 + i, 0:8]
            dve.tensor_tensor(m(0), a, b, ALU.max)
            dve.tensor_tensor(m(1), a, b, ALU.min)
            dve.tensor_tensor(m(2), c, d, ALU.max)
            link(dve.tensor_tensor(m(3), c, d, ALU.min))
            dve.tensor_tensor(m(4), m(0), m(2), ALU.max)
            dve.tensor_tensor(m(5), m(0), m(2), ALU.min)
            link(dve.tensor_tensor(m(6), m(1), m(3), ALU.max))
            link(dve.tensor_tensor(m(5), m(5), m(6), ALU.max))
            link(dve.tensor_tensor(m(0), m(4), m(5), ALU.add))
            best = R[:, 10, 0:TT]

            def first_best(values, weights, onehot, n_):
                link(dve.tensor_reduce(best, values, AXX, ALU.max))
                link(dve.tensor_tensor(onehot, values, inner(best, n_), ALU.is_equal))
                link(dve.tensor_tensor(onehot, onehot, outer(weights, TT), ALU.mult))
                link(dve.tensor_reduce(best, onehot, AXX, ALU.max))
                link(dve.tensor_tensor(onehot, onehot, inner(best, n_), ALU.is_equal))

            first_best(tg(3), con("first4"), tg(4), 4)
            ing = R[:, 4, 0:8]
            link(dve.tensor_scalar(R[:, 5, 0:8], ing, 1.0, -NEG, ALU.subtract, ALU.mult))
            link(dve.tensor_tensor(ge(2), ge(2), inner(ing, 4), ALU.mult))
            link(dve.tensor_tensor(ge(2), ge(2), inner(R[:, 5, 0:8], 4), ALU.add))
            first_best(te(2), con("first16"), te(6), E_N)
            link(dve.scalar_tensor_tensor(flat(2), flat(6), NEG, flat(2), ALU.mult, ALU.add))
            first_best(te(2), con("first16"), te(7), E_N)
            link(dve.tensor_tensor(flat(6), flat(6), flat(7), ALU.add))
            link(dve.tensor_tensor(flat(6), flat(6), flat(1), ALU.mult))
            link(dve.tensor_reduce(best, te(6), AXX, ALU.add))
            link(dve.reciprocal(R[:, 11, 0:TT], best))
            dve.tensor_tensor(G128[:, :, 0:E_N], te(6), inner(R[:, 11, 0:TT], E_N), ALU.mult)\
               .then_inc(dve_done, st.one("dve", "gates"))
            dve.drain().then_inc(dve_done, 1)

        def ada_pe(pe, n):
            st = enter(pe, n)

            def product(s_, i, free):
                if free is not None:
                    pe.wait_ge(act_done, free)
                for q in range(HALVES):
                    value = st.h0 + HALVES * s_ + q + 1
                    pe.wait_ge(lo_done, value if i is None else value + 2 * HALVES * i)
                    for k in range(2):
                        for part_ in (w_hi, w_lo):
                            ins = pe.matmul(ps[0:4, s_ % 2, :], cond4[:, 2 * q + k, :], part_[:, q, k * 512:(k + 1) * 512],
                                            start=(q == k == 0 and part_ is w_hi), stop=(q == HALVES - 1 and k == 1 and part_ is w_lo),
                                            skip_group_check=True)
                    ins.then_inc(half_used, 1)

            def turn(e, copied, free):
                pe.wait_ge(act_done, copied)
                if free is not None:
                    pe.wait_ge(dve_done, free)
                for c in range(4):
                    ins = pe.matmul(ps[:, 2 + e, 2 * c:2 * c + 2], row[0:4, e, c * P:(c + 1) * P], comb[0:4, :],
                                    start=True, stop=True)
                ins.then_inc(pe_done, 1)

            product(0, None, None)
            product(1, None, None)
            turn(0, st.v("act", 1), None)
            with pe.Fori(0, N_MOD - 1) as i:
                for e in range(2):
                    product(2 + e, i, st.v("act", 1 + e) + 2 * i)
                    turn(1 - e, st.v("act", 2 + e) + 2 * i, st.v("dve", 1) - 1 + e + 2 * i)
            turn(1, st.v("act", 2 * N_MOD), st.v("dve", 2 * N_MOD - 2))
            pe.drain().then_inc(pe_done, 1)

        def ada_act(act, n, follows):
            st = enter(act, n)

            def step(g, i):
                for q in range(HALVES):
                    split_hi(act, st, HALVES * (g + 1) + q, i)
                value = st.h0 + HALVES * (g + 1)
                act.wait_ge(half_used, value if i is None else value + 2 * HALVES * i)
                act.activation(row[0:4, g % 2, :], ps[0:4, g % 2, :], ACT.Copy).then_inc(act_done, 1)

            with act.Fori(0, N_MOD - 1) as i:
                for g in range(2):
                    step(g, i)
            step(2 * N_MOD - 2, None)
            split_first(act, split_hi, follows)
            act.wait_ge(half_used, st.h0 + HALVES * 2 * N_MOD)
            act.activation(row[0:4, 1, :], ps[0:4, 1, :], ACT.Copy).then_inc(act_done, 1)
            act.drain().then_inc(act_done, 1)

        def ada_dve(dve, link, n, l, follows):
            st = enter(dve, n)
            a = COLS[f"adab{l}"][0]
            bias = cols[:, a:a + N_MOD * DC].rearrange("p (m k) -> p m k", m=N_MOD)

            def split(g, i):
                for q in range(HALVES):
                    split_lo(dve, st, HALVES * g + q, i)

            def store(m, e, value):
                dve.wait_ge(pe_done, value)
                dve.tensor_tensor(MD[:, l, m, 4 * e:4 * e + 4, :], ps[:, 2 + e, 0:8].rearrange("p (c b) -> p c b", b=2),
                                  inner(bias[:, m, 4 * e:4 * e + 4], 2), ALU.add).then_inc(dve_done, 1)

            split(1, None)
            split(2, None)
            with dve.Fori(0, N_MOD - 2) as i:
                for e in range(2):
                    split(3 + e, i)
                    store(i, e, st.v("pe", 1 + e) + 2 * i)
            split(2 * N_MOD - 1, None)
            store(N_MOD - 2, 0, st.v("pe", 2 * N_MOD - 3))
            split_first(dve, split_lo, follows)
            store(N_MOD - 2, 1, st.v("pe", 2 * N_MOD - 2))
            store(N_MOD - 1, 0, st.v("pe", 2 * N_MOD - 1))
            store(N_MOD - 1, 1, st.v("pe", 2 * N_MOD))
            dve.wait_ge(dve_done, st.v("dve", 2 * N_MOD))
            for m in (1, 4, 7):
                dve.tensor_scalar(MD[:, l, m, :, :], MD[:, l, m, :, :], 1.0, None, ALU.add)
            for m in (2, 8):
                dve.tensor_scalar(MD[:, l, m, :, :], MD[:, l, m, :, :], 0.5, None, ALU.mult)
            dve.drain().then_inc(dve_done, 1)

        def in2_pe(pe, n):
            st = enter(pe, n)
            for c in range(20):
                wt = unit_here(pe, st.u0 + c // 2)
                if c >= 8:
                    pe.wait_ge(act_done, st.v("act", f"c{c - 8}"))
                o = (c % 2) * D
                dot(pe, ps[:, c % 8, :], [(wt[:, o + k * P:o + (k + 1) * P], HM[:, k, :]) for k in range(DC)])\
                    .then_inc(pe_done, st.one("pe", f"c{c}"))
            wt = unit_here(pe, st.u0 + 10)
            pe.wait_ge(act_done, st.v("act", "c15"))
            for t in range(4):
                ins = dot(pe, ps[:, 4, t * 16:t * 16 + 16], [(HM[:, k, tile(t)], wt[:, k * 16:k * 16 + 16]) for k in range(DC)])
            ins.then_inc(pe_done, st.one("pe", "ab"))
            pe.wait_ge(act_done, st.v("act", "c19"))
            for u in range(2):
                wt = unit_here(pe, st.u0 + 11 + u)
                for t in range(4):
                    for k in range(4):
                        ins = pe.matmul(ps[:, t, :], HM[:, 4 * u + k, tile(t)], wt[:, k * 512:(k + 1) * 512],
                                        start=(u == 0 and k == 0), stop=(u == 1 and k == 3))
            ins.then_inc(pe_done, st.one("pe", "z"))
            pe.drain().then_inc(pe_done, 1)

        def seqs(ap):
            return ap.rearrange("p (s t) -> p s t", s=2)

        def in2_act(act, n):
            st = enter(act, n)
            for i in range(CCH):
                c = 2 * i
                copy_marked(act, st, c, [(VAL[:, i, :], ps[:, c, :])], f"c{c}")
                act.wait_ge(pe_done, st.v("pe", f"c{c + 1}"))
                if i > 1:
                    act.wait_ge(dve_done, st.v("dve", f"g{i - 2}"))
                act.activation(SGt[:, i % 2, :], ps[:, c + 1, :], ACT.Sigmoid).then_inc(act_done, st.one("act", f"c{c + 1}"))
            for c in range(12):
                copy_marked(act, st, c % 8, [(CI[:, c, :, 2:2 + T], seqs(ps[:, c % 8, :]))], f"c{c + 8}")
            copy_marked(act, st, 4, [(AB.rearrange("p a b -> p (a b)"), ps[:, 4, 0:64])], "ab")
            for c in range(12):
                act.wait_ge(dve_done, st.v("dve", f"conv{c}"))
                act.activation(QKV[:, c, :], QKV[:, c, :], ACT.Silu).then_inc(act_done, st.one("act", f"silu{c}"))
            act.wait_ge(pe_done, st.v("pe", "z"))
            act.activation(Zr, ps[:, 0:4, :], ACT.Silu).then_inc(act_done, st.one("act", "z"))
            act.drain().then_inc(act_done, 1)

        def in2_dve(dve, link, n):
            st = enter(dve, n)
            hc, hl = GCONV // 2, CCONV // 2
            dve.memset(CI[:, :, :, 0:hc].rearrange("p a b c -> p (a b) c"), 0.0)
            dve.memset(CI[:, :, :, hc + T:].rearrange("p a b c -> p (a b) c"), 0.0)
            dve.memset(GL[:, :, :, 0:hl].rearrange("p a b c -> p (a b) c"), 0.0)
            dve.memset(GL[:, :, :, hl + T:].rearrange("p a b c -> p (a b) c"), 0.0)

            def glu(i):
                dve.wait_ge(act_done, st.v("act", f"c{1 + 2 * i}"))
                dve.tensor_tensor(GL[:, i, :, hl:hl + T], seqs(VAL[:, i, :]), seqs(SGt[:, i % 2, :]), ALU.mult)\
                   .then_inc(dve_done, st.one("dve", f"g{i}"))

            glu(0)
            for c in range(CCH):
                if c < CCH - 1:
                    glu(c + 1)
                dve.wait_ge(dve_done, st.v("dve", f"g{c}"))
                o = seqs(CF[:, c, :])
                link(dve.tensor_scalar(o, GL[:, c, :, 0:T], col("cconv", c * CCONV), col("cbias", c), ALU.mult, ALU.add))
                for k in range(1, CCONV):
                    link(dve.scalar_tensor_tensor(o, GL[:, c, :, k:k + T], col("cconv", c * CCONV + k), o, ALU.mult, ALU.add))
            for c in range(12):
                o = seqs(QKV[:, c, :])
                dve.wait_ge(act_done, st.v("act", f"c{c + 8}"))
                link(dve.tensor_scalar(o, CI[:, c, :, 0:T], col("gconv", c * GCONV), None, ALU.mult))
                for k in range(1, GCONV):
                    ins = dve.scalar_tensor_tensor(o, CI[:, c, :, k:k + T], col("gconv", c * GCONV + k), o, ALU.mult, ALU.add)
                    if k < GCONV - 1:
                        link(ins)
                ins.then_inc(dve_done, st.one("dve", f"conv{c}"))
            dve.drain().then_inc(dve_done, 1)

        def conv_dve(dve, link, n):
            st = enter(dve, n)
            dve.wait_ge(act_done, st.v("act", "ln"))
            dve.tensor_tensor(CF, CF, outer(row[:, 0, :], CCH), ALU.subtract).then_inc(dve_done, st.one("dve", "centred"))
            dve.wait_ge(pe_done, st.v("pe", "var"))
            dve.tensor_scalar(row[:, 0, :], ps[:, 1, :], 1.0 / (CCH * P), LN_EPS, ALU.mult, ALU.add)\
               .then_inc(dve_done, st.one("dve", "eps"))
            dve.wait_ge(act_done, st.v("act", "root"))
            link(dve.reciprocal(row[:, 0, :], row[:, 1, :]))
            dve.tensor_tensor(CF, CF, outer(row[:, 0, :], CCH), ALU.mult).then_inc(dve_done, st.one("dve", "normed"))
            dve.drain().then_inc(dve_done, 1)

        def conv_act(act, n):
            st = enter(act, n)
            act.wait_ge(pe_done, st.v("pe", "mean"))
            act.activation(row[:, 0, :], ps[:, 0, :], ACT.Copy, scale=1.0 / (CCH * P)).then_inc(act_done, st.one("act", "ln"))
            act.wait_ge(dve_done, st.v("dve", "centred"))
            act.activation(Y[:, 0:CCH, :], CF, ACT.Square).then_inc(act_done, st.one("act", "sq"))
            act.wait_ge(dve_done, st.v("dve", "eps"))
            act.activation(row[:, 1, :], row[:, 0, :], ACT.Sqrt).then_inc(act_done, st.one("act", "root"))
            act.wait_ge(dve_done, st.v("dve", "normed"))
            for c in range(CCH):
                act.activation(CF[:, c, :], CF[:, c, :], ACT.Silu, bias=col("clnb", c), scale=col("clng", c))
            act.drain().then_inc(act_done, 1)

        def conv_pe(pe, n):
            st = enter(pe, n)
            dot(pe, ps[:, 0, :], [(ones, CF[:, c, :]) for c in range(CCH)]).then_inc(pe_done, st.one("pe", "mean"))
            pe.wait_ge(act_done, st.v("act", "sq"))
            dot(pe, ps[:, 1, :], [(ones, Y[:, c, :]) for c in range(CCH)]).then_inc(pe_done, st.one("pe", "var"))
            pe.drain().then_inc(pe_done, 1)

        def pick(c, n):
            return con("pick", 11 - c, n)

        spread_c = Y[:, 0:3, :].rearrange("p a b -> p (a b)").rearrange("p (c q) -> p c q", q=P)

        def l2_pe(pe, n):
            st = enter(pe, n)
            for c in range(2 * GH):
                pe.wait_ge(act_done, st.v("act", f"sq{c}"))
                ins = pe.matmul(ps[0:2 * GH, 0, :], pick(c, 2 * GH), HM[:, c, :], start=(c == 0), stop=(c == 2 * GH - 1))
            ins.then_inc(pe_done, st.one("pe", "sums"))
            pe.wait_ge(dve_done, st.v("dve", "inverse"))
            for c in range(2 * GH):
                pe.matmul(ps[:, c, :], spread_c[0:2 * GH, c, :], row[0:2 * GH, 0, :], start=True, stop=True)\
                    .then_inc(pe_done, st.one("pe", f"spread{c}"))
            pe.drain().then_inc(pe_done, 1)

        def l2_act(act, n):
            st = enter(act, n)
            for c in range(2 * GH):
                act.activation(HM[:, c, :], QKV[:, c, :], ACT.Square).then_inc(act_done, st.one("act", f"sq{c}"))
            act.wait_ge(dve_done, st.v("dve", "eps"))
            act.activation(row[0:2 * GH, 1, :], row[0:2 * GH, 0, :], ACT.Sqrt).then_inc(act_done, st.one("act", "root"))
            act.drain().then_inc(act_done, 1)

        def l2_dve(dve, link, n):
            st = enter(dve, n)
            link(dve.tensor_copy(spread_c, inner(con("ident", 0, 12), P)))
            dve.wait_ge(pe_done, st.v("pe", "sums"))
            dve.tensor_scalar(row[0:2 * GH, 0, :], ps[0:2 * GH, 0, :], RMS_EPS, None, ALU.add).then_inc(dve_done, st.one("dve", "eps"))
            dve.wait_ge(act_done, st.v("act", "root"))
            dve.reciprocal(row[0:2 * GH, 0, :], row[0:2 * GH, 1, :]).then_inc(dve_done, st.one("dve", "inverse"))
            for c in range(2 * GH):
                dve.wait_ge(pe_done, st.v("pe", f"spread{c}"))
                if c < GH:
                    dve.scalar_tensor_tensor(QKV[:, c, :], QKV[:, c, :], GD ** -0.5, ps[:, c, :], ALU.mult, ALU.mult)
                else:
                    dve.tensor_tensor(QKV[:, c, :], QKV[:, c, :], ps[:, c, :], ALU.mult)
            dve.drain().then_inc(dve_done, 1)

        def rows_pe(pe, n):
            st = enter(pe, n)
            for t in range(4):
                for i, kind in enumerate("kv"):
                    b = 2 * t + i
                    for h in range(GH):
                        ins = pe.transpose(ps[:, b, h * P:(h + 1) * P], QKV[:, GH * (1 + i) + h, tile(t)], ident)
                    ins.then_inc(pe_done, st.one("pe", f"{kind}{t}"))
            pe.drain().then_inc(pe_done, 1)

        def rows_act(act, link, n):
            st = enter(act, n)
            act.activation(gp[:, 0, 32:40], col("alog", 0, 8), ACT.Exp)
            act.activation(AB[:, :, 8:16], AB[:, :, 8:16], ACT.Exp, scale=-1.0)
            act.wait_ge(dve_done, st.v("dve", "dt"))
            act.activation(gp[:, :, 16:24], gp[:, :, 8:16], ACT.Exp).then_inc(act_done, st.one("act", "exp"))
            for t in range(4):
                for i, kind in enumerate("kv"):
                    act.wait_ge(pe_done, st.v("pe", f"{kind}{t}"))
                    dst = (rowK, rowV)[i]
                    act.activation(dst[:, t, :, :].rearrange("p a b -> p (a b)"), ps[:, 2 * t + i, :], ACT.Copy)\
                       .then_inc(act_done, st.one("act", f"{kind}{t}"))
            act.drain().then_inc(act_done, 1)

        def rows_dve(dve, link, n):
            st = enter(dve, n)
            x, neg, e, m = [gp[:, :, 8 * i:8 * i + 8] for i in range(4)]
            link(dve.tensor_tensor(x, AB[:, :, 0:8], outer(col("dtb", 0, 8), 4), ALU.add))
            dve.scalar_tensor_tensor(neg, x, -1.0, x, ALU.mult, ALU.min).then_inc(dve_done, st.one("dve", "dt"))
            dve.tensor_scalar(m, x, 0.0, None, ALU.max)
            dve.memset(St, 0.0)
            dve.wait_ge(act_done, st.v("act", "exp"))
            link(dve.tensor_scalar(neg, e, 2.0, None, ALU.add))
            link(dve.reciprocal(neg, neg))
            link(dve.tensor_tensor(e, e, neg, ALU.mult))
            link(dve.tensor_tensor(x, e, e, ALU.mult))
            link(dve.tensor_scalar(neg, x, 2.0 / (2 * ATANH_TERMS + 1), None, ALU.mult))
            for i in range(ATANH_TERMS - 1, 0, -1):
                link(dve.scalar_tensor_tensor(neg, neg, 2.0 / (2 * i + 1), x, ALU.add, ALU.mult))
            link(dve.scalar_tensor_tensor(e, neg, 2.0, e, ALU.add, ALU.mult))
            link(dve.tensor_scalar(AB[:, :, 8:16], AB[:, :, 8:16], 1.0, None, ALU.add))
            dve.reciprocal(Bb, AB[:, :, 8:16])
            link(dve.tensor_tensor(Gg, m, e, ALU.add))
            dve.scalar_tensor_tensor(Gg, Gg, -1.0, outer(gp[:, 0, 32:40], 4), ALU.mult, ALU.mult)
            dve.drain().then_inc(dve_done, 1)

        ORDER = ((2, 3, 0, 1), (3, 2, 1, 0))

        def scan_pe(pe, n, step):
            st = enter(pe, n)
            for d in range(2):
                t, b, m = ORDER[d][step], 4 * d, DN[d]
                tri = con(f"tri{d}")
                pe.wait_ge(dve_done, st.v("dve", f"inp.{d}"))
                for h in range(GH):
                    c = slice(h * P, (h + 1) * P)
                    kT = QKV[:, GH + h, tile(t)]
                    pe.matmul(ps[:, b, c], m["gB"][:, h, :], tri, start=True, stop=True)
                    pe.matmul(ps[:, b + 1, c], m["bB"][:, h, :], ident, start=True, stop=True)
                    ins = pe.matmul(ps[:, b + 3, c], kT, kT, start=True, stop=True)
                ins.then_inc(pe_done, st.one("pe", f"A.{d}"))
            for d in range(2):
                t, b = ORDER[d][step], 4 * d
                pe.wait_ge(dve_done, st.v("dve", f"mt.{d}"))
                for h in range(GH):
                    c = slice(h * P, (h + 1) * P)
                    qT, kT, S_h = QKV[:, h, tile(t)], QKV[:, GH + h, tile(t)], St[:, d, c]
                    pe.matmul(ps[:, b, c], kT, qT, start=True, stop=True)
                    pe.matmul(ps[:, b + 1, c], kT, S_h, start=True, stop=True)
                    ins = pe.matmul(ps[:, b + 2, c], qT, S_h, start=True, stop=True)
                ins.then_inc(pe_done, st.one("pe", f"B.{d}"))
            for j in range(LEVELS):
                for d in range(2):
                    b, m = 4 * d, DN[d]
                    pe.wait_ge(dve_done, st.v("dve", f"X{j - 1}.{d}" if j else f"mt.{d}"))
                    for h in range(GH):
                        ins = pe.matmul(ps[:, b + 3, h * P:(h + 1) * P], m[f"ET{j % 2}"][:, h, :], m["Xi"][:, h, :] if j else ident,
                                        start=True, stop=True)
                    ins.then_inc(pe_done, st.one("pe", f"Y{j}.{d}"))
                for d in range(2 if j else 0):
                    b, m = 4 * d, DN[d]
                    pe.wait_ge(act_done, st.v("act", f"Y{j}.{d}"))
                    if j == 1:
                        pe.wait_ge(dve_done, st.v("dve", f"at.{d}"))
                    for h in range(GH):
                        c = slice(h * P, (h + 1) * P)
                        if j < LEVELS - 1:
                            pe.matmul(ps[:, b, c], m["XT"][:, h, :], m["Yv"][:, h, :], start=True, stop=True)
                        ins = pe.matmul(ps[:, b + 1, c], m["Yv"][:, h, :], m["XT"][:, h, :], start=True, stop=True)
                    ins.then_inc(pe_done, st.one("pe", f"Z{j}.{d}"))
            for d in range(2):
                m = DN[d]
                pe.wait_ge(dve_done, st.v("dve", f"X{LEVELS - 1}.{d}"))
                for h in range(GH):
                    ins = pe.matmul(ps[:, 4 * d + 3, h * P:(h + 1) * P], m["XT"][:, h, :], m["R"][:, h, :], start=True, stop=True)
                ins.then_inc(pe_done, st.one("pe", f"V.{d}"))
            for d in range(2):
                b, m = 4 * d, DN[d]
                pe.wait_ge(act_done, st.v("act", f"vn.{d}"))
                for h in range(GH):
                    c = slice(h * P, (h + 1) * P)
                    pe.matmul(ps[:, b, c], m["AT"][:, h, :], m["bB"][:, h, :], start=True, stop=True)
                    ins = pe.matmul(ps[:, b + 1, c], m["gB"][:, h, :], m["bB"][:, h, :], start=True, stop=True)
                ins.then_inc(pe_done, st.one("pe", f"O.{d}"))
            pe.drain().then_inc(pe_done, 1)

        def scan_act(act, link, n):
            st = enter(act, n)
            for d in range(2):
                m = DN[d]
                act.wait_ge(dve_done, st.v("dve", f"dec.{d}"))
                act.activation(m["sm"][:, 12:24], m["sm"][:, 0:12], ACT.Exp)
                act.activation(fl(m["DEC"]), fl(m["DEC"]), ACT.Exp).then_inc(act_done, st.one("act", f"exp.{d}"))
            for d in range(2):
                m = DN[d]
                act.wait_ge(act_done, st.v("act", f"exp.{d}"))
                act.wait_ge(pe_done, st.v("pe", f"B.{d}"))
                for h in range(GH):
                    ins = act.activation(m["QS"][:, h, :], ps[:, 4 * d + 2, h * P:(h + 1) * P], ACT.Copy,
                                         scale=m["sm"][:, 12 + h:13 + h])
                ins.then_inc(act_done, st.one("act", f"qs.{d}"))
            for j in range(1, LEVELS):
                for d in range(2):
                    act.wait_ge(pe_done, st.v("pe", f"Y{j}.{d}"))
                    act.activation(fl(DN[d]["Yv"]), ps[:, 4 * d + 3, :], ACT.Copy).then_inc(act_done, st.one("act", f"Y{j}.{d}"))
            for d in range(2):
                act.wait_ge(pe_done, st.v("pe", f"V.{d}"))
                act.activation(fl(DN[d]["bB"]), ps[:, 4 * d + 3, :], ACT.Copy).then_inc(act_done, st.one("act", f"vn.{d}"))
            act.drain().then_inc(act_done, 1)

        def scan_dve(dve, link, n, step):
            st = enter(dve, n)
            for d in range(2):
                t, m = ORDER[d][step], DN[d]
                dve.tensor_copy(m["bB"], inner(Bb[:, t, GH * d:GH * d + GH], P))
                dve.tensor_copy(m["gB"], inner(Gg[:, t, GH * d:GH * d + GH], P)).then_inc(dve_done, st.one("dve", f"inp.{d}"))
            for d in range(2):
                t, b, m = ORDER[d][step], 4 * d, DN[d]
                sm = m["sm"]
                dve.wait_ge(pe_done, st.v("pe", f"A.{d}"))
                GC = ps[:, b, :].rearrange("p (h i) -> p h i", h=GH)
                link(dve.tensor_tensor(m["DEC"], GC, outer(ident, GH), ALU.mult))
                link(dve.tensor_reduce(sm[:, 0:4], m["DEC"], AXX, ALU.add))
                link(dve.tensor_copy(sm[:, 4:8], GC[:, :, (P - 1, 0)[d]]))
                dve.tensor_tensor(sm[:, 8:12], sm[:, 4:8], sm[:, 0:4], ALU.subtract)
                for h in range(GH):
                    ins = dve.tensor_scalar(m["DEC"][:, h, :], ps[:, b, h * P:(h + 1) * P], sm[:, h:h + 1], 0.0,
                                            ALU.subtract, ALU.min)
                ins.then_inc(dve_done, st.one("dve", f"dec.{d}"))
            for d in range(2):
                b, m = 4 * d, DN[d]
                dve.wait_ge(act_done, st.v("act", f"exp.{d}"))
                link(dve.tensor_tensor(fl(m["MT"]), fl(m["DEC"]), ps[:, b + 3, :], ALU.mult))
                link(dve.tensor_tensor(fl(m["MT"]), fl(m["MT"]), ps[:, b + 1, :], ALU.mult))
                dve.tensor_tensor(m["ET0"], m["MT"], outer(con(f"lvl{d}", 0, P), GH), ALU.mult)\
                   .then_inc(dve_done, st.one("dve", f"mt.{d}"))
            for d in range(2):
                t, b, m = ORDER[d][step], 4 * d, DN[d]
                sm = m["sm"]
                link(dve.scalar_tensor_tensor(sm[:, 24:28], sm[:, 12:16], -1.0, Bb[:, t, GH * d:GH * d + GH], ALU.mult, ALU.mult))
                for h in range(GH):
                    dve.tensor_scalar(m["VB"][:, h, :], rowV[:, t, h, :], Bb[:, t, GH * d + h:GH * d + h + 1], None, ALU.mult)
                    ins = dve.tensor_scalar(m["gB"][:, h, :], rowK[:, t, h, :], sm[:, 20 + h:21 + h], None, ALU.mult)
                link(ins)
                dve.wait_ge(pe_done, st.v("pe", f"B.{d}"))
                link(dve.tensor_tensor(fl(m["AT"]), fl(m["DEC"]), ps[:, b, :], ALU.mult))
                dve.tensor_tensor(m["AT"], m["AT"], outer(con(f"tri{d}"), GH), ALU.mult)
                for h in range(GH):
                    ins = dve.scalar_tensor_tensor(m["R"][:, h, :], ps[:, b + 1, h * P:(h + 1) * P], sm[:, 24 + h:25 + h],
                                                   m["VB"][:, h, :], ALU.mult, ALU.add)
                ins.then_inc(dve_done, st.one("dve", f"at.{d}"))
            for j in range(LEVELS):
                for d in range(2):
                    b, m = 4 * d, DN[d]
                    if j < LEVELS - 1:
                        dve.tensor_tensor(m[f"ET{(j + 1) % 2}"], m["MT"], outer(con(f"lvl{d}", (j + 1) * P, P), GH), ALU.mult)
                    if j == 0:
                        dve.tensor_tensor(m["XT"], outer(ident, GH), m["ET0"], ALU.subtract)
                        dve.wait_ge(pe_done, st.v("pe", f"Y0.{d}"))
                        dve.tensor_tensor(m["Xi"], outer(ident, GH), ps[:, b + 3, :].rearrange("p (h i) -> p h i", h=GH),
                                          ALU.subtract).then_inc(dve_done, st.one("dve", f"X0.{d}"))
                        dve.wait_ge(dve_done, st.v("dve", f"X0.{d}"))
                        continue
                    dve.wait_ge(pe_done, st.v("pe", f"Z{j}.{d}"))
                    if j < LEVELS - 1:
                        dve.tensor_tensor(fl(m["Xi"]), fl(m["Xi"]), ps[:, b, :], ALU.subtract)
                    dve.tensor_tensor(fl(m["XT"]), fl(m["XT"]), ps[:, b + 1, :], ALU.subtract)\
                       .then_inc(dve_done, st.one("dve", f"X{j}.{d}"))
                    dve.wait_ge(dve_done, st.v("dve", f"X{j}.{d}"))
            for d in range(2):
                t, b, m = ORDER[d][step], 4 * d, DN[d]
                dve.wait_ge(pe_done, st.v("pe", f"O.{d}"))
                dve.wait_ge(act_done, st.v("act", f"qs.{d}"))
                o = fl(OR[:, t, :, :])
                if step in (0, 2):
                    dve.tensor_tensor(o, fl(m["QS"]), ps[:, b, :], ALU.add)
                else:
                    link(dve.tensor_tensor(o, o, fl(m["QS"]), ALU.add))
                    dve.tensor_tensor(o, o, ps[:, b, :], ALU.add)
                for h in range(GH):
                    c = slice(h * P, (h + 1) * P)
                    dve.scalar_tensor_tensor(St[:, d, c], St[:, d, c], m["sm"][:, 16 + h:17 + h], ps[:, b + 1, c], ALU.mult, ALU.add)
            dve.drain().then_inc(dve_done, 1)

        def merge_act(act, n):
            st = enter(act, n)
            flat = OR.rearrange("p a b c -> p (a b c)")
            act.activation(Yf[:, 0:2048], flat, ACT.Square).then_inc(act_done, st.one("act", "sq"))
            act.wait_ge(dve_done, st.v("dve", "eps"))
            act.activation(small2[:, 16:32], small2[:, 0:16], ACT.Sqrt).then_inc(act_done, st.one("act", "root"))
            act.wait_ge(pe_done, st.v("pe", "turned"))
            act.activation(HM[:, 0:GH, :].rearrange("p a b -> p (a b)"), ps[:, 0:4, :].rearrange("p a b -> p (a b)"), ACT.Copy)
            act.drain().then_inc(act_done, 1)

        def merge_dve(dve, link, n):
            st = enter(dve, n)
            o3 = OR.rearrange("p a b c -> p (a b) c")
            dve.wait_ge(act_done, st.v("act", "sq"))
            link(dve.tensor_reduce(small2[:, 0:16], Yf[:, 0:2048].rearrange("p (a c) -> p a c", c=P), AXX, ALU.add))
            dve.tensor_scalar(small2[:, 0:16], small2[:, 0:16], 1.0 / GD, RMS_EPS, ALU.mult, ALU.add)\
               .then_inc(dve_done, st.one("dve", "eps"))
            dve.wait_ge(act_done, st.v("act", "root"))
            link(dve.reciprocal(small2[:, 0:16], small2[:, 16:32]))
            link(dve.tensor_tensor(o3, o3, inner(small2[:, 0:16], P), ALU.mult))
            link(dve.tensor_tensor(o3, o3, outer(col("outn", 0, P), 16), ALU.mult))
            dve.tensor_tensor(OR.rearrange("p a b c -> p a (b c)"), OR.rearrange("p a b c -> p a (b c)"), Zr, ALU.mult)\
               .then_inc(dve_done, st.one("dve", "ready"))
            dve.drain().then_inc(dve_done, 1)

        def merge_pe(pe, n):
            st = enter(pe, n)
            pe.wait_ge(dve_done, st.v("dve", "ready"))
            for h in range(GH):
                for t in range(4):
                    ins = pe.transpose(ps[:, h, tile(t)], OR[:, t, h, :], ident)
            ins.then_inc(pe_done, st.one("pe", "turned"))
            pe.drain().then_inc(pe_done, 1)

        def in3_pe(pe, n):
            st = enter(pe, n)
            for c in range(AH + AKV):
                wt = unit_here(pe, st.u0 + c // 2)
                if c >= 8:
                    pe.wait_ge(act_done, st.v("act", f"q{c - 8}"))
                o = (c % 2) * D
                name, m = (f"q{c}", T) if c < AH else (f"k{c - AH}", N2)
                dot(pe, ps[:, c % 8, 0:m], [(wt[:, o + k * P:o + (k + 1) * P], HM[:, k, 0:m]) for k in range(DC)])\
                    .then_inc(pe_done, st.one("pe", name))
            wt = unit_here(pe, st.u0 + 5)
            pe.wait_ge(act_done, st.v("act", "q5"))
            for t in range(4):
                ins = dot(pe, ps[:, 2 + t, 0:AKV * AD], [(HM[:, k, tile(t)], wt[:, k * 256:(k + 1) * 256]) for k in range(DC)])
            ins.then_inc(pe_done, st.one("pe", "v"))
            pe.drain().then_inc(pe_done, 1)

        def in3_act(act, n):
            st = enter(act, n)
            for c in range(AH):
                copy_marked(act, st, c, [(AQ[:, c, :], ps[:, c, 0:T])], f"q{c}")
            for c in range(AKV):
                copy_marked(act, st, c, [(AK[:, c, :], ps[:, c, :])], f"k{c}")
            copy_marked(act, st, 2, [(AV, ps[:, 2:6, 0:AKV * AD])], "v")
            act.drain().then_inc(act_done, 1)

        HEADS3 = AH + 2 * AKV
        heads3 = area[:, 0:HEADS3 * T].rearrange("p (c t) -> p c t", t=T)
        sq_all = area[:, HEADS3 * T:2 * HEADS3 * T]
        squares3 = sq_all.rearrange("p (c t) -> p c t", t=T)

        def rms3_pe(pe, n):
            st = enter(pe, n)
            for c in range(HEADS3):
                if c % 2 == 0:
                    pe.wait_ge(act_done, st.v("act", f"sq{c // 2}"))
                ins = pe.matmul(ps[0:HEADS3, 0, 0:T], pick(c, HEADS3), squares3[:, c, :], start=(c == 0), stop=(c == HEADS3 - 1))
            ins.then_inc(pe_done, st.one("pe", "sums"))
            pe.wait_ge(dve_done, st.v("dve", "inverse"))
            for c in range(HEADS3):
                ins = pe.matmul(ps[:, c // 2, (c % 2) * T:(c % 2 + 1) * T], spread_c[0:HEADS3, c, :], row[0:HEADS3, 0, 0:T],
                                start=True, stop=True)
                if c % 2:
                    ins.then_inc(pe_done, st.one("pe", f"spread{c // 2}"))
            pe.drain().then_inc(pe_done, 1)

        def rms3_act(act, n):
            st = enter(act, n)
            for b in range(6):
                act.activation(squares3[:, 2 * b:2 * b + 2, :], heads3[:, 2 * b:2 * b + 2, :], ACT.Square)\
                   .then_inc(act_done, st.one("act", f"sq{b}"))
            act.wait_ge(dve_done, st.v("dve", "eps"))
            act.activation(row[0:HEADS3, 1, 0:T], row[0:HEADS3, 0, 0:T], ACT.Sqrt).then_inc(act_done, st.one("act", "root"))
            act.drain().then_inc(act_done, 1)

        def rms3_dve(dve, link, n):
            st = enter(dve, n)
            link(dve.tensor_copy(spread_c, inner(con("ident", 0, 12), P)))
            dve.wait_ge(pe_done, st.v("pe", "sums"))
            dve.tensor_scalar(row[0:HEADS3, 0, 0:T], ps[0:HEADS3, 0, 0:T], 1.0 / AD, RMS_EPS, ALU.mult, ALU.add)\
               .then_inc(dve_done, st.one("dve", "eps"))
            dve.wait_ge(act_done, st.v("act", "root"))
            dve.reciprocal(row[0:HEADS3, 0, 0:T], row[0:HEADS3, 1, 0:T]).then_inc(dve_done, st.one("dve", "inverse"))
            for b in range(6):
                dve.wait_ge(pe_done, st.v("pe", f"spread{b}"))
                dve.scalar_tensor_tensor(heads3[:, 2 * b:2 * b + 2, :], heads3[:, 2 * b:2 * b + 2, :], col("qn" if 2 * b < AH else "kn"),
                                         ps[:, b, :].rearrange("p (c t) -> p c t", t=T), ALU.mult, ALU.mult)
            dve.drain().then_inc(dve_done, 1)

        def rope3_pe(pe, n):
            st = enter(pe, n)
            for c in range(AH):
                pe.matmul(ps[:, c // 2, (c % 2) * T:(c % 2 + 1) * T], con("permA"), AQ[:, c, :], start=True, stop=True)
            for c in range(AKV):
                ins = pe.matmul(ps[:, 4, c * T:(c + 1) * T], con("permA"), AK[:, c, 0:T], start=True, stop=True)
            ins.then_inc(pe_done, st.one("pe", "swapped"))
            pe.drain().then_inc(pe_done, 1)

        def rope3_dve(dve, link, n):
            st = enter(dve, n)
            dve.wait_ge(pe_done, st.v("pe", "swapped"))
            sw = ps[:, 0:5, :].rearrange("p a (b t) -> p (a b) t", b=2)
            prod = sq_all[:, 0:(AH + AKV) * T].rearrange("p (c t) -> p c t", t=T)
            dve.tensor_tensor(AQ, AQ, outer(con("cosA"), AH), ALU.mult)
            dve.tensor_tensor(AK[:, :, 0:T], AK[:, :, 0:T], outer(con("cosA"), AKV), ALU.mult)
            link(dve.tensor_tensor(prod, sw, outer(con("sinA"), AH + AKV), ALU.mult))
            dve.tensor_tensor(AQ, AQ, prod[:, 0:AH, :], ALU.add)
            dve.tensor_tensor(AK[:, :, 0:T], AK[:, :, 0:T], prod[:, AH:AH + AKV, :], ALU.add)
            dve.drain().then_inc(dve_done, 1)

        def gqa_scores(t, g_):
            return [[(AQ[:, 4 * g_ + h, tile(t)], AK[:, g_, :])] for h in range(4)]

        def gqa_mix(g_):
            return [[(AV[:, s_, g_ * AD:(g_ + 1) * AD], h * 4 + s_) for s_ in range(4)] for h in range(4)]

        block = ctx.enter_context(nc.Block())

        @block.sync
        def _(sp):
            sp.dma_start(X[:, :, 0:T], w["x"]).then_inc(x_in, 16)
            fill_ring(sp)
            sp.wait_ge(act_done, now["act"])
            sp.dma_start(out, X[:, :, 0:T]).then_inc(out_done, 16)
            sp.wait_ge(out_done, 16)

        @block.scalar
        def _(act):
            link = Chain(act, act_step)
            act.dma_start(cols[:], w["cols"]).then_inc(tables_in, 16)
            act.dma_start(cons[:], w["cons"]).then_inc(tables_in, 16)
            act.wait_ge(tables_in, 32)
            act.dma_start(X[:, :, T:N2], w["ctx"]).then_inc(ctx_in, 16)
            link(act.activation(condT[:].rearrange("p a b -> p (a b)"), col("cond", 0, 2 * DC), ACT.Silu))
            link(act.activation(cond4[:, :, 0:2], condT[:], ACT.Copy))
            for l in range(DEPTH):
                n = f"b1.{l}."
                in1_act(act, n + "in")
                rms1_act(act, n + "rms")
                up1_act(act, n + "up")
                idle(act, act_done, n + "rope")
                attend_act(act, n + "attend", ACT_ORDER1, H, S1, PT1, [OT1[:, 4 * e:4 * e + 4, tile(t)] for t in range(TT) for e in range(2)])
                idle(act, act_done, n + "out")
                ln_act(act, n + "ln1", T, f"ln1g{l}", f"ln1b{l}", n + "moe")
                router_act(act, n + "router")
                ffn_act(act, n + "moe", T, X, m_hi)
                ln_act(act, n + "ln2", T, f"ln2g{l}", f"ln2b{l}", "b2.0.ada" if l == DEPTH - 1 else None)
            for l in range(DEPTH):
                n = f"b2.{l}."
                ada_act(act, n + "ada", n + "ffn0")
                ffn_act(act, n + "ffn0", N2, Y, x_hi)
                ln_act(act, n + "ln0", N2, f"lng0{l}", f"lnb0{l}")
                idle(act, act_done, n + "mod1")
                if l == 0:
                    in2_act(act, n + "in")
                    conv_act(act, n + "conv")
                    l2_act(act, n + "l2")
                    rows_act(act, link, n + "rows")
                    for i in range(4):
                        scan_act(act, link, f"{n}scan{i}")
                    merge_act(act, n + "merge")
                else:
                    in3_act(act, n + "in")
                    rms3_act(act, n + "rms")
                    idle(act, act_done, n + "rope")
                    attend_act(act, n + "attend", ACT_ORDER2, 4, S2, PT2, [OT2[:, 4 * h:4 * h + 4, tile(t)] for t in range(TT) for h in range(AKV)])
                m = N2 if l < DEPTH - 1 else T
                idle(act, act_done, n + "out")
                ln_act(act, n + "ln1", m, f"lng1{l}", f"lnb1{l}", n + "ffn1")
                ffn_act(act, n + "ffn1", m, Y, x_hi)
                ln_act(act, n + "ln2", m, f"lng2{l}", f"lnb2{l}", f"b2.{l + 1}.ada" if l < DEPTH - 1 else None)

        @block.vector
        def _(dve):
            link = Chain(dve, dve_step)
            dve.wait_ge(tables_in, 32)
            dve.wait_ge(act_step, 2)
            dve.tensor_tensor(cond4[:, :, 2:4], condT[:], cond4[:, :, 0:2].bitcast(F32), ALU.subtract)
            dve.tensor_tensor(comb[:], con("ident", 0, 2), con("ident", 2, 2), ALU.add)
            for l in range(DEPTH):
                n = f"b1.{l}."
                in1_dve(dve, n + "in")
                rms1_dve(dve, link, n + "rms", l)
                idle(dve, dve_done, n + "up")
                rope1_dve(dve, link, n + "rope")
                attend_dve(dve, link, n + "attend", DVE_ORDER1, S1, H, [(NOPE + ROPE_D) ** -0.5, VD ** -0.5] * TT,
                           [m_ for t in range(TT) for m_ in (outer(con("causal", t * T, T), H), SB)])
                add_residual(dve, link, enter(dve, n + "out"), l, None, T)
                ln_dve(dve, link, n + "ln1", T, n + "moe")
                router_dve(dve, link, n + "router")
                ffn_dve(dve, link, n + "moe", l, T, X, m_hi, m_lo, e_hi, e_lo, None)
                ln_dve(dve, link, n + "ln2", T, "b2.0.ada" if l == DEPTH - 1 else None)
            dve.wait_ge(ctx_in, 16)
            for l in range(DEPTH):
                n = f"b2.{l}."
                ada_dve(dve, link, n + "ada", l, n + "ffn0")
                ffn_dve(dve, link, n + "ffn0", l, N2, Y, x_hi, x_lo, h_hi, h_lo, 2)
                ln_dve(dve, link, n + "ln0", N2)
                modulate(dve, n + "mod1", l, 3, 4)
                if l == 0:
                    in2_dve(dve, link, n + "in")
                    conv_dve(dve, link, n + "conv")
                    l2_dve(dve, link, n + "l2")
                    rows_dve(dve, link, n + "rows")
                    for i in range(4):
                        scan_dve(dve, link, f"{n}scan{i}", i)
                    merge_dve(dve, link, n + "merge")
                else:
                    idle(dve, dve_done, n + "in")
                    rms3_dve(dve, link, n + "rms")
                    rope3_dve(dve, link, n + "rope")
                    attend_dve(dve, link, n + "attend", DVE_ORDER2, S2, 4, [AD ** -0.5] * 4, [None] * 4)
                m = N2 if l < DEPTH - 1 else T
                add_residual(dve, link, enter(dve, n + "out"), l, 5, m)
                ln_dve(dve, link, n + "ln1", m, n + "ffn1")
                ffn_dve(dve, link, n + "ffn1", l, m, Y, x_hi, x_lo, h_hi, h_lo, 8)
                ln_dve(dve, link, n + "ln2", m, f"b2.{l + 1}.ada" if l < DEPTH - 1 else None)

        @block.tensor
        def _(pe):
            pe.wait_ge(x_in, 16)
            for l in range(DEPTH):
                n = f"b1.{l}."
                in1_pe(pe, n + "in")
                rms1_pe(pe, n + "rms")
                up1_pe(pe, n + "up")
                rope1_pe(pe, n + "rope")
                attend_pe(pe, n + "attend", PE_ORDER1, [u for t in range(TT) for u in (
                    (mla_scores(t), pair_mix(lambda h, s_: Vz[:, s_, h, :])),
                    (dsa_scores(t), pair_mix(lambda h, s_: DVz[:, s_, h % 2, :])))], S1, PT1)
                out_pe(pe, n + "out", lambda k: OT1[:, k, :], T)
                ln_pe(pe, n + "ln1", T)
                router_pe(pe, n + "router")
                ffn_pe(pe, n + "moe", T, m_hi, m_lo, e_hi, e_lo)
                ln_pe(pe, n + "ln2", T)
            for l in range(DEPTH):
                n = f"b2.{l}."
                ada_pe(pe, n + "ada")
                ffn_pe(pe, n + "ffn0", N2, x_hi, x_lo, h_hi, h_lo)
                ln_pe(pe, n + "ln0", N2)
                idle(pe, pe_done, n + "mod1")
                if l == 0:
                    in2_pe(pe, n + "in")
                    conv_pe(pe, n + "conv")
                    l2_pe(pe, n + "l2")
                    rows_pe(pe, n + "rows")
                    for i in range(4):
                        scan_pe(pe, f"{n}scan{i}", i)
                    merge_pe(pe, n + "merge")
                else:
                    in3_pe(pe, n + "in")
                    rms3_pe(pe, n + "rms")
                    rope3_pe(pe, n + "rope")
                    attend_pe(pe, n + "attend", PE_ORDER2, [(gqa_scores(t, h), gqa_mix(h)) for t in range(TT) for h in range(AKV)], S2, PT2)
                m = N2 if l < DEPTH - 1 else T
                src = (lambda k: HM[:, k, :] if k < GH else CF[:, k - GH, :]) if l == 0 else (lambda k: OT2[:, k, :])
                out_pe(pe, n + "out", src, m)
                ln_pe(pe, n + "ln1", m)
                ffn_pe(pe, n + "ffn1", m, x_hi, x_lo, h_hi, h_lo)
                ln_pe(pe, n + "ln2", m)


def constants():
    f = np.float32
    p = np.arange(P)
    rot = np.arange(T, dtype=f)
    c = {"ident": np.eye(P), "ones": np.ones((P, P)), "perm32": np.eye(P)[p ^ 16], "permA": np.eye(P)[p ^ 1]}
    inv = f(10000.0) ** (-np.arange(16, dtype=f) / f(16))
    ang = (rot[None, :] * inv[p % 16][:, None]).astype(f)
    c["cos32"] = np.cos(ang)
    c["sin32"] = np.sin(ang) * np.where(p % 32 < 16, -1, 1)[:, None]
    inv = f(10000.0) ** (-np.arange(32, dtype=f) / f(32))
    rows_, cols_ = (np.arange(T) // 64).astype(f), (np.arange(T) % 64).astype(f)
    ang = np.concatenate([inv[:, None] * rows_, inv[:, None] * cols_]).astype(f)
    c["cosA"] = np.cos(ang)[p // 2]
    c["sinA"] = np.sin(ang)[p // 2] * np.where(p % 2 == 0, -1, 1)[:, None]
    d = (np.arange(TT)[None, :, None] * P + p[:, None, None] - np.arange(T)[None, None, :]).astype(f)
    c["dist"] = d
    c["causal"] = np.where(d >= 0, 0, NEG)
    c["first4"] = np.broadcast_to(4 - np.arange(4), (P, 4))
    c["first16"] = np.broadcast_to(E_N - np.arange(E_N), (P, E_N))
    c["pick"] = np.broadcast_to(np.arange(23) == 11, (P, 23))
    j, i = p[:, None], p[None, :]
    for d_, late in enumerate((j < i, j > i)):
        c[f"tri{d_}"] = late | (j == i)
        c[f"lvl{d_}"] = np.stack([late & (j // (2 * b) == i // (2 * b)) & (j // b != i // b)
                                  for b in (1, 2, 4, 8, 16, 32, 64)], axis=1)
    out = np.zeros((P, NCONS), f)
    for name, (a, n) in CONS.items():
        out[:, a:a + n] = np.asarray(c[name]).astype(f).reshape(P, n)
    return out


def chunks_of(wt):
    k, n = wt.shape[0] // P, wt.shape[1] // P
    return wt.reshape(k, P, n, P).transpose(2, 1, 0, 3).reshape(n, P, k * P)


def rows_of(wt):
    k, n = wt.shape[0] // P, wt.shape[1]
    return wt.reshape(k, P, n).transpose(1, 0, 2).reshape(P, k * n)


def grouped(ch, m):
    n, _, wd = ch.shape
    return ch.reshape(n // m, m, P, wd).transpose(0, 2, 1, 3).reshape(n // m, P, m * wd)


def column(v):
    return v.reshape(-1, P).T


def spread(v):
    return np.broadcast_to(v.reshape(1, -1), (P, v.size))


def lay_out(a):
    w = {}
    w["x"] = a["x"][0].reshape(T, DC, P).transpose(2, 1, 0)
    w["ctx"] = a["ctx_2"][0].reshape(T, DC, P).transpose(2, 1, 0)
    cut = np.cumsum([Q_LORA, KV_LORA, ROPE_D, H * VD, VD, VD, H * IDX_DIM, IDX_DIM])
    w_in, rows_, qup, ukv, wo, mu, md = [], [], [], [], [], [], []
    for l in range(DEPTH):
        qa, kva, kr, dq, dk, dv, iq, ik, iw = np.split(a["w_in"][l], cut, axis=1)
        w_in.append(grouped(chunks_of(np.concatenate([qa, kva, dq, iq] + [kr] * 4 + [ik] * 4 + [dk] * 2, axis=1)), 2))
        rows_.append(rows_of(np.concatenate([iw, dv], axis=1))[None])
        q = a["w_q_up"][l].reshape(Q_LORA, H, NOPE + ROPE_D)
        q = np.concatenate([q[:, :, :NOPE].reshape(Q_LORA, -1), q[:, :, NOPE:].reshape(Q_LORA, -1)], axis=1)
        qup.append(grouped(chunks_of(q), 3))
        ukv.append(np.concatenate([grouped(chunks_of(a["w_uk"][l]), 4)[0], rows_of(a["w_uv"][l])], axis=1)[None])
        wo.append(grouped(chunks_of(a["w_o"][l]), 2))
        mu.append(np.concatenate([np.concatenate([chunks_of(a["w_gate"][l, e]) for e in range(E_N)]),
                                  np.concatenate([chunks_of(a["w_up"][l, e]) for e in range(E_N)])], axis=2))
        md.append(grouped(a["w_down"][l].reshape(MOE_CH, P, D), 2))
    w.update(w_in=np.stack(w_in), w_in_rows=np.stack(rows_), w_q_up=np.stack(qup), w_ukv=np.stack(ukv), w_o=np.stack(wo),
             moe_up=np.stack(mu), moe_down=np.stack(md))
    w["ada"] = a["ada_w_2"].reshape(DEPTH, 2, 4, P, 2 * N_MOD, 512).transpose(0, 4, 1, 3, 2, 5).reshape(DEPTH, 4 * N_MOD, P, UNIT)
    gu, dn = a["ffn_w_gu_2"], a["ffn_w_down_2"]
    w["ff_up"] = np.stack([np.stack([np.concatenate([chunks_of(gu[l, i][:, :DFF]), chunks_of(gu[l, i][:, DFF:])], axis=2)
                                     for i in range(2)]) for l in range(DEPTH)])
    w["ff_down"] = np.stack([np.stack([grouped(dn[l, i].reshape(FF_CH, P, D), 2) for i in range(2)]) for l in range(DEPTH)])
    qkv, z, ab, val, gate = np.split(a["even_w_in_2"][0], [3 * GH * GD, 4 * GH * GD, 4 * GH * GD + 4 * GH,
                                                            4 * GH * GD + 4 * GH + CCH * P], axis=1)
    glu = np.stack([chunks_of(val), chunks_of(gate)], axis=1).reshape(2 * CCH, P, D)
    w["even_in"] = grouped(np.concatenate([glu, chunks_of(qkv)]), 2)
    w["even_ab"] = rows_of(ab)[None]
    w["even_z"] = np.stack([rows_of(z[0:D // 2]), rows_of(z[D // 2:])])
    w["even_out"] = grouped(chunks_of(a["even_w_out_2"][0]), 2)
    ai = a["attn_w_in_2"][0]
    w["attn_in"] = grouped(chunks_of(ai[:, :(AH + AKV) * AD]), 2)
    w["attn_v"] = rows_of(ai[:, (AH + AKV) * AD:])[None]
    w["attn_out"] = grouped(chunks_of(a["attn_w_out_2"][0]), 2)
    c = {}
    for l in range(DEPTH):
        c[f"qg{l}"], c[f"kvg{l}"] = column(a["q_norm_g"][l]), column(a["kv_norm_g"][l])
        for i in (1, 2):
            c[f"ln{i}g{l}"], c[f"ln{i}b{l}"] = column(a[f"ln{i}_g"][l]), column(a[f"ln{i}_b"][l])
        c[f"adab{l}"] = column(a["ada_b_2"][l])
        for i in range(3):
            c[f"lng{i}{l}"], c[f"lnb{i}{l}"] = column(a["ln_g_2"][l, i]), column(a["ln_b_2"][l, i])
    c["cond"] = np.stack([column(a["c_2"][0]), column(a["c_ctx_2"])], axis=2).reshape(P, 2 * DC)
    c["gconv"] = a["even_qkv_conv_2"][0].T.reshape(12, P, GCONV).transpose(1, 0, 2).reshape(P, -1)
    c["cconv"] = a["cf_dw_conv_2"][0].T.reshape(CCH, P, CCONV).transpose(1, 0, 2).reshape(P, -1)
    c["cbias"], c["clng"], c["clnb"] = [column(a[k][0]) for k in ("cf_dw_bias_2", "cf_ln_g_2", "cf_ln_b_2")]
    c["qn"], c["kn"] = column(a["attn_q_norm_2"][0]), column(a["attn_k_norm_2"][0])
    c["rbias"], c["alog"], c["dtb"] = spread(a["router_bias"]), spread(a["gdn_a_log_2"][0]), spread(a["gdn_dt_bias_2"][0])
    c["outn"], c["rw"] = spread(a["gdn_out_norm_2"][0]), rows_of(a["router_w"])
    w["cols"] = np.zeros((P, NCOLS), np.float32)
    for name, (at, n) in COLS.items():
        w["cols"][:, at:at + n] = c[name]
    w["cons"] = constants()
    return {k: np.ascontiguousarray(v) for k, v in w.items()}


def kernel(**inputs):
    import concourse.bacc as bacc
    from concourse.bass_utils import run_bass_kernel_spmd

    nc = bacc.Bacc("TRN2", target_bir_lowering=False, num_devices=1)
    arrays, w = {}, {}
    for name, v in lay_out({k: np.asarray(v) for k, v in inputs.items()}).items():
        arrays[f"in_{name}"] = v
        w[name] = nc.dram_tensor(f"in_{name}", v.shape, F32, kind="ExternalInput").ap()
    out = nc.dram_tensor("out_x", (P, DC, T), F32, kind="ExternalOutput").ap()
    build(nc, w, out)
    r = run_bass_kernel_spmd(nc, [arrays], core_ids=[0])
    got = np.asarray(r.results[0]["out_x"])
    return np.ascontiguousarray(got.transpose(2, 1, 0).reshape(1, T, D))
```
